# Optimizing a Trainium2 kernel written in Bass

```python
import math
import functools
import numpy as np
import jax
import jax.numpy as jnp
from jax import lax

D_MODEL = 2048
BATCH = 1
SEQ = 256
DEPTH = 1
DEC_BATCH = 8
DEC_SEQ = 8
PAST_LEN = 256
PAGE_SIZE = 128

N_HEADS = 16
HEAD_DIM = D_MODEL // N_HEADS
KV_HEADS = 4
Q_PER_KV = N_HEADS // KV_HEADS
IDX_HEADS = 16
IDX_DIM = 64
TOPK_MAX = 256
Q_BLOCK = 64
N_BUCKETS = 32
MAX_DISTANCE = 128
HG_EXPAND = 128
HG_HEADS = D_MODEL // HG_EXPAND
HG_DK = HG_EXPAND
HG_DV = D_MODEL // HG_HEADS
HG_CHUNK = 32
MEM_LEN = 256
X_HEADS = 4
X_HEAD_DIM = D_MODEL // X_HEADS
D_FF = 11 * D_MODEL // 4
CONV_W = 3
EPS = 1e-6

A_WIDTH = N_HEADS * HEAD_DIM
KV_WIDTH = KV_HEADS * HEAD_DIM
B_WIDTH = HG_HEADS * HG_DV
HG_KWIDTH = HG_HEADS * HG_DK
MERGE_WIDTH = A_WIDTH
MIX_SIZES = (A_WIDTH, KV_WIDTH, KV_WIDTH, IDX_HEADS * IDX_DIM, IDX_HEADS, IDX_DIM,
             HG_KWIDTH, HG_KWIDTH, B_WIDTH, B_WIDTH, MERGE_WIDTH, MERGE_WIDTH)
MIX_WIDTH = sum(MIX_SIZES)

kernel_name = 'hybrid_dsa_hgrn2_memxattn_convffn_step'

def rms_norm(x, g):
    xf = x.astype(jnp.float32)
    y = xf * lax.rsqrt(jnp.mean(xf * xf, axis=-1, keepdims=True) + EPS)
    return (y * g.astype(jnp.float32)).astype(x.dtype)

def rel_bucket(dist):
    max_exact = N_BUCKETS // 2
    d = jnp.maximum(dist, 0)
    log_ratio = jnp.log(jnp.maximum(d, 1).astype(jnp.float32) / max_exact) / math.log(MAX_DISTANCE / max_exact)
    large = jnp.minimum(max_exact + (log_ratio * (N_BUCKETS - max_exact)).astype(jnp.int32), N_BUCKETS - 1)
    return jnp.where(d < max_exact, d, large)

def indexer_scores(iq, iw, ik):
    qk = jnp.einsum('bthd,bsd->bths', iq, ik, preferred_element_type=jnp.float32) * (IDX_DIM ** -0.5)
    return jnp.einsum('bths,bth->bts', jax.nn.relu(qk), iw.astype(jnp.float32))

def sparse_attend(q, k_sel, v_sel, dist, rel_bias):
    B, T = q.shape[:2]
    qg = q.reshape(B, T, KV_HEADS, Q_PER_KV, HEAD_DIM)
    s = jnp.einsum('bthgd,btnhd->bthgn', qg, k_sel, preferred_element_type=jnp.float32) * (HEAD_DIM ** -0.5)
    bias = rel_bias.astype(jnp.float32)[rel_bucket(dist)]
    bias = jnp.moveaxis(bias.reshape(B, T, -1, KV_HEADS, Q_PER_KV), 2, -1)
    s = jnp.where((dist >= 0)[:, :, None, None, :], s + bias, -jnp.inf)
    p = jax.nn.softmax(s, axis=-1)
    o = jnp.einsum('bthgn,btnhd->bthgd', p.astype(v_sel.dtype), v_sel)
    return o.reshape(B, T, A_WIDTH)

def dsa_prompt(q, k, v, iq, iw, ik, rel_bias):
    B, S = q.shape[:2]
    topk = min(TOPK_MAX, S // 4)
    nblk = S // Q_BLOCK
    key_pos = jnp.arange(S)
    bidx = jnp.arange(B)[:, None, None]

    def to_blocks(a):
        return jnp.swapaxes(a.reshape((B, nblk, Q_BLOCK) + a.shape[2:]), 0, 1)

    def block(args):
        blk, qb, iqb, iwb = args
        q_pos = blk * Q_BLOCK + jnp.arange(Q_BLOCK)
        sc = indexer_scores(iqb, iwb, ik)
        sc = jnp.where((key_pos[None, :] <= q_pos[:, None])[None], sc, -jnp.inf)
        _, sel = lax.top_k(sc, topk)
        return sparse_attend(qb, k[bidx, sel], v[bidx, sel], q_pos[None, :, None] - sel, rel_bias)

    out = lax.map(block, (jnp.arange(nblk), to_blocks(q), to_blocks(iq), to_blocks(iw)))
    return jnp.swapaxes(out, 0, 1).reshape(B, S, A_WIDTH)

def dsa_sample(q, k, v, iq, iw, ik, cache_k, cache_v, cache_idx_k, page_table, rel_bias):
    B, T = q.shape[:2]
    page = cache_k.shape[1]
    past = page_table.shape[1] * page
    L = past + T
    topk = min(TOPK_MAX, L // 4)
    ik_past = cache_idx_k[page_table].reshape(B, past, IDX_DIM)
    ik_all = jnp.concatenate([ik_past, ik.astype(ik_past.dtype)], axis=1)
    q_pos = past + jnp.arange(T)
    sc = indexer_scores(iq, iw, ik_all)
    sc = jnp.where(jnp.arange(L)[None, None, :] <= q_pos[None, :, None], sc, -jnp.inf)
    _, sel = lax.top_k(sc, topk)
    bidx = jnp.arange(B)[:, None, None]
    sel_past = jnp.minimum(sel, past - 1)
    phys = page_table[bidx, sel_past // page]
    off = sel_past % page
    sel_new = jnp.clip(sel - past, 0, T - 1)
    in_past = (sel < past)[..., None, None]
    k_sel = jnp.where(in_past, cache_k[phys, off], k[bidx, sel_new].astype(cache_k.dtype))
    v_sel = jnp.where(in_past, cache_v[phys, off], v[bidx, sel_new].astype(cache_v.dtype))
    return sparse_attend(q, k_sel, v_sel, q_pos[None, :, None] - sel, rel_bias)

def hgrn_lower_bounds(hg_lb):
    sm = jax.nn.softmax(hg_lb.astype(jnp.float32), axis=0)
    return jnp.cumsum(sm, axis=0)[1:] - sm[0]

def hgrn_chunk(S0, q, k, v, logf):
    C = q.shape[1]
    b = jnp.cumsum(logf, axis=1)
    causal = jnp.tril(jnp.ones((C, C), dtype=bool))[None, :, :, None, None]
    decay = jnp.exp(jnp.where(causal, b[:, :, None] - b[:, None, :], -jnp.inf))
    a = jnp.sum(q[:, :, None] * k[:, None, :] * decay, axis=-1)
    o = jnp.einsum('btsh,bshv->bthv', a, v) + jnp.einsum('bthc,bhcv->bthv', q * jnp.exp(b), S0)
    b_end = b[:, -1]
    S = jnp.exp(b_end)[..., None] * S0 + jnp.einsum('bshc,bshv->bhcv', k * jnp.exp(b_end[:, None] - b), v)
    return S, o

def hgrn_prompt(q, k, v, logf):
    B, S = q.shape[:2]
    C = math.gcd(HG_CHUNK, S)
    n = S // C

    def split(a):
        return jnp.swapaxes(a.reshape((B, n, C) + a.shape[2:]), 0, 1)

    S0 = jnp.zeros((B, HG_HEADS, HG_DK, HG_DV), jnp.float32)
    S_fin, o = lax.scan(lambda st, xs: hgrn_chunk(st, *xs), S0, (split(q), split(k), split(v), split(logf)))
    return jnp.swapaxes(o, 0, 1).reshape(B, S, HG_HEADS, HG_DV), S_fin

def hgrn_sample(q, k, v, logf, S0):
    S, o = hgrn_chunk(S0.astype(jnp.float32), q, k, v, logf)
    return o, S

def mem_kv(mem, g_mem, w_xk, w_xv):
    B, M, _ = mem.shape
    m = rms_norm(mem, g_mem)
    mk = jnp.einsum('bmd,de->bme', m, w_xk).reshape(B, M, X_HEADS, X_HEAD_DIM)
    mv = jnp.einsum('bmd,de->bme', m, w_xv).reshape(B, M, X_HEADS, X_HEAD_DIM)
    return mk, mv

def cross_attend(h, w_xq, mem_k, mem_v, w_xo):
    B, T, _ = h.shape
    q = jnp.einsum('btd,de->bte', h, w_xq).reshape(B, T, X_HEADS, X_HEAD_DIM)
    s = jnp.einsum('bthd,bmhd->bhtm', q, mem_k, preferred_element_type=jnp.float32) * (X_HEAD_DIM ** -0.5)
    p = jax.nn.softmax(s, axis=-1)
    o = jnp.einsum('bhtm,bmhd->bthd', p.astype(mem_v.dtype), mem_v).reshape(B, T, D_MODEL)
    return jnp.einsum('bte,ed->btd', o, w_xo)

def conv_ffn(h, buf, w_up, conv_w, conv_b, w_down):
    T = h.shape[1]
    a, b = jnp.split(jnp.einsum('btd,de->bte', h, w_up), 2, axis=-1)
    a_ext = jnp.concatenate([buf.astype(a.dtype), a], axis=1)
    c = conv_b + sum(conv_w[j] * a_ext[:, j:j + T] for j in range(CONV_W))
    y = jax.nn.gelu(c) * b
    return jnp.einsum('btf,fd->btd', y, w_down), a_ext[:, T:]

def trunk_layer(x, p, lb, dsa_fn, hgrn_fn, mem_k, mem_v, conv_buf):
    B, T, _ = x.shape
    f32 = jnp.float32
    h = rms_norm(x, p['g_pre_mix'])
    z = jnp.einsum('btd,de->bte', h, p['w_in'])
    splits = np.cumsum(MIX_SIZES)[:-1].tolist()
    q, k, v, iq, iw, ik, hq, hf, hi, hg, ga, gb = jnp.split(z, splits, axis=-1)
    q = q.reshape(B, T, N_HEADS, HEAD_DIM)
    k = k.reshape(B, T, KV_HEADS, HEAD_DIM)
    v = v.reshape(B, T, KV_HEADS, HEAD_DIM)
    iq = iq.reshape(B, T, IDX_HEADS, IDX_DIM)
    iw = iw * (IDX_HEADS ** -0.5)
    o_a = dsa_fn(q, k, v, iq, iw, ik)
    f = lb + (1.0 - lb) * jax.nn.sigmoid(hf.astype(f32))
    kshape = (B, T, HG_HEADS, HG_DK)
    o_b, S_new = hgrn_fn(hq.astype(f32).reshape(kshape), (1.0 - f).reshape(kshape),
                         hi.astype(f32).reshape(B, T, HG_HEADS, HG_DV), jnp.log(f).reshape(kshape))
    o_b = rms_norm(o_b, p['hg_norm'].reshape(HG_HEADS, HG_DV)).reshape(B, T, B_WIDTH).astype(x.dtype) * jax.nn.silu(hg)
    u = jax.nn.sigmoid(ga) * o_a + jax.nn.sigmoid(gb) * o_b
    x = x + rms_norm(jnp.einsum('bte,ed->btd', u, p['w_out']), p['g_post_mix'])
    h = rms_norm(x, p['g_pre_x'])
    x = x + rms_norm(cross_attend(h, p['w_xq'], mem_k, mem_v, p['w_xo']), p['g_post_x'])
    h = rms_norm(x, p['g_pre_ffn'])
    y, new_buf = conv_ffn(h, conv_buf, p['w_up'], p['conv_w'], p['conv_b'], p['w_down'])
    x = x + rms_norm(y, p['g_post_ffn'])
    return x, k, v, ik, S_new.astype(x.dtype), new_buf

def setup_inputs(seed: int = 0) -> dict:
    key = jax.random.key(seed)
    keys = iter(jax.random.split(key, 48))

    def nrm(shape, scale):
        return jax.random.normal(next(keys), shape, jnp.float32) * scale

    def gain(shape):
        return 1.0 + nrm(shape, 0.05)

    n_pages = PAST_LEN // PAGE_SIZE
    n_used = DEC_BATCH * n_pages
    n_pool = n_used + n_used // 4
    page_table = jax.random.permutation(next(keys), n_pool)[:n_used].reshape(DEC_BATCH, n_pages).astype(jnp.int32)
    return {
        'x_prompt': nrm((BATCH, SEQ, D_MODEL), 1.0),
        'x_sample': nrm((DEC_BATCH, DEC_SEQ, D_MODEL), 1.0),
        'mem_prompt': nrm((BATCH, MEM_LEN, D_MODEL), 1.0),
        'cache_k': nrm((DEPTH, n_pool, PAGE_SIZE, KV_HEADS, HEAD_DIM), 1.0),
        'cache_v': nrm((DEPTH, n_pool, PAGE_SIZE, KV_HEADS, HEAD_DIM), 1.0),
        'cache_idx_k': nrm((DEPTH, n_pool, PAGE_SIZE, IDX_DIM), 1.0),
        'cache_mem_k': nrm((DEPTH, DEC_BATCH, MEM_LEN, X_HEADS, X_HEAD_DIM), 1.0),
        'cache_mem_v': nrm((DEPTH, DEC_BATCH, MEM_LEN, X_HEADS, X_HEAD_DIM), 1.0),
        'state_hgrn': nrm((DEPTH, DEC_BATCH, HG_HEADS, HG_DK, HG_DV), 0.5),
        'state_conv': nrm((DEPTH, DEC_BATCH, CONV_W - 1, D_FF), 1.0),
        'page_table': page_table,
        'rel_bias': nrm((N_BUCKETS, N_HEADS), 0.2),
        'hg_lb': nrm((DEPTH + 1, HG_KWIDTH), 0.1),
        'g_pre_mix': gain((DEPTH, D_MODEL)),
        'w_in': nrm((DEPTH, D_MODEL, MIX_WIDTH), D_MODEL ** -0.5),
        'hg_norm': gain((DEPTH, B_WIDTH)),
        'w_out': nrm((DEPTH, MERGE_WIDTH, D_MODEL), MERGE_WIDTH ** -0.5),
        'g_post_mix': gain((DEPTH, D_MODEL)),
        'g_pre_x': gain((DEPTH, D_MODEL)),
        'g_mem': gain((DEPTH, D_MODEL)),
        'w_xq': nrm((DEPTH, D_MODEL, D_MODEL), D_MODEL ** -0.5),
        'w_xk': nrm((DEPTH, D_MODEL, D_MODEL), D_MODEL ** -0.5),
        'w_xv': nrm((DEPTH, D_MODEL, D_MODEL), D_MODEL ** -0.5),
        'w_xo': nrm((DEPTH, D_MODEL, D_MODEL), D_MODEL ** -0.5),
        'g_post_x': gain((DEPTH, D_MODEL)),
        'g_pre_ffn': gain((DEPTH, D_MODEL)),
        'w_up': nrm((DEPTH, D_MODEL, 2 * D_FF), D_MODEL ** -0.5),
        'conv_w': nrm((DEPTH, CONV_W, D_FF), CONV_W ** -0.5),
        'conv_b': nrm((DEPTH, D_FF), 0.02),
        'w_down': nrm((DEPTH, D_FF, D_MODEL), D_FF ** -0.5),
        'g_post_ffn': gain((DEPTH, D_MODEL)),
    }

def reference(x_prompt, x_sample, mem_prompt, cache_k, cache_v, cache_idx_k, cache_mem_k, cache_mem_v,
              state_hgrn, state_conv, page_table, rel_bias, hg_lb, g_pre_mix, w_in, hg_norm, w_out,
              g_post_mix, g_pre_x, g_mem, w_xq, w_xk, w_xv, w_xo, g_post_x, g_pre_ffn, w_up, conv_w,
              conv_b, w_down, g_post_ffn):
    lbs = hgrn_lower_bounds(hg_lb)
    xp, xs = x_prompt, x_sample
    new = [[] for _ in range(12)]
    for l in range(DEPTH):
        p = {'g_pre_mix': g_pre_mix[l], 'w_in': w_in[l], 'hg_norm': hg_norm[l], 'w_out': w_out[l],
             'g_post_mix': g_post_mix[l], 'g_pre_x': g_pre_x[l], 'w_xq': w_xq[l], 'w_xo': w_xo[l],
             'g_post_x': g_post_x[l], 'g_pre_ffn': g_pre_ffn[l], 'w_up': w_up[l], 'conv_w': conv_w[l],
             'conv_b': conv_b[l], 'w_down': w_down[l], 'g_post_ffn': g_post_ffn[l]}
        mk, mv = mem_kv(mem_prompt, g_mem[l], w_xk[l], w_xv[l])
        conv0 = jnp.zeros((xp.shape[0], CONV_W - 1, D_FF), xp.dtype)
        xp, kp, vp, ikp, sp, cp = trunk_layer(
            xp, p, lbs[l], functools.partial(dsa_prompt, rel_bias=rel_bias), hgrn_prompt, mk, mv, conv0)
        dsa_s = functools.partial(dsa_sample, cache_k=cache_k[l], cache_v=cache_v[l],
                                  cache_idx_k=cache_idx_k[l], page_table=page_table, rel_bias=rel_bias)
        xs, ks, vs, iks, ss, cs = trunk_layer(
            xs, p, lbs[l], dsa_s, functools.partial(hgrn_sample, S0=state_hgrn[l]),
            cache_mem_k[l], cache_mem_v[l], state_conv[l])
        for store, val in zip(new, (kp, vp, ikp, ks, vs, iks, mk, mv, sp, ss, cp, cs)):
            store.append(val)
    (new_k_prompt, new_v_prompt, new_idx_k_prompt, new_k_sample, new_v_sample, new_idx_k_sample,
     new_mem_k_prompt, new_mem_v_prompt, new_hgrn_prompt, new_hgrn_sample,
     new_conv_prompt, new_conv_sample) = [jnp.stack(s, axis=0) for s in new]
    y_prompt, y_sample = xp, xs
    return (y_prompt, y_sample, new_k_prompt, new_v_prompt, new_idx_k_prompt, new_k_sample, new_v_sample,
            new_idx_k_sample, new_mem_k_prompt, new_mem_v_prompt, new_hgrn_prompt, new_hgrn_sample,
            new_conv_prompt, new_conv_sample)


_drawn_inputs = setup_inputs


def setup_inputs(seed=0):
    import zlib

    import numpy as np

    out = dict(_drawn_inputs(seed))
    spreads = {}
    factors = {'conv_b': 5.734}
    for name, (base, spread) in spreads.items():
        noise = np.random.default_rng([zlib.crc32(name.encode()), seed]).standard_normal(out[name].shape)
        drawn = base * np.exp(spread * noise) if base else spread * noise
        out[name] = jnp.asarray(drawn.astype(out[name].dtype))
    for name, factor in factors.items():
        out[name] = (out[name] * factor).astype(out[name].dtype)
    return out
```

```python
import math
from contextlib import ExitStack

import numpy as np
import concourse.bass as bass
from concourse import mybir

FP32 = mybir.dt.float32
FP32R = mybir.dt.float32r
I32 = mybir.dt.int32
ALU = mybir.AluOpType
ACT = mybir.ActivationFunctionType
AX = mybir.AxisListType

P = 128
D = 2048
KD = D // P
SEQ = 256
DB, DT = 8, 8
NS = DB * DT
T = SEQ + NS
MEM = 256
PAGE = 128
NPG = 2
PAST = PAGE * NPG
POOL = 20
KVH, QPK, H = 4, 4, 16
IDX = 64
L_S = PAST + DT
TOPK_P, TOPK_S = 64, 66
PAD_S = -TOPK_S % 8
NB, NHG = 32, 16
XH, XD = 4, 4
FF = 5632
FT = FF // P
LV = 7
LVS = 3
R = 4
DOWN_K = FT // R
ARENA = 53184 - R * KD * P - KD * T
EPS = 1e-6
NEG = -1e30
O_Q, O_K, O_V, O_IQ, O_IW, O_IK = 0, 2048, 2560, 3072, 4096, 4112
O_HQ, O_HF, O_HI, O_HG, O_GA, O_GB = 4176, 6224, 8272, 10320, 12368, 14416
DIST0 = PAST + DT - 1
NDIST = 392

PAR_ROWS = (P, 120, 88)
PAR_DMAS = 14
BIAS_DMAS = 1 + 2 * H
HEAD_STEPS = 41


def parameter_rows(A):
    vec = [(0, 16 * i, A[n]) for i, n in enumerate(("g_pre_mix", "hg_norm", "g_post_mix", "g_pre_x", "g_mem",
                                                    "g_post_x", "g_pre_ffn", "g_post_ffn"))]
    vec += [(1, 0, A["hg_lb"][0:1]), (1, 16, A["hg_lb"][1:2]), (1, 32, A["conv_b"]), (1, 76, A["conv_w"][0, 0:1]),
            (2, 0, A["conv_w"][0, 1:2]), (2, 44, A["conv_w"][0, 2:3])]
    return [(g, r, v.rearrange("o (k p) -> (o k) p", p=P)) for g, r, v in vec]


CONST = {}
_at = 0
for _name, _cols in (("ident", 128), ("ones", 128), ("level", 8 * 128), ("level_s", 4 * 64), ("causal", 512),
                     ("causal_new", 8), ("other_seq", 64), ("dist", NDIST), ("heads_of", 128),
                     ("w_place", 512), ("spread", 1024), ("scan_keep", T), ("seq_of", 8)):
    CONST[_name] = (_at, _cols)
    _at += _cols
NCONST = _at


def shape_constants():
    c = np.zeros((P, NCONST), np.float32)

    def put(name, a):
        o, n = CONST[name]
        a = np.asarray(a, np.float32).reshape(a.shape[0], n)
        c[:a.shape[0], o:o + n] = a

    put("ident", np.eye(P))
    put("ones", np.ones((P, P)))
    s, t = np.meshgrid(np.arange(P), np.arange(P), indexing="ij")
    lev = np.zeros((P, 8, P))
    for l in range(LV):
        same = (s >> (l + 1)) == (t >> (l + 1))
        lev[:, l] = same & (((s >> l) & 1) == 0) & (((t >> l) & 1) == 1)
    lev[:, 7] = s == t
    put("level", lev)
    put("level_s", lev[:NS, [0, 1, 2, 7], :NS])
    q = np.arange(P)[:, None, None] + P * np.arange(2)[None, :, None]
    put("causal", np.where(np.arange(SEQ)[None, None, :] <= q, 0.0, NEG))
    row = np.arange(NS)
    put("causal_new", np.where(np.arange(DT)[None] <= (row % DT)[:, None], 0.0, NEG))
    put("other_seq", np.where((row // DT)[:, None] == (row // DT)[None], 0.0, NEG))
    dist = DIST0 - np.arange(NDIST)
    d = np.maximum(dist, 0)
    ratio = np.log(np.maximum(d, 1).astype(np.float32) / np.float32(16)) / np.float32(math.log(8))
    large = np.minimum(16 + (ratio * np.float32(16)).astype(np.int32), NB - 1)
    bucket = np.where(d < 16, d, large)
    put("dist", np.arange(NB)[:, None] == bucket[None])
    r = np.arange(P)
    put("heads_of", np.arange(H)[:, None] == (2 * ((r // 8) % 8) + r // 64)[None])
    seq, tok = np.arange(NS) // DT, np.arange(NS) % DT
    put("w_place", (np.arange(DB)[None, :, None] == seq[None, None]) & ((r % 8)[:, None, None] == tok[None, None]))
    put("spread", (seq[:, None, None] == np.arange(DB)[None, :, None]) & (tok[:, None, None] == (r % 8)[None, None]))
    keep = np.ones(T)
    keep[[0, P]] = 0
    keep[SEQ::DT] = 0
    put("scan_keep", np.broadcast_to(keep, (P, T)))
    put("seq_of", (row // DT)[:, None] == np.arange(DB)[None])
    return c


class Steps:

    def __init__(self, eng, sem):
        self.eng, self.sem, self.base, self.n = eng, sem, 0, 0

    def did(self, ins):
        ins.then_inc(self.sem, 1)
        self.n += 1

    def sync(self):
        self.eng.wait_ge(self.sem, self.base + self.n)

    def then(self, ins):
        self.did(ins)
        self.sync()

    def enter(self, it, per):
        self.start, self.per = self.base + self.n, per
        self.base, self.n = self.start + it * per, 0

    def leave(self, count):
        assert self.n == self.per, (self.n, self.per)
        self.base, self.n = self.start + count * self.per, 0


def hybrid_layer(nc, A, O, const_dram):
    ctx = ExitStack()
    with ctx:
        def sem(name):
            return ctx.enter_context(nc.semaphore(name))

        ds = bass.ds
        ring_at = -(-nc.sbuf_base // 64) * 64
        ring = ctx.enter_context(nc.sbuf_tensor("ring", [P, R, KD, P], FP32))[:]
        h_at = ring_at + 4 * R * KD * P
        hT = ctx.enter_context(nc.sbuf_tensor("h", [P, KD, T], FP32))[:]
        arena_at = h_at + 4 * KD * T
        arena = ctx.enter_context(nc.sbuf_tensor("arena", [P, ARENA], FP32))
        pages = ctx.enter_context(nc.sbuf_tensor("pages", [1, DB * NPG], I32))
        psum = ctx.enter_context(nc.psum_tensor("psum", [P, 8 * 512], FP32))
        bias_dram = nc.dram_tensor("bias_by_distance", (H, P, NDIST), FP32, kind="Internal").ap()

        top = [0]

        def take(*shape):
            n = int(np.prod(shape))
            a = arena[:, top[0]:top[0] + n]
            top[0] += n
            assert top[0] <= ARENA
            if len(shape) == 2:
                a = a.rearrange("p (a b) -> p a b", a=shape[0])
            elif len(shape) == 3:
                a = a.rearrange("p (a b c) -> p a b c", a=shape[0], b=shape[1])
            return a

        def alias(name, offset, *shape):
            return nc.alloc_sbuf_tensor_at(name, [P] + list(shape), FP32R, offset=offset)[:]

        h_lo = alias("h_low", h_at, KD, T)
        w_lo = alias("w_low", ring_at, R, KD, P)

        def take_split(name, *shape):
            low = alias(name, arena_at + 4 * top[0], *shape)
            return take(*shape), low

        def take_high(name, *shape):
            high = alias(name, arena_at + 4 * top[0], *shape)
            take(*shape)
            return high

        def bank(i, n=1):
            return psum[:, 512 * i:512 * (i + n)]

        consts = take(NCONST)

        def const(name, rows=P):
            o, n = CONST[name]
            return consts[0:rows, o:o + n]

        ident, ones = const("ident"), const("ones")
        level = const("level").rearrange("p (l t) -> p l t", l=8)
        level_s = const("level_s", NS).rearrange("p (l t) -> p l t", l=4)
        causal = const("causal").rearrange("p (a k) -> p a k", a=2)

        par = take(3, P)
        head_par = take(NHG, 3)
        conv_par = take(FT, 4)
        xT = take(KD, T)
        small = take(64)
        sqacc = take(T)
        rstd = take(T)
        var = take(T)
        ntmp = take(T)
        sqbuf = take(2, T)
        BASE = top[0]
        G_PRE_MIX, G_HG, G_POST_MIX, G_PRE_X, G_MEM, G_POST_X, G_PRE_FFN, G_POST_FFN = \
            [par[:, 0, 16 * i:16 * i + 16] for i in range(8)]

        zq = take(KD, T)
        MIX = top[0]
        kT = take(KVH, T)
        vN = take(3, 512)
        sel_p = take(2, SEQ)
        sel_s = take(T)
        key_out = take(3, 512)
        ik_out = take(3, IDX)
        mT = take(KD, MEM)
        mem_out = take(2, 512)
        C0 = top[0] - 1024
        top[0] = C0
        iqT = take(8, T)
        w_ik = take(KD, 144)
        ikz = take(2, SEQ)
        ikd = take(T)
        iwT = take(T)
        iwN = take(2, H)
        iq_s = take(DB, P)
        ik_page = key_out.rearrange("p a b -> p (a b)")[:, 0:DB * NPG * IDX].rearrange("p (n d) -> p n d", n=DB * NPG)
        ik_dup = w_ik.rearrange("p a b -> p (a b)")[:, 0:DB * NPG * 2 * IDX]\
            .rearrange("p (n o d) -> p n o d", n=DB * NPG, o=2)
        ik_all = take(DB, L_S)
        w_sel = take(DB, NS)
        score = take(2, SEQ)
        score_t = take(4, SEQ)
        relu_s = take(2, L_S)
        work = take(PAD_S + L_S)
        best = take(8)
        top[0] = C0
        x_rows = take(3, D)
        TA = top[0]
        top[0] = C0 - 1024 - 4096
        top[0] = C0 + 1024
        toep = take(H, SEQ)
        bias_s = take(T)
        qs = take(QPK, SEQ)
        vs = take(2, P)
        bm = take(2, 384)
        prob = take(2, 384)
        probT = take(2, 384)
        smx = take(8, 4)
        ktp = take(KVH, PAST)
        q_b = take(2, H, DT)
        rep_b = take(2, P)
        rel_sb = take(H)
        dist_sb = take(NDIST)
        top[0] = C0 - 4096
        k_page = take(2, NPG, 512)
        v_page = take(2, NPG, 512)
        logit = take(2, 384)
        top[0] = TA
        m_rows = take(2, D)
        junk = hT.rearrange("p a b -> p (a b)")[:, 0:D]
        diag = take(5, P)
        par_rows = zq.rearrange("p a b -> p (a b)")[:, 0:384].rearrange("p (g c) -> p g c", g=3)

        top[0] = MIX
        uT, u_lo = take_split("u_low", KD, T)
        f_e = take(T)
        f_k = take(T)
        f_b = take(T)
        hq = take(T)
        vh = take(3, P)
        lev = take(LV, T)
        levq = take(LV, T)
        a_m = take(8, P)
        a_T = take(3, P)
        eb = take(T)
        qb = take(T)
        ke = take(T)
        keN = take(3, P)
        s1 = take(P)
        s2 = take(P)
        v_m = take(DB, P)
        s_old = take(2, DB, P)
        s_new = take(DB, P)
        gate = take(3, T)
        hgr = take(T)
        osq = take(T)
        o_n = take(T)
        o_r = take(T)
        pcol = take(3)
        TF = top[0]

        top[0] = BASE
        qx, q_lo = take_split("q_low", KD, T)
        top[0] = MIX + KD * T
        kx = take(2, 2, D)
        x_hi = take_high("x_high", KD, T)
        w_hi = take_high("w_high", 2, KD, P)
        SPLIT_AT = top[0] - KD * T - 2 * KD * P
        top[0] = CONST["level"][0]
        kxT = take(2, XD, P)
        top[0] = MIX
        sxT = take(2, 4 * MEM // 4)
        px = take(2, MEM)
        pxT = take(2, MEM)
        pp = take(2, XH, MEM)
        ppT = take(2, 2 * SEQ)
        smx2 = take(8, 4)
        assert top[0] <= MIX + KD * T

        top[0] = BASE
        yT = take(FT, T)
        top[0] = BASE + 3 * D
        conv_rows = take(FF)
        assert top[0] <= BASE + FT * T
        top[0] = CONST["level"][0]
        conv_old = take(FT, 16)
        top[0] = BASE + FT * T
        conv_new = take(FT, 18)
        a_ext = take(2, SEQ + 2 + DB * (DT + 2))
        cv = take(2, T)
        cvt = take(2, T)
        zb = take(2, T)
        gl = take(2, T)
        pcf = take(2, 4)
        x_out = conv_rows
        assert top[0] <= SPLIT_AT
        top[0] = BASE
        y_rows = take(3, D)

        S = {n: sem(n) for n in """
            x_loaded mem_loaded const_loaded par_loaded pages_loaded wik_loaded ikpage_loaded rel_loaded
            slab_used bank_free act_step dve_step pool_step small_set
            sumsq_done var_ready seed_ready diag_ready par_T par_evac lb_max lb_exp
            row_T x_evac h_evac m_evac
            ik_mm ik_evac idx_zero iw_T iw_evac idx_mm idx_free page_T page_evac dup_ready iqs_ready
            sidx_mm sidx_relu sidx_sum selected out_T out_evac out_sent memo_sent
            bias_mm bias_evac bias_stored bias_loaded
            q_staged v_staged bm_ready s_mm s_read s_max s_exp s_prob p_T p_evac pv_mm o_evac
            kv_loaded0 kv_loaded1 kt_T kt_evac b_staged
            f_ready logf_ready d_ready e_ready qk_ready a_mm aT_ready ke_T keN_ready s1_mm s1_ready st_mm
            vm_ready o_mm osq_ready ss_mm v_ready r_seed st_ready state_sent head_done pcol_ready
            sold_loaded0 sold_loaded1
            n_sum n_mm n_var n_seed n_t n_x n_sq n_h slab_hi slab_lo in_hi in_lo
            kx_loaded0 kx_loaded1 kx_T kx_edve kx_eact kx_used sx_evac sx_T sx_max sx_exp sx_prob sx_pT sx_pevac
            px_max px_exp px_prob px_T px_evac vx_mm vx_evac
            conv_loaded conv_T conv_evac ctx_ready c_ready g_ready y_done cn_T cn_evac xo_T xo_edve xo_eact final_sent
            """.split()}
        N = type("Semaphores", (), S)
        slab_ready = [sem(f"slab{j}_ready") for j in range(R)]
        kv_loaded = [N.kv_loaded0, N.kv_loaded1]
        sold_loaded = [N.sold_loaded0, N.sold_loaded1]
        kx_loaded = [N.kx_loaded0, N.kx_loaded1]

        w_in = A["w_in"][0].rearrange("(k p) n -> p k n", p=P)
        B_IQ, B_K, B_V, B_QQ, B_MEM = 0, 8, 12, 16, 32
        B_HG = 64
        B_OUT = B_HG + 6 * NHG
        B_XQ, B_XO = B_OUT + KD, B_OUT + 2 * KD
        B_UP = B_XO + KD
        B_DOWN = B_UP + 2 * FT
        B_END = B_DOWN + R * KD
        SPLIT_OUT = 4
        SPLIT_XQ = SPLIT_OUT + KD
        SPLIT_XO = SPLIT_XQ + 4
        SPLIT_UP = SPLIT_XO + KD
        FREE = 2
        ATT_S = float(P) ** -0.5
        X_S = float(512) ** -0.5
        TOK = [(0, P), (P, P), (SEQ, NS)]
        x_rows_of = [A["x_prompt"][0, 0:P], A["x_prompt"][0, P:SEQ], A["x_sample"].rearrange("b t d -> (b t) d")]
        mem_rows_of = A["mem_prompt"][0].rearrange("(m p) d -> p m d", p=P)
        new_k = O["new_k_prompt"][0, 0].rearrange("(m p) h d -> p m (h d)", p=P)
        new_v = O["new_v_prompt"][0, 0].rearrange("(m p) h d -> p m (h d)", p=P)
        new_ik = O["new_idx_k_prompt"][0, 0].rearrange("(m p) d -> p m d", p=P)
        new_ks = O["new_k_sample"][0].rearrange("b t h d -> (b t) (h d)")
        new_vs = O["new_v_sample"][0].rearrange("b t h d -> (b t) (h d)")
        new_iks = O["new_idx_k_sample"][0].rearrange("b t d -> (b t) d")
        new_mk = O["new_mem_k_prompt"][0, 0].rearrange("(m p) h d -> p m (h d)", p=P)
        new_mv = O["new_mem_v_prompt"][0, 0].rearrange("(m p) h d -> p m (h d)", p=P)
        mem_k = A["cache_mem_k"][0].rearrange("b (m p) h d -> b p m (h d)", p=P)
        mem_v = A["cache_mem_v"][0].rearrange("b (m p) h d -> b p m (h d)", p=P)
        hg_in = A["state_hgrn"][0].rearrange("b h c v -> h c b v")
        hg_out_s = O["new_hgrn_sample"][0].rearrange("b h c v -> h c b v")
        hg_out_p = O["new_hgrn_prompt"][0, 0]
        iq_cols = iq_s.rearrange("p b (j t) -> p b j t", t=DT)

        def two_back(it, per, g):
            return it * per + max(g - 1, 0)

        block = ctx.enter_context(nc.Block())

        @block.sync
        def _(sp):
            for m, (_, rows) in enumerate(TOK):
                sp.dma_start(x_rows[0:rows, m, :], x_rows_of[m]).then_inc(N.x_loaded, 16)
            sp.dma_start(m_rows, mem_rows_of).then_inc(N.mem_loaded, 16)

            def slab(s, j, src):
                sp.wait_ge(N.slab_used, s - (R - 1))
                sp.dma_start(ring[:, j], src).then_inc(slab_ready[j], 16)

            def stretch(s0, tiles, w, col):
                with sp.Fori(0, tiles // R) as it:
                    for j in range(R):
                        slab(it * R + s0 + j, j, w[:, :, ds(it * (R * P) + col + j * P, P)])

            for j in range(R):
                sp.dma_start(ring[:, j], w_in[:, :, O_IQ + j * P:O_IQ + (j + 1) * P]).then_inc(slab_ready[j], 16)
            sp.wait_ge(N.row_T, 3 * KD)
            sp.dma_start(w_ik[:, :, 0:80], w_in[:, :, O_IW:O_IW + 80]).then_inc(N.wik_loaded, 16)
            sp.dma_start(w_ik[:, :, 80:144], w_in[:, :, O_IK:O_IK + 64]).then_inc(N.wik_loaded, 16)
            stretch(B_IQ + R, 4, w_in, O_IQ + R * P)
            stretch(B_K, 8, w_in, O_K)
            stretch(B_QQ, 16, w_in, O_Q)
            for w, s0 in ((A["w_xk"], B_MEM), (A["w_xv"], B_MEM + 16)):
                stretch(s0, 16, w[0].rearrange("(k p) n -> p k n", p=P), 0)
            with sp.Fori(0, NHG // 2) as it:
                for e in range(2):
                    for g, col in enumerate((O_HF, O_HQ, O_HI, O_HG, O_GA, O_GB)):
                        n = 6 * e + g
                        slab(it * 12 + B_HG + n, n % R, w_in[:, :, ds(it * (2 * P) + col + e * P, P)])
                        if g == 4:
                            sp.wait_ge(N.head_done, two_back(it, 2, e))
                            sp.dma_start(s_old[:, e], hg_in[ds(it * 2 + e, 1)].rearrange("o c b v -> (o c) b v"))\
                              .then_inc(sold_loaded[e], 16)
            stretch(B_OUT, 16, A["w_out"][0].rearrange("(k p) n -> p k n", p=P), 0)
            sp.wait_ge(N.head_done, NHG)
            sp.wait_ge(N.state_sent, 32 * NHG)
            for n in range(2):
                sp.dma_start(kx[:, n], mem_k[n]).then_inc(kx_loaded[n], 16)
            stretch(B_XQ, 16, A["w_xq"][0].rearrange("(k p) n -> p k n", p=P), 0)
            with sp.Fori(0, 3) as it:
                for e in range(2):
                    sp.wait_ge(N.kx_used, it * 2 + e + 1)
                    sp.dma_start(kx[:, e], mem_k[ds(it * 2 + 2 + e, 1)].rearrange("o p m d -> (o p) m d"))\
                      .then_inc(kx_loaded[e], 16)
            sp.wait_ge(N.kx_used, 7)
            sp.wait_ge(N.memo_sent, 16 * 8)
            sp.dma_start(kx[:, 0], new_mk).then_inc(kx_loaded[0], 16)
            sp.wait_ge(N.kx_used, 8)
            sp.dma_start(kx[:, 1], new_mv).then_inc(kx_loaded[1], 16)
            sp.wait_ge(N.kx_used, 9)
            sp.dma_start(kx[:, 0], mem_v[0]).then_inc(kx_loaded[0], 16)
            sp.wait_ge(N.vx_mm, KD)
            sp.dma_start(kx[:, 1], mem_v[1]).then_inc(kx_loaded[1], 16)
            with sp.Fori(0, 3) as it:
                for e in range(2):
                    sp.wait_ge(N.vx_mm, it * 2 + e + KD + 1)
                    sp.dma_start(kx[:, e], mem_v[ds(it * 2 + e + 2, 1)].rearrange("o p m d -> (o p) m d"))\
                      .then_inc(kx_loaded[e], 16)
            stretch(B_XO, 16, A["w_xo"][0].rearrange("(k p) n -> p k n", p=P), 0)
            sp.wait_ge(N.vx_evac, KD + DB)
            sp.dma_start(conv_rows[0:16, :], A["state_conv"][0].rearrange("b j f -> (b j) f"))\
              .then_inc(N.conv_loaded, 16)
            w_up = A["w_up"][0].rearrange("(k p) n -> p k n", p=P)
            with sp.Fori(0, FT // 2) as it:
                for j in range(R):
                    slab(it * R + B_UP + j, j, w_up[:, :, ds(it * (2 * P) + (j % 2) * FF + (j // 2) * P, P)])
            w_down = A["w_down"][0].rearrange("(k p) n -> p k n", p=P)
            with sp.Fori(0, KD) as it:
                for j in range(R):
                    sp.wait_ge(N.slab_used, it * R + B_DOWN + j - (R - 1))
                    sp.dma_start(ring[:, j, 0:DOWN_K], w_down[:, j * DOWN_K:(j + 1) * DOWN_K, ds(it * P, P)])\
                      .then_inc(slab_ready[j], 16)
            sp.wait_ge(N.xo_edve, 6)
            sp.wait_ge(N.xo_eact, 6)
            sp.dma_start(O["y_prompt"][0].rearrange("(m p) d -> p m d", p=P), y_rows[:, 0:2]).then_inc(N.final_sent, 16)
            sp.dma_start(O["y_sample"].rearrange("b t d -> (b t) d"), y_rows[0:NS, 2]).then_inc(N.final_sent, 16)
            sp.wait_ge(N.cn_evac, 11)
            sp.dma_start(O["new_conv_prompt"][0, 0], x_out[0:2, :]).then_inc(N.final_sent, 16)
            sp.dma_start(O["new_conv_sample"][0].rearrange("b j f -> (b j) f"), x_out[2:18, :])\
              .then_inc(N.final_sent, 16)
            sp.wait_ge(N.final_sent, 64)

        @block.tensor
        def _(pe):
            mm, tr = nc.tensor.matmul, nc.tensor.transpose

            def project(s0, tiles, rhs, n=T):
                with pe.Fori(0, tiles // R) as it:
                    for j in range(R):
                        pe.wait_ge(slab_ready[j], it * 16 + 16 * (s0 // R + 1))
                        pe.wait_ge(N.bank_free, it * R + s0 + j + FREE - 1)
                        for k in range(KD):
                            last = mm(bank(j % 2)[:, 0:n], ring[:, j, k, :], rhs[:, k, :], start=k == 0, stop=k == KD - 1)
                        last.then_inc(N.slab_used, 1)

            def project_split(s0, tiles, lo, split):
                pe.wait_ge(N.in_lo, split)
                with pe.Fori(0, tiles // R) as it:
                    for j in range(R):
                        pe.wait_ge(N.slab_lo, it * R + s0 - B_OUT + j + 1)
                        pe.wait_ge(N.bank_free, it * R + s0 + j + FREE - 1)
                        for k in range(KD):
                            wh = w_hi[:, j % 2, k, :]
                            mm(bank(j % 2)[:, 0:T], wh, x_hi[:, k, :], start=k == 0, stop=False)
                            mm(bank(j % 2)[:, 0:T], wh, lo[:, k, :], start=False, stop=False)
                            last = mm(bank(j % 2)[:, 0:T], w_lo[:, j, k, :], x_hi[:, k, :], start=False, stop=k == KD - 1)
                        last.then_inc(N.slab_used, 1)

            def project_rows(s_ready, j, free, xx, tiles):
                pe.wait_ge(slab_ready[j], s_ready)
                pe.wait_ge(N.bank_free, free)
                for m, (t0, rows) in enumerate(tiles):
                    for k in range(KD):
                        last = mm(bank(j % 2)[0:rows, m * P:(m + 1) * P], xx[:, k, t0:t0 + rows], ring[:, j, k, :],
                                  start=k == 0, stop=k == KD - 1)
                last.then_inc(N.slab_used, 1)

            pe.wait_ge(N.const_loaded, 16)
            pe.wait_ge(N.par_loaded, PAR_DMAS * 16)
            for g, rows in enumerate(PAR_ROWS):
                last = tr(bank(6)[:, g * P:g * P + rows], par_rows[0:rows, g, :], ident[0:rows, 0:rows])
            last.then_inc(N.par_T, 1)
            pe.wait_ge(N.x_loaded, 48)
            pe.wait_ge(N.mem_loaded, 16)
            pe.wait_ge(N.diag_ready, 1)
            for f in range(KD):
                fc = slice(f * P, (f + 1) * P)
                if f >= 2:
                    pe.wait_ge(N.x_evac, f - 1)
                for m, (t0, rows) in enumerate(TOK):
                    last = tr(bank(f % 2)[:, t0:t0 + rows], x_rows[0:rows, m, fc], ident[0:rows, 0:rows])
                last.then_inc(N.row_T, 1)
                if f >= 2:
                    pe.wait_ge(N.h_evac, f - 1)
                for m, (t0, rows) in enumerate(TOK):
                    last = mm(bank(2 + f % 2)[:, t0:t0 + rows], x_rows[0:rows, m, fc], diag[0:rows, m, 0:rows],
                              start=True, stop=True)
                last.then_inc(N.row_T, 1)
                if f >= 2:
                    pe.wait_ge(N.m_evac, f - 1)
                for m in range(2):
                    last = mm(bank(4 + f % 2)[:, m * P:(m + 1) * P], m_rows[:, m, fc], diag[:, 3 + m, :],
                              start=True, stop=True)
                last.then_inc(N.row_T, 1)
            pe.wait_ge(N.h_evac, KD)

            project(B_IQ, 8, hT)
            pe.wait_ge(N.wik_loaded, 32)
            pe.wait_ge(N.m_evac, KD)
            for b, (c0, c1) in ((2, (16, 144)), (3, (0, 16))):
                for k in range(KD):
                    last = mm(bank(b)[0:c1 - c0, 0:T], w_ik[:, k, c0:c1], hT[:, k, :], start=k == 0, stop=k == KD - 1)
                last.then_inc(N.ik_mm, 1)
            project(B_K, 4, hT)
            for j in range(R):
                project_rows(16 * (B_V // R + 1), j, B_V + j + FREE - 1, hT, TOK)

            pe.wait_ge(N.ik_evac, 4)
            for m in range(2):
                tr(bank(4)[:, m * H:(m + 1) * H], iwT[0:H, m * P:(m + 1) * P], ident[0:H, 0:H])
            mm(bank(4)[:, 64:64 + NS], const("heads_of", H), iwT[0:H, SEQ:T], start=True, stop=True).then_inc(N.iw_T, 1)
            pe.wait_ge(N.iw_evac, 2)
            pe.wait_ge(N.idx_zero, 2)
            for n in range(16):
                qt, j = n // 8, n % 8
                if n >= 6:
                    pe.wait_ge(N.idx_free, n - 5)
                kk = P * (qt + 1)
                mm(bank(2 + n % 6)[:, 0:2 * kk], iqT[:, j, qt * P:(qt + 1) * P], ikz[:, :, 0:kk],
                   start=True, stop=True).then_inc(N.idx_mm, 1)
            pe.wait_ge(N.idx_free, 16)
            pe.wait_ge(N.dup_ready, 1)
            for i in range(4):
                for q in range(4):
                    last = tr(bank(2 + i)[:, q * P:(q + 1) * P], ik_dup[:, 4 * i + q].rearrange("p a d -> p (a d)"), ident)
                last.then_inc(N.page_T, 1)
            pe.wait_ge(N.page_evac, 5)
            pe.wait_ge(N.iqs_ready, 2)

            def sample_scores(b):
                if b >= 2:
                    pe.wait_ge(N.sidx_relu, b - 1)
                mm(bank(6 + b % 2)[:, 0:L_S], iq_s[:, b], ik_all[:, b], start=True, stop=True).then_inc(N.sidx_mm, 1)

            def sample_sum(b):
                pe.wait_ge(N.sidx_relu, b + 1)
                mm(bank(2)[0:NS, 0:L_S], w_sel[:, b], relu_s[:, b % 2], start=b == 0, stop=b == DB - 1)\
                    .then_inc(N.sidx_sum, 1)

            sample_scores(0)
            for b in range(1, DB):
                sample_scores(b)
                sample_sum(b - 1)
            sample_sum(DB - 1)
            for m, (t0, rows) in enumerate(TOK):
                for h in range(KVH):
                    last = tr(bank(3 + m)[0:rows, h * P:(h + 1) * P], kT[:, h, t0:t0 + rows], ident)
                last.then_inc(N.out_T, 1)
            for m, (t0, rows) in enumerate(TOK):
                last = tr(bank(6)[0:rows, m * IDX:(m + 1) * IDX], ikd[0:IDX, t0:t0 + rows], ident[0:IDX, 0:IDX])
            last.then_inc(N.out_T, 1)

            project(B_QQ, 16, hT)
            with pe.Fori(0, 8) as it:
                for j in range(R):
                    project_rows(it * 16 + 16 * (B_MEM // R + 1), j, it * R + B_MEM + j + FREE - 1, mT, TOK[:2])

            pe.wait_ge(N.rel_loaded, 16)
            mm(bank(7)[0:H, 0:NDIST], rel_sb[0:NB, :], const("dist", NB), start=True, stop=True).then_inc(N.bias_mm, 1)

            def scores(it, g):
                pe.wait_ge(N.s_read, two_back(it, QPK, g))
                b = bank(2 + g % 2)
                mm(b[:, 0:P], qs[:, g, 0:P], kT[:, ds(it, 1), 0:P].rearrange("p o k -> p (o k)"), start=True, stop=True)
                mm(b[:, P:3 * P], qs[:, g, P:SEQ], kT[:, ds(it, 1), 0:SEQ].rearrange("p o k -> p (o k)"),
                   start=True, stop=True).then_inc(N.s_mm, 1)

            def weigh(it, g):
                pe.wait_ge(N.s_prob, it * QPK + g + 1)
                pe.wait_ge(N.p_evac, two_back(it, QPK, g))
                b = bank(4 + g % 2)
                for i, (src) in enumerate((0, P, 2 * P)):
                    last = tr(b[:, i * P:(i + 1) * P], prob[:, g % 2, src:src + P], ident)
                last.then_inc(N.p_T, 1)
                pe.wait_ge(N.p_evac, it * QPK + g + 1)
                pe.wait_ge(N.o_evac, two_back(it, QPK, g))
                o = bank(6 + g % 2)
                mm(o[:, 0:SEQ], vs[:, 0], probT[:, g % 2, 0:SEQ], start=True, stop=False)
                mm(o[:, P:SEQ], vs[:, 1], probT[:, g % 2, SEQ:384], start=False, stop=True).then_inc(N.pv_mm, 1)

            pe.wait_ge(N.bias_evac, 1)
            with pe.Fori(0, KVH) as it:
                pe.wait_ge(N.q_staged, it + 1)
                pe.wait_ge(N.v_staged, it + 1)
                scores(it, 0)
                for g in range(1, QPK):
                    scores(it, g)
                    weigh(it, g - 1)
                weigh(it, QPK - 1)

            with pe.Fori(0, DB // 2) as it:
                for e in range(2):
                    n1 = it * 2 + e + 1
                    pe.wait_ge(kv_loaded[e], it * 64 + 64)
                    pe.wait_ge(N.kt_evac, it * 4 + 2 * e)
                    pe.wait_ge(N.s_read, it * 2 + e + H)
                    for i in range(2):
                        for hh in range(2):
                            for pg in range(NPG):
                                h = 2 * i + hh
                                last = tr(bank(2 + i)[:, (2 * hh + pg) * P:(2 * hh + pg + 1) * P],
                                          k_page[:, e, pg, h * P:(h + 1) * P], ident)
                        last.then_inc(N.kt_T, 1)
                    pe.wait_ge(N.b_staged, it * 4 + 2 * e + 2)
                    pe.wait_ge(N.kt_evac, it * 4 + 2 * e + 2)
                    s = bank(4)
                    mm(s[:, 0:T], rep_b[0:NS, e], sel_s[0:NS, :], start=True, stop=False, skip_group_check=True)
                    for h in range(KVH):
                        q4 = q_b[:, e, 4 * h:4 * h + 4, :].rearrange("p g t -> p (g t)")
                        mm(s[32 * h:32 * h + 32, 0:PAST], q4, ktp[:, h, :], start=False, stop=False,
                           skip_group_check=True)
                        last = mm(s[32 * h:32 * h + 32, PAST:T], q4, kT[:, h, SEQ:T], start=False, stop=True,
                                  skip_group_check=True)
                    last.then_inc(N.s_mm, 1)
                    pe.wait_ge(N.s_prob, n1 + H)
                    pe.wait_ge(N.p_evac, it * 2 + e + H)
                    for i in range(2):
                        tr(bank(5)[:, i * P:(i + 1) * P], prob[:, e, i * P:(i + 1) * P], ident)
                    tr(bank(5)[0:NS, 2 * P:3 * P], prob[:, e, PAST:T], ident).then_inc(N.p_T, 1)
                    pe.wait_ge(N.p_evac, n1 + H)
                    pe.wait_ge(N.o_evac, it * 2 + e + H)
                    for h in range(KVH):
                        oc = slice(32 * h, 32 * h + 32)
                        for pg in range(NPG):
                            mm(bank(6)[:, oc], v_page[:, e, pg, h * P:(h + 1) * P],
                               probT[:, e, pg * P + 32 * h:pg * P + 32 * h + 32], start=pg == 0, stop=False)
                        last = mm(bank(6)[:, oc], vN[0:NS, 2, h * P:(h + 1) * P],
                                  probT[0:NS, e, 2 * P + 32 * h:2 * P + 32 * h + 32], start=False, stop=True)
                    last.then_inc(N.pv_mm, 1)
            pe.wait_ge(N.o_evac, H + DB)

            def head(it, e):
                k1 = it * 2 + e + 1

                def tile(g):
                    n = 6 * e + g
                    return it * 48 + 16 * ((B_HG + n) // R + 1), n % R, it * 12 + B_HG + n + FREE - 1

                def project_one(g):
                    ready, j, free = tile(g)
                    pe.wait_ge(slab_ready[j], ready)
                    pe.wait_ge(N.bank_free, free)
                    for k in range(KD):
                        last = mm(bank(j % 2)[:, 0:T], ring[:, j, k, :], hT[:, k, :], start=k == 0, stop=k == KD - 1)
                    last.then_inc(N.slab_used, 1)

                project_one(0)
                project_one(1)
                ready, j, free = tile(2)
                project_rows(ready, j, free, hT, TOK)
                project_one(3)
                pe.wait_ge(N.head_done, it * 2 + e)
                pe.wait_ge(N.qk_ready, k1)
                for b in range(2):
                    c = slice(b * P, (b + 1) * P)
                    for l in range(LV + 1):
                        kk, qq = (lev[:, l, c], levq[:, l, c]) if l < LV else (f_k[:, c], hq[:, c])
                        last = mm(bank(2 + 2 * b + l // 4)[:, (l % 4) * P:(l % 4 + 1) * P], kk, qq, start=True, stop=True)
                    last.then_inc(N.a_mm, 1)
                for l in range(LVS + 1):
                    kk, qq = (lev[:, l, SEQ:T], levq[:, l, SEQ:T]) if l < LVS else (f_k[:, SEQ:T], hq[:, SEQ:T])
                    last = mm(bank(6)[0:NS, l * NS:(l + 1) * NS], kk, qq, start=True, stop=True)
                last.then_inc(N.a_mm, 1)
                for m, (t0, rows) in enumerate(TOK):
                    last = tr(bank(7)[0:rows, m * P:(m + 1) * P], ke[:, t0:t0 + rows], ident)
                last.then_inc(N.ke_T, 1)
                project_one(4)
                pe.wait_ge(N.keN_ready, k1)
                pe.wait_ge(N.aT_ready, k1)
                mm(bank(4)[:, 0:P], keN[:, 0], vh[:, 0], start=True, stop=True).then_inc(N.s1_mm, 1)
                mm(bank(5)[:, 0:P], keN[:, 1], vh[:, 1], start=True, stop=True)
                pe.wait_ge(N.vm_ready, k1)
                for i in range(2):
                    last = mm(bank(2 + i)[:, 0:512], keN[0:NS, 2], v_m[0:NS, 4 * i:4 * i + 4, :], start=True, stop=True)
                last.then_inc(N.st_mm, 1)
                o = bank(6)
                mm(o[:, 0:P], vh[:, 0], a_T[:, 0], start=True, stop=True)
                mm(o[:, P:SEQ], vh[:, 1], a_T[:, 1], start=True, stop=False)
                pe.wait_ge(N.s1_ready, k1)
                mm(o[:, P:SEQ], s1, qb[:, P:SEQ], start=False, stop=True)
                mm(o[:, SEQ:T], vh[0:NS, 2], a_T[0:NS, 2, 0:NS], start=True, stop=False, skip_group_check=True)
                pe.wait_ge(sold_loaded[e], it * 16 + 16)
                for b in range(DB):
                    c = slice(SEQ + b * DT, SEQ + (b + 1) * DT)
                    last = mm(o[:, c], s_old[:, e, b], qb[:, c], start=False, stop=b == DB - 1, skip_group_check=True)
                last.then_inc(N.o_mm, 1)
                project_one(5)
                pe.wait_ge(N.osq_ready, k1)
                mm(bank(7)[:, 0:T], ones, osq, start=True, stop=True).then_inc(N.ss_mm, 1)

            with pe.Fori(0, NHG // 2) as it:
                head(it, 0)
                head(it, 1)

            def norm_sums(i, pre):
                pe.wait_ge(N.n_sum, i + 1)
                mm(bank(2)[:, 0:T], ones, sqacc, start=True, stop=True).then_inc(N.n_mm, 1)
                if pre:
                    for f in range(KD):
                        pe.wait_ge(N.n_sq, i * KD + f + 1)
                        last = mm(bank(3)[:, 0:T], ones, sqbuf[:, f % 2], start=f == 0, stop=f == KD - 1)
                        last.then_inc(N.n_mm, 1)

            pe.wait_ge(N.head_done, NHG)
            project_split(B_OUT, 16, u_lo, SPLIT_OUT)
            norm_sums(0, True)
            project_split(B_XQ, 16, h_lo, SPLIT_XQ)
            pe.wait_ge(N.bank_free, B_XQ + KD + FREE)

            def chunk_T(c, e):
                for dt in range(XD):
                    last = tr(bank(2 + c % 2)[:, dt * P:(dt + 1) * P],
                              kx[:, e, c % 2, (c // 2) * 512 + dt * P:(c // 2) * 512 + (dt + 1) * P], ident)
                last.then_inc(N.kx_T, 1)

            def chunk_evac_wait(half, c):
                pe.wait_ge(N.kx_eact if c % 2 else N.kx_edve, half + c // 2 + 1)

            def sample_chunk(it, e, c):
                chunk_evac_wait((it * 2 + e) * 4, c)
                x, mt = c // 2, c % 2
                for dt in range(XD):
                    last = mm(bank(0)[:, ds(it * 64 + mt * 256 + e * 32 + x * 8, 8)], kxT[:, mt, dt],
                              qx[:, 4 * x + dt, ds(it * 16 + SEQ + e * DT, DT)], start=dt == 0, stop=dt == XD - 1)
                if c == 7:
                    last.then_inc(N.kx_used, 1)

            with pe.Fori(0, DB // 2) as it:
                for e in range(2):
                    pe.wait_ge(kx_loaded[e], it * 16 + 16)
                    chunk_T(0, e)
                    for c in range(1, 8):
                        chunk_T(c, e)
                        sample_chunk(it, e, c - 1)
                    sample_chunk(it, e, 7)

            def prompt_chunk(c):
                chunk_evac_wait(32, c)
                x, mt = c // 2, c % 2
                for qt in range(2):
                    for dt in range(XD):
                        last = mm(bank(4 + 2 * qt + x // 2)[:, (x % 2) * 256 + mt * P:(x % 2) * 256 + (mt + 1) * P],
                                  qx[:, 4 * x + dt, qt * P:(qt + 1) * P], kxT[:, mt, dt], start=dt == 0, stop=dt == XD - 1)
                if c == 7:
                    last.then_inc(N.kx_used, 1)

            pe.wait_ge(kx_loaded[0], 5 * 16)
            chunk_T(0, 0)
            for c in range(1, 8):
                chunk_T(c, 0)
                prompt_chunk(c - 1)
            prompt_chunk(7)
            pe.wait_ge(N.sx_evac, 1)
            for rt in range(2):
                for mt in range(2):
                    last = tr(bank(1)[:, rt * 256 + mt * P:rt * 256 + (mt + 1) * P],
                              sxT[:, mt, rt * P:(rt + 1) * P], ident)
            last.then_inc(N.sx_T, 1)
            pe.wait_ge(kx_loaded[1], 5 * 16)
            for x in range(XH):
                pe.wait_ge(N.px_prob, 2)
                if x >= 2:
                    pe.wait_ge(N.px_evac, x - 1)
                for mt in range(2):
                    for qt in range(2):
                        last = tr(bank(2 + x % 2)[:, mt * 256 + qt * P:mt * 256 + (qt + 1) * P],
                                  pp[:, qt, x, mt * P:(mt + 1) * P], ident)
                last.then_inc(N.px_T, 1)
                pe.wait_ge(N.px_evac, x + 1)
                for dt in range(XD):
                    n = x * XD + dt
                    if n >= 2:
                        pe.wait_ge(N.vx_evac, n - 1)
                    for mt in range(2):
                        last = mm(bank(4 + n % 2)[:, 0:SEQ], kx[:, 1, mt, n * P:(n + 1) * P],
                                  ppT[:, x % 2, mt * 256:(mt + 1) * 256], start=mt == 0, stop=mt == 1)
                    last.then_inc(N.vx_mm, 1)
            pe.wait_ge(N.sx_prob, 2)
            for mt in range(2):
                for rt in range(2):
                    last = tr(bank(6)[:, mt * 256 + rt * P:mt * 256 + (rt + 1) * P], px[:, rt, mt * P:(mt + 1) * P], ident)
            last.then_inc(N.sx_pT, 1)
            pe.wait_ge(N.sx_pevac, 1)
            with pe.Fori(0, DB // 2) as it:
                for e in range(2):
                    pe.wait_ge(kx_loaded[e], it * 16 + 6 * 16)
                    pe.wait_ge(N.vx_evac, it * 2 + max(e - 1, 0) + 16)
                    for n in range(KD):
                        for mt in range(2):
                            last = mm(bank(2 + e)[:, n * DT:(n + 1) * DT], kx[:, e, mt, n * P:(n + 1) * P],
                                      pxT[:, mt, ds(it * 64 + e * 32 + (n // 4) * 8, DT)], start=mt == 0, stop=mt == 1)
                    last.then_inc(N.vx_mm, 1)
            pe.wait_ge(N.vx_evac, 16 + DB)
            project_split(B_XO, 16, q_lo, SPLIT_XO)
            norm_sums(1, True)
            pe.wait_ge(N.conv_loaded, 16)
            for f in range(FT):
                last = tr(bank(4 + f // 32)[:, (f % 32) * 16:(f % 32) * 16 + 16], conv_rows[0:16, f * P:(f + 1) * P],
                          ident[0:16, 0:16])
            last.then_inc(N.conv_T, 1)
            project_split(B_UP, 2 * FT, h_lo, SPLIT_UP)
            pe.wait_ge(N.y_done, FT)
            with pe.Fori(0, KD // 2) as it:
                for e in range(2):
                    pe.wait_ge(N.bank_free, it * 2 + B_DOWN + e + FREE - 1)
                    for j in range(R):
                        pe.wait_ge(slab_ready[j], it * 32 + 16 * (B_DOWN // R + e + 1))
                        for k in range(DOWN_K):
                            kk = j * DOWN_K + k
                            last = mm(bank(e)[:, 0:T], ring[:, j, k, :], yT[:, kk, :], start=kk == 0, stop=kk == FT - 1)
                        last.then_inc(N.slab_used, 1)
            norm_sums(2, False)
            for f in range(FT):
                g, c = f // 4, f % 4
                if c == 0 and g >= 2:
                    pe.wait_ge(N.cn_evac, g - 1)
                last = tr(bank(4 + g % 2)[0:18, c * P:(c + 1) * P], conv_new[:, f, :], ident)
                if c == 3:
                    last.then_inc(N.cn_T, 1)
            pe.wait_ge(N.n_x, 3 * KD)
            i = 0
            for m, (t0, rows) in enumerate(TOK):
                for g in range(4):
                    if i >= 2:
                        pe.wait_ge(N.xo_eact if i % 2 else N.xo_edve, (i - 2) // 2 + 1)
                    for c in range(4):
                        last = tr(bank(6 + i % 2)[0:rows, c * P:(c + 1) * P], xT[:, 4 * g + c, t0:t0 + rows], ident)
                    last.then_inc(N.xo_T, 1)
                    i += 1

        @block.vector
        def _(dve):
            V = nc.vector
            st = Steps(dve, N.dve_step)

            def refine(r, v, tmp):
                st.then(V.tensor_tensor(tmp, r, r, ALU.mult))
                st.then(V.tensor_tensor(tmp, tmp, v, ALU.mult))
                st.then(V.tensor_scalar(tmp, tmp, -0.5, 1.5, ALU.mult, ALU.add))
                return V.tensor_tensor(r, r, tmp, ALU.mult)

            V.memset(small, 1.0).then_inc(N.small_set, 1)
            dve.wait_ge(N.sumsq_done, 5)
            V.tensor_scalar(small[:, 8:13], small[:, 0:5], 1.0 / D, EPS, ALU.mult, ALU.add).then_inc(N.var_ready, 1)
            dve.wait_ge(N.var_ready, 1)
            dve.wait_ge(N.par_T, 1)
            for g, rows in enumerate(PAR_ROWS):
                last = V.tensor_copy(par[:, g, 0:rows], bank(6)[:, g * P:g * P + rows])
            last.then_inc(N.par_evac, 1)
            dve.wait_ge(N.seed_ready, 1)
            st.then(refine(small[:, 24:29], small[:, 8:13], small[:, 32:37]))
            dve.wait_ge(N.const_loaded, 16)
            for i in range(5):
                last = V.tensor_scalar(diag[:, i], ident, small[:, 24 + i:25 + i], None, ALU.mult)
            last.then_inc(N.diag_ready, 1)
            dve.wait_ge(N.par_evac, 1)
            l0, l1 = par[:, 1, 0:16], par[:, 1, 16:32]
            t0_, t1_, t2_, t3_ = [sqbuf[:, 0, 16 * i:16 * i + 16] for i in range(4)]
            st.then(V.tensor_tensor(t0_, l0, l1, ALU.max))
            st.then(V.tensor_tensor(t1_, l0, t0_, ALU.subtract))
            V.tensor_tensor(t2_, l1, t0_, ALU.subtract).then_inc(N.lb_max, 1)
            dve.wait_ge(N.lb_exp, 1)
            st.then(V.tensor_tensor(t0_, t1_, t2_, ALU.add))
            st.then(V.reciprocal(t3_, t0_))
            st.then(V.tensor_tensor(t1_, t1_, t3_, ALU.mult))
            st.then(V.tensor_tensor(t2_, t2_, t3_, ALU.mult))
            st.then(V.tensor_tensor(t2_, t1_, t2_, ALU.add))
            st.then(V.tensor_tensor(head_par[:, :, 0], t2_, t1_, ALU.subtract))
            st.did(V.tensor_scalar(head_par[:, :, 1], head_par[:, :, 0], -1.0, 1.0, ALU.mult, ALU.add))
            st.did(V.tensor_copy(head_par[:, :, 2], G_HG))
            for i, src in enumerate((par[:, 1, 76:120], par[:, 2, 0:44], par[:, 2, 44:88], par[:, 1, 32:76])):
                st.did(V.tensor_copy(conv_par[:, :, i], src))
            st.sync()
            for f in range(KD - 2):
                dve.wait_ge(N.row_T, 3 * f + 1)
                V.tensor_copy(xT[:, f], bank(f % 2)[:, 0:T]).then_inc(N.x_evac, 1)

            dve.wait_ge(N.idx_zero, 2)
            dve.wait_ge(N.bank_free, 8 + FREE)
            for par_, off in ((0, 0), (1, 64)):
                rows = slice(off, off + 64)
                V.tensor_copy(iq_s[rows, :, off:off + 64].rearrange("p b (j t) -> p b j t", t=DT),
                              iqT[rows, :, SEQ:T].rearrange("p j (b t) -> p b j t", t=DT)).then_inc(N.iqs_ready, 1)
            dve.wait_ge(N.iw_T, 1)
            V.tensor_copy(iwN.rearrange("p a h -> p (a h)"), bank(4)[:, 0:2 * H]).then_inc(N.iw_evac, 1)
            V.tensor_tensor(w_sel, bank(4)[:, 64:64 + NS].rearrange("p (o c) -> p o c", o=1).broadcast_to([P, DB, NS]),
                            const("w_place").rearrange("p (b c) -> p b c", b=DB), ALU.mult).then_inc(N.iw_evac, 1)
            dve.wait_ge(N.iw_evac, 2)
            for n in range(16):
                qt, j = n // 8, n % 8
                kk = P * (qt + 1)
                dve.wait_ge(N.idx_mm, n + 1)
                for hp in range(2):
                    dst = score[:, qt, 0:kk] if j == 0 and hp == 0 else score_t[:, (2 * n + hp) % 4, 0:kk]
                    ins = V.tensor_scalar(dst, bank(2 + n % 6)[:, hp * kk:(hp + 1) * kk], 0.0,
                                          iwN[:, qt, 2 * j + hp:2 * j + hp + 1], ALU.max, ALU.mult)
                    if hp == 0:
                        st.did(ins)
                ins.then_inc(N.idx_free, 1)
                st.sync()
                if j:
                    st.then(V.tensor_tensor(score[:, qt, 0:kk], score[:, qt, 0:kk], score_t[:, (2 * n) % 4, 0:kk], ALU.add))
                dve.wait_ge(N.idx_free, n + 1)
                st.then(V.tensor_tensor(score[:, qt, 0:kk], score[:, qt, 0:kk], score_t[:, (2 * n + 1) % 4, 0:kk], ALU.add))

            def top(w, rounds, rows):
                for _ in range(rounds):
                    st.then(V.max(best[0:rows], w))
                    st.then(V.match_replace(w, best[0:rows], w, -3e38))

            for qt in range(2):
                kk = P * (qt + 1)
                w = work[:, 0:kk]
                st.then(V.scalar_tensor_tensor(w, causal[:, qt, 0:kk], 1e8, score[:, qt, 0:kk], ALU.mult, ALU.add))
                top(w, TOPK_P // 8, P)
                st.then(V.tensor_scalar(w, w, -2e38, NEG, ALU.is_gt, ALU.mult))
                V.tensor_tensor(sel_p[:, qt, 0:kk], w, causal[:, qt, 0:kk], ALU.add).then_inc(N.selected, 1)
                dve.wait_ge(N.selected, qt + 1)
            dve.wait_ge(N.sidx_sum, DB)
            st.did(V.memset(work[0:NS, 0:PAD_S], 3e38))
            st.did(V.tensor_copy(work[0:NS, PAD_S:PAD_S + PAST], bank(2)[0:NS, 0:PAST]))
            st.then(V.scalar_tensor_tensor(work[0:NS, PAD_S + PAST:PAD_S + L_S], const("causal_new", NS), 1e8,
                                           bank(2)[0:NS, PAST:L_S], ALU.mult, ALU.add))
            top(work[0:NS, 0:PAD_S + L_S], (TOPK_S + PAD_S) // 8, NS)
            w = work[0:NS, PAD_S:PAD_S + L_S]
            st.then(V.tensor_scalar(w, w, -2e38, NEG, ALU.is_gt, ALU.mult))
            st.did(V.tensor_copy(sel_s[0:NS, 0:PAST], w[:, 0:PAST]))
            new = w[:, PAST:L_S]
            st.then(V.tensor_tensor(new, new, const("causal_new", NS), ALU.add))
            V.tensor_tensor(sel_s[0:NS, PAST:T].rearrange("p (b t) -> p b t", t=DT),
                            new.rearrange("p (o t) -> p o t", o=1).broadcast_to([NS, DB, DT]),
                            const("other_seq", NS).rearrange("p (b t) -> p b t", t=DT), ALU.add).then_inc(N.selected, 1)
            dve.wait_ge(N.selected, 3)

            dve.wait_ge(N.bias_mm, 1)
            V.tensor_copy(dist_sb[0:H, :], bank(7)[0:H, 0:NDIST]).then_inc(N.bias_evac, 1)
            dve.wait_ge(N.bias_loaded, 16 * BIAS_DMAS)

            def logits(it, g):
                dve.wait_ge(N.s_mm, it * QPK + g + 1)
                dve.wait_ge(N.bm_ready, it * 8 + 2 * g + 2)
                V.scalar_tensor_tensor(logit[:, g % 2], bank(2 + g % 2)[:, 0:384], ATT_S, bm[:, g % 2], ALU.mult, ALU.add)\
                    .then_inc(N.s_read, 1)
                dve.wait_ge(N.s_read, it * QPK + g + 1)
                st.did(V.tensor_reduce(smx[:, g, 0:1], logit[:, g % 2, 0:P], AX.X, ALU.max, negate=True))
                V.tensor_reduce(smx[:, g, 1:2], logit[:, g % 2, P:384], AX.X, ALU.max, negate=True).then_inc(N.s_max, 1)

            def normalise(it, g):
                dve.wait_ge(N.s_exp, it * QPK + g + 1)
                st.then(V.reciprocal(smx[:, 4 + g, 2:4], smx[:, g, 2:4]))
                st.did(V.tensor_scalar(prob[:, g % 2, 0:P], prob[:, g % 2, 0:P], smx[:, 4 + g, 2:3], None, ALU.mult))
                V.tensor_scalar(prob[:, g % 2, P:384], prob[:, g % 2, P:384], smx[:, 4 + g, 3:4], None, ALU.mult)\
                    .then_inc(N.s_prob, 1)

            with dve.Fori(0, KVH) as it:
                st.enter(it, 3 * QPK)
                dve.wait_ge(N.pv_mm, it * QPK)
                V.tensor_copy(vs, vN[:, 0:2, ds(it * P, P)]).then_inc(N.v_staged, 1)
                logits(it, 0)
                for g in range(1, QPK):
                    logits(it, g)
                    normalise(it, g - 1)
                normalise(it, QPK - 1)
            st.leave(KVH)

            with dve.Fori(0, DB // 2) as it:
                st.enter(it, 2)
                for e in range(2):
                    n1 = it * 2 + e + 1 + H
                    dve.wait_ge(N.s_mm, n1)
                    V.scalar_tensor_tensor(logit[:, e, 0:T], bank(4)[:, 0:T], ATT_S, bias_s, ALU.mult, ALU.add)\
                        .then_inc(N.s_read, 1)
                    dve.wait_ge(N.s_read, n1)
                    V.tensor_reduce(smx[:, e, 0:1], logit[:, e, 0:T], AX.X, ALU.max, negate=True).then_inc(N.s_max, 1)
                    dve.wait_ge(N.s_exp, n1)
                    st.then(V.reciprocal(smx[:, 4 + e, 2:3], smx[:, e, 2:3]))
                    V.tensor_scalar(prob[:, e, 0:T], prob[:, e, 0:T], smx[:, 4 + e, 2:3], None, ALU.mult)\
                        .then_inc(N.s_prob, 1)
            st.leave(DB // 2)
            dve.wait_ge(N.o_evac, H + DB)

            def bcast(a, n):
                return a.rearrange("p (o t) -> p o t", o=1).broadcast_to([P, n, a.shape[1]])

            def head(it, e):
                k1 = it * 2 + e + 1
                s0 = it * 12 + B_HG + 6 * e + FREE
                dve.wait_ge(N.bank_free, s0 + 1)
                dve.wait_ge(N.pcol_ready, k1)
                st.then(V.tensor_scalar(f_e, f_e, 1.0, None, ALU.add))
                st.then(V.reciprocal(f_k, f_e))
                V.tensor_scalar(f_e, f_k, pcol[:, 1:2], pcol[:, 0:1], ALU.mult, ALU.add).then_inc(N.f_ready, 1)
                dve.wait_ge(N.f_ready, k1)
                st.did(V.tensor_scalar(f_k, f_e, -1.0, 1.0, ALU.mult, ALU.add))
                dve.wait_ge(N.logf_ready, k1)
                st.then(V.tensor_tensor_scan(f_b, const("scan_keep"), eb, 0.0, ALU.mult, ALU.add))
                for l in range(LV):
                    w, half = (T if l < LVS else SEQ), 2 ** l
                    segs = w // (2 * half)
                    b4 = f_b[:, 0:w].rearrange("p (s u h) -> p s u h", u=2, h=half)
                    d4 = lev[:, l, 0:w].rearrange("p (s u h) -> p s u h", u=2, h=half)
                    mid = b4[:, :, 0, half - 1:half].broadcast_to([P, segs, half])
                    st.did(V.tensor_tensor(d4[:, :, 0, :], mid, b4[:, :, 0, :], ALU.subtract))
                    st.did(V.tensor_tensor(d4[:, :, 1, :], b4[:, :, 1, :], mid, ALU.subtract))
                for c0, c1, w in ((0, SEQ, P), (SEQ, T, DT)):
                    b3 = f_b[:, c0:c1].rearrange("p (s t) -> p s t", t=w)
                    last = V.tensor_tensor(ke[:, c0:c1].rearrange("p (s t) -> p s t", t=w),
                                           b3[:, :, w - 1:w].broadcast_to([P, (c1 - c0) // w, w]), b3, ALU.subtract)
                    if c0 == 0:
                        st.did(last)
                last.then_inc(N.d_ready, 1)
                dve.wait_ge(N.e_ready, k1)
                dve.wait_ge(N.bank_free, s0 + 2)
                st.did(V.tensor_tensor(levq[:, 0:LVS], lev[:, 0:LVS], bcast(hq, LVS), ALU.mult))
                st.did(V.tensor_tensor(levq[:, LVS:LV, 0:SEQ], lev[:, LVS:LV, 0:SEQ], bcast(hq[:, 0:SEQ], LV - LVS), ALU.mult))
                st.did(V.tensor_tensor(lev[:, 0:LVS], lev[:, 0:LVS], bcast(f_k, LVS), ALU.mult))
                st.did(V.tensor_tensor(lev[:, LVS:LV, 0:SEQ], lev[:, LVS:LV, 0:SEQ], bcast(f_k[:, 0:SEQ], LV - LVS), ALU.mult))
                st.did(V.tensor_tensor(ke, ke, f_k, ALU.mult))
                V.tensor_tensor(qb[:, P:T], eb[:, P:T], hq[:, P:T], ALU.mult).then_inc(N.qk_ready, 1)
                for b in range(3):
                    rows, nl, w = (P, LV + 1, P) if b < 2 else (NS, LVS + 1, NS)
                    src = (bank(2 + 2 * b, 2) if b < 2 else bank(6)[0:NS, 0:nl * NS]).rearrange("p (l t) -> p l t", l=nl)
                    am = a_m.rearrange("p l t -> p (l t)")[0:rows, 0:nl * w].rearrange("p (l t) -> p l t", l=nl)
                    dve.wait_ge(N.a_mm, it * 6 + 3 * e + b + 1)
                    st.then(V.tensor_tensor(am, src, level if b < 2 else level_s, ALU.mult))
                    last = V.tensor_reduce(a_T[0:rows, b, 0:w], am.rearrange("p l t -> p t l"), AX.X, ALU.add)
                    if b < 2:
                        st.then(last)
                last.then_inc(N.aT_ready, 1)
                dve.wait_ge(N.st_mm, k1)
                dve.wait_ge(N.s1_ready, k1)
                dve.wait_ge(N.state_sent, it * 64 + 32 * e)
                dve.wait_ge(sold_loaded[e], it * 16 + 16)
                st.did(V.scalar_tensor_tensor(s2, s1, eb[:, SEQ - 1:SEQ], bank(5)[:, 0:P], ALU.mult, ALU.add))
                for b in range(DB):
                    at = SEQ + (b + 1) * DT
                    last = V.scalar_tensor_tensor(s_new[:, b], s_old[:, e, b], eb[:, at - 1:at],
                                                  bank(2 + b // 4)[:, (b % 4) * P:(b % 4 + 1) * P], ALU.mult, ALU.add)
                last.then_inc(N.st_ready, 1)
                dve.wait_ge(N.ss_mm, k1)
                V.tensor_scalar(osq, bank(7)[:, 0:T], 1.0 / P, EPS, ALU.mult, ALU.add).then_inc(N.v_ready, 1)
                dve.wait_ge(N.bank_free, s0 + 6)
                st.did(V.tensor_scalar(gate[:, 0:2], gate[:, 0:2], 1.0, None, ALU.add))
                st.sync()
                st.then(V.scalar_tensor_tensor(gate[:, 1], gate[:, 2], 1.0, gate[:, 1], ALU.add, ALU.mult))
                st.then(V.reciprocal(gate[:, 0:2], gate[:, 0:2]))
                dve.wait_ge(N.r_seed, k1)
                dve.wait_ge(N.v_ready, k1)
                st.then(refine(o_r, osq, ntmp))
                st.then(V.tensor_tensor(o_n, bank(6)[:, 0:T], o_r, ALU.mult))
                st.then(V.scalar_tensor_tensor(o_n, o_n, pcol[:, 2:3], hgr, ALU.mult, ALU.mult))
                st.then(V.tensor_tensor(o_n, o_n, gate[:, 1], ALU.mult))
                st.then(V.tensor_tensor(gate[:, 0], gate[:, 0], zq[:, ds(it * 2 + e, 1)].rearrange("p o t -> p (o t)"), ALU.mult))
                V.tensor_tensor(uT[:, ds(it * 2 + e, 1)].rearrange("p o t -> p (o t)"), gate[:, 0], o_n, ALU.add)\
                    .then_inc(N.head_done, 1)

            with dve.Fori(0, NHG // 2) as it:
                st.enter(it, 2 * HEAD_STEPS)
                head(it, 0)
                head(it, 1)
            st.leave(NHG // 2)
            dve.wait_ge(N.head_done, NHG)

            def slab_low(n, j):
                dve.wait_ge(N.slab_hi, n - B_OUT + 1)
                V.tensor_tensor(w_lo[:, j], ring[:, j], w_hi[:, j % 2].bitcast(FP32), ALU.subtract).then_inc(N.slab_lo, 1)

            def squares_split(s0):
                st.then(V.memset(sqacc, 0.0))

                def four(it, last):
                    for j in range(R):
                        if j < R - 1 or not last:
                            slab_low(it * R + s0 + j + 1, (j + 1) % R)
                        y = hT[:, ds(it * R + j, 1)].rearrange("p o t -> p (o t)")
                        dve.wait_ge(N.bank_free, it * R + s0 + FREE + j + 1)
                        st.then(V.tensor_tensor(ntmp, y, y, ALU.mult))
                        st.then(V.tensor_tensor(sqacc, sqacc, ntmp, ALU.add))

                with dve.Fori(0, KD // R - 1) as it:
                    st.enter(it, 2 * R)
                    four(it, False)
                st.leave(KD // R - 1)
                four(KD // R - 1, True)
                V.memset(rstd[:, 0:1], 0.0).then_inc(N.n_sum, 1)

            def squares(i, free0):
                st.then(V.memset(sqacc, 0.0))
                with dve.Fori(0, KD // 2) as it:
                    st.enter(it, 4)
                    for e in range(2):
                        y = hT[:, ds(it * 2 + e, 1)].rearrange("p o t -> p (o t)")
                        dve.wait_ge(N.bank_free, it * 2 + free0 + e + 1)
                        st.then(V.tensor_tensor(ntmp, y, y, ALU.mult))
                        st.then(V.tensor_tensor(sqacc, sqacc, ntmp, ALU.add))
                st.leave(KD // 2)
                V.memset(rstd[:, 0:1], 0.0).then_inc(N.n_sum, 1)

            def post_norm(i, nv, g_post, g_pre, mmv):
                dve.wait_ge(N.n_mm, mmv)
                V.tensor_scalar(var, bank(2)[:, 0:T], 1.0 / D, EPS, ALU.mult, ALU.add).then_inc(N.n_var, 1)
                dve.wait_ge(N.n_seed, nv)
                dve.wait_ge(N.n_var, nv)
                st.then(refine(rstd, var, ntmp))
                for f in range(KD):
                    V.scalar_tensor_tensor(hT[:, f], hT[:, f], g_post[:, f:f + 1], rstd, ALU.mult, ALU.mult)\
                        .then_inc(N.n_t, 1)
                if g_pre is None:
                    return
                dve.wait_ge(N.n_mm, mmv + KD)
                V.tensor_scalar(var, bank(3)[:, 0:T], 1.0 / D, EPS, ALU.mult, ALU.add).then_inc(N.n_var, 1)
                dve.wait_ge(N.n_seed, nv + 1)
                dve.wait_ge(N.n_var, nv + 1)
                st.then(refine(rstd, var, ntmp))
                for f in range(KD):
                    V.scalar_tensor_tensor(hT[:, f], xT[:, f], g_pre[:, f:f + 1], rstd, ALU.mult, ALU.mult).then_inc(N.n_h, 1)
                dve.wait_ge(N.n_h, KD * (i + 1))

            slab_low(B_OUT, 0)
            squares_split(B_OUT)
            slab_low(B_XQ, 0)
            post_norm(0, 1, G_POST_MIX, G_PRE_X, 1)

            def evac_even(it, e, n0):
                for c in range(0, 8, 2):
                    cc = n0 + c if it is None else it * 16 + 8 * e + c
                    dve.wait_ge(N.kx_T, cc + 1)
                    V.tensor_copy(kxT[:, 0].rearrange("p a b -> p (a b)"), bank(2)).then_inc(N.kx_edve, 1)

            for j in range(1, R):
                slab_low(B_XQ + j, j)
            with dve.Fori(1, KD // R) as it:
                for j in range(R):
                    slab_low(it * R + B_XQ + j, j)
            with dve.Fori(0, DB // 2) as it:
                evac_even(it, 0, 0)
                evac_even(it, 1, 0)
            evac_even(None, 0, 64)
            dve.wait_ge(N.kx_used, 9)
            for qt in range(2):
                s3 = bank(4 + 2 * qt, 2).rearrange("p (x m) -> p x m", x=XH)
                st.then(V.tensor_reduce(smx2[:, qt, :], s3, AX.X, ALU.max, negate=True))
                V.tensor_scalar(smx2[:, 2 + qt, :], smx2[:, qt, :], X_S, None, ALU.mult).then_inc(N.px_max, 1)
            dve.wait_ge(N.sx_T, 1)
            s3 = bank(1).rearrange("p (r m) -> p r m", r=2)
            st.then(V.tensor_reduce(smx2[:, 6, 0:2], s3, AX.X, ALU.max, negate=True))
            V.tensor_scalar(smx2[:, 6, 2:4], smx2[:, 6, 0:2], X_S, None, ALU.mult).then_inc(N.sx_max, 1)
            for qt in range(2):
                dve.wait_ge(N.px_exp, 4 * qt + 4)
                st.then(V.reciprocal(smx2[:, qt, :], smx2[:, 4 + qt, :]))
                V.tensor_tensor(pp[:, qt], pp[:, qt], smx2[:, qt, :].rearrange("p (x o) -> p x o", o=1)
                                .broadcast_to([P, XH, MEM]), ALU.mult).then_inc(N.px_prob, 1)
            dve.wait_ge(N.sx_exp, 2)
            st.then(V.reciprocal(smx2[:, 6, 0:2], smx2[:, 7, 0:2]))
            for rt in range(2):
                V.tensor_scalar(px[:, rt], px[:, rt], smx2[:, 6, rt:rt + 1], None, ALU.mult).then_inc(N.sx_prob, 1)
            slab_low(B_XO, 0)
            squares_split(B_XO)
            for j in range(2):
                slab_low(B_UP + j, j)
            post_norm(1, 3, G_POST_X, G_PRE_FFN, 1 + KD + 1)

            dve.wait_ge(N.conv_T, 1)
            st.did(V.tensor_copy(conv_old.rearrange("p f c -> p (f c)")[:, 0:512], bank(4)))
            V.tensor_copy(conv_old.rearrange("p f c -> p (f c)")[:, 512:FT * 16], bank(5)[:, 0:FT * 16 - 512])\
                .then_inc(N.conv_evac, 1)
            st.did(V.memset(a_ext[:, :, 0:2], 0.0))
            st.sync()
            def conv_gate(it, e, more):
                f1 = it * 2 + e + 1
                if more:
                    slab_low(it * R + B_UP + 2 * e + 2, (2 * e + 2) % R)
                dve.wait_ge(N.ctx_ready, it * 4 + 2 * e + 2)
                dve.wait_ge(N.bank_free, it * 4 + B_UP + 2 * e + 1 + FREE)
                ap = a_ext[:, e, 0:SEQ + 2]
                asm = a_ext[:, e, SEQ + 2:].rearrange("p (b t) -> p b t", t=DT + 2)
                cp = cv[:, e, 0:SEQ]
                cs = cv[:, e, SEQ:T].rearrange("p (b t) -> p b t", t=DT)
                st.did(V.tensor_scalar(cp, ap[:, 0:SEQ], pcf[:, e, 0:1], pcf[:, e, 3:4], ALU.mult, ALU.add))
                st.then(V.tensor_scalar(cs, asm[:, :, 0:DT], pcf[:, e, 0:1], pcf[:, e, 3:4], ALU.mult, ALU.add))
                st.did(V.scalar_tensor_tensor(cp, ap[:, 1:SEQ + 1], pcf[:, e, 1:2], cp, ALU.mult, ALU.add))
                st.then(V.scalar_tensor_tensor(cs, asm[:, :, 1:DT + 1], pcf[:, e, 1:2], cs, ALU.mult, ALU.add))
                st.did(V.scalar_tensor_tensor(cp, ap[:, 2:SEQ + 2], pcf[:, e, 2:3], cp, ALU.mult, ALU.add))
                V.scalar_tensor_tensor(cs, asm[:, :, 2:DT + 2], pcf[:, e, 2:3], cs, ALU.mult, ALU.add)\
                    .then_inc(N.c_ready, 1)
                if more:
                    slab_low(it * R + B_UP + 2 * e + 3, (2 * e + 3) % R)
                tail = conv_new[:, ds(it * 2 + e, 1), :].rearrange("p o c -> p (o c)")
                st.did(V.tensor_copy(tail[:, 0:2], ap[:, SEQ:SEQ + 2]))
                st.did(V.tensor_copy(tail[:, 2:18].rearrange("p (b t) -> p b t", t=2), asm[:, :, DT:DT + 2]))
                dve.wait_ge(N.g_ready, f1)
                V.tensor_tensor(yT[:, ds(it * 2 + e, 1)].rearrange("p o t -> p (o t)"), gl[:, e], zb[:, e], ALU.mult)\
                    .then_inc(N.y_done, 1)

            with dve.Fori(0, FT // 2 - 1) as it:
                st.enter(it, 2 * 7)
                conv_gate(it, 0, True)
                conv_gate(it, 1, True)
            st.leave(FT // 2 - 1)
            conv_gate(FT // 2 - 1, 0, True)
            conv_gate(FT // 2 - 1, 1, False)
            squares(2, B_DOWN + FREE)
            post_norm(2, 5, G_POST_FFN, None, 2 * (1 + KD) + 1)
            for i in range(0, 12, 2):
                m, g = i // 4, i % 4
                rows = TOK[m][1]
                dve.wait_ge(N.xo_T, i + 1)
                V.tensor_copy(y_rows[0:rows, m, g * 512:(g + 1) * 512], bank(6)[0:rows]).then_inc(N.xo_edve, 1)

        @block.scalar
        def _(act):
            F = nc.scalar.activation
            st = Steps(act, N.act_step)
            act.dma_start(consts, const_dram).then_inc(N.const_loaded, 16)

            def met():
                act.wait_ge(N.const_loaded, 16)

            for g, r0, src in parameter_rows(A):
                act.dma_start(par_rows[r0:r0 + src.shape[0], g, :], src).then_inc(N.par_loaded, 16)
            act.wait_ge(N.small_set, 1)
            act.wait_ge(N.x_loaded, 48)
            for m, (_, rows) in enumerate(TOK):
                F(junk[0:rows], x_rows[0:rows, m], ACT.Square, accum_out=small[0:rows, m:m + 1]).then_inc(N.sumsq_done, 1)
                act.wait_ge(N.sumsq_done, m + 1)
            act.wait_ge(N.mem_loaded, 16)
            for m in range(2):
                F(junk, m_rows[:, m], ACT.Square, accum_out=small[:, 3 + m:4 + m]).then_inc(N.sumsq_done, 1)
                act.wait_ge(N.sumsq_done, m + 4)
            act.wait_ge(N.var_ready, 1)
            st.then(F(small[:, 16:21], small[:, 8:13], ACT.Ln))
            F(small[:, 24:29], small[:, 16:21], ACT.Exp, scale=-0.5).then_inc(N.seed_ready, 1)
            act.wait_ge(N.lb_max, 1)
            F(sqbuf[:, 0, 16:48], sqbuf[:, 0, 16:48], ACT.Exp).then_inc(N.lb_exp, 1)
            act.wait_ge(N.par_evac, 1)
            for f in range(KD):
                if f >= KD - 2:
                    act.wait_ge(N.row_T, 3 * f + 1)
                    F(xT[:, f], bank(f % 2)[:, 0:T], ACT.Copy).then_inc(N.bank_free, 1)
                act.wait_ge(N.row_T, 3 * f + 2)
                F(hT[:, f], bank(2 + f % 2)[:, 0:T], ACT.Copy, scale=G_PRE_MIX[:, f:f + 1]).then_inc(N.h_evac, 1)
                act.wait_ge(N.row_T, 3 * f + 3)
                F(mT[:, f], bank(4 + f % 2)[:, 0:MEM], ACT.Copy, scale=G_MEM[:, f:f + 1]).then_inc(N.m_evac, 1)

            def evacuate(s0, tiles, dst, n=T):
                with act.Fori(0, tiles // 2) as it:
                    for e in range(2):
                        act.wait_ge(N.slab_used, it * 2 + s0 + e + 1)
                        met()
                        F(dst[:, ds(it * 2 + e, 1), 0:n].rearrange("p o t -> p (o t)"), bank(e)[:, 0:n], ACT.Copy)\
                            .then_inc(N.bank_free, 1)

            evacuate(B_IQ, 8, iqT)
            act.wait_ge(N.ik_mm, 1)
            act.wait_ge(N.idx_zero, 1)
            F(ikd, bank(2)[:, 0:T], ACT.Copy).then_inc(N.ik_evac, 1)
            F(ikz[0:64, 0], bank(2)[0:64, 0:SEQ], ACT.Copy).then_inc(N.ik_evac, 1)
            F(ikz[64:P, 1], bank(2)[64:P, 0:SEQ], ACT.Copy).then_inc(N.ik_evac, 1)
            act.wait_ge(N.ik_mm, 2)
            F(iwT[0:H], bank(3)[0:H, 0:T], ACT.Copy, scale=(IDX ** -0.5) * (H ** -0.5)).then_inc(N.ik_evac, 1)
            evacuate(B_K, 4, kT)
            for j in range(R):
                act.wait_ge(N.slab_used, B_V + j + 1)
                F(vN[:, 0:2, j * P:(j + 1) * P], bank(j % 2)[:, 0:2 * P].rearrange("p (m c) -> p m c", m=2), ACT.Copy)
                F(vN[0:NS, 2, j * P:(j + 1) * P], bank(j % 2)[0:NS, 2 * P:3 * P], ACT.Copy).then_inc(N.bank_free, 1)
            act.wait_ge(N.ik_evac, 4)
            for i in range(4):
                act.wait_ge(N.page_T, i + 1)
                F(ik_all[:, 2 * i:2 * i + 2, 0:PAST], bank(2 + i).rearrange("p (b s) -> p b s", b=2), ACT.Copy)\
                    .then_inc(N.page_evac, 1)
            F(ik_all[:, :, PAST:L_S], ikd[:, SEQ:T].rearrange("p (b t) -> p b t", t=DT), ACT.Copy).then_inc(N.page_evac, 1)
            for b in range(DB):
                act.wait_ge(N.sidx_mm, b + 1)
                if b >= 2:
                    act.wait_ge(N.sidx_sum, b - 1)
                F(relu_s[:, b % 2], bank(6 + b % 2)[:, 0:L_S], ACT.Relu).then_inc(N.sidx_relu, 1)
            for m, (_, rows) in enumerate(TOK):
                act.wait_ge(N.out_T, m + 1)
                F(key_out[0:rows, m], bank(3 + m)[0:rows], ACT.Copy).then_inc(N.out_evac, 1)
            act.wait_ge(N.out_T, 4)
            F(ik_out[:, 0:2], bank(6)[:, 0:2 * IDX].rearrange("p (m c) -> p m c", m=2), ACT.Copy).then_inc(N.out_evac, 1)
            F(ik_out[0:NS, 2], bank(6)[0:NS, 2 * IDX:3 * IDX], ACT.Copy).then_inc(N.out_evac, 1)
            evacuate(B_QQ, 16, zq)
            for which, dst in ((0, new_mk), (1, new_mv)):
                with act.Fori(0, 4) as it:
                    act.wait_ge(N.memo_sent, it * 16 + 64 * which)
                    for j in range(R):
                        act.wait_ge(N.slab_used, it * R + B_MEM + 16 * which + j + 1)
                        F(mem_out[:, :, j * P:(j + 1) * P], bank(j % 2)[:, 0:2 * P].rearrange("p (m c) -> p m c", m=2), ACT.Copy)\
                            .then_inc(N.bank_free, 1)
                    act.wait_ge(N.bank_free, it * R + B_MEM + 16 * which + R + FREE)
                    act.dma_start(dst[:, :, ds(it * 512, 512)], mem_out).then_inc(N.memo_sent, 16)
            act.wait_ge(N.memo_sent, 128)

            def exps(it, g):
                act.wait_ge(N.s_max, it * QPK + g + 1)
                act.wait_ge(N.p_T, two_back(it, QPK, g))
                F(prob[:, g % 2, 0:P], logit[:, g % 2, 0:P], ACT.Exp, bias=smx[:, g, 0:1], accum_out=smx[:, g, 2:3])
                F(prob[:, g % 2, P:384], logit[:, g % 2, P:384], ACT.Exp, bias=smx[:, g, 1:2],
                  accum_out=smx[:, g, 3:4]).then_inc(N.s_exp, 1)

            def copies(it, g):
                act.wait_ge(N.p_T, it * QPK + g + 1)
                F(probT[:, g % 2], bank(4 + g % 2)[:, 0:384], ACT.Copy).then_inc(N.p_evac, 1)
                met()
                act.wait_ge(N.pv_mm, it * QPK + g + 1)
                F(zq[:, ds(it * QPK + g, 1), 0:SEQ].rearrange("p o t -> p (o t)"), bank(6 + g % 2)[:, 0:SEQ], ACT.Copy)\
                    .then_inc(N.o_evac, 1)

            act.wait_ge(N.selected, 3)
            with act.Fori(0, KVH) as it:
                act.wait_ge(N.s_mm, it * QPK)
                met()
                F(qs, zq[:, ds(it * QPK, QPK), 0:SEQ], ACT.Copy).then_inc(N.q_staged, 1)
                exps(it, 0)
                for g in range(1, QPK):
                    exps(it, g)
                    copies(it, g - 1)
                copies(it, QPK - 1)

            with act.Fori(0, DB // 2) as it:
                for e in range(2):
                    n1 = it * 2 + e + 1 + H
                    act.wait_ge(N.pv_mm, it * 2 + e + H)
                    new = ds(it * 16 + SEQ + e * DT, DT)
                    F(q_b[:, e], zq[:, :, new], ACT.Copy).then_inc(N.b_staged, 1)
                    met()
                    F(rep_b[0:NS, e], const("spread", NS)[:, ds(it * 256 + e * P, P)], ACT.Copy).then_inc(N.b_staged, 1)
                    for i in range(2):
                        act.wait_ge(N.kt_T, it * 4 + 2 * e + i + 1)
                        F(ktp[:, 2 * i:2 * i + 2, :], bank(2 + i).rearrange("p (h s) -> p h s", h=2), ACT.Copy)\
                            .then_inc(N.kt_evac, 1)
                    act.wait_ge(N.s_max, n1)
                    F(prob[:, e, 0:T], logit[:, e, 0:T], ACT.Exp, bias=smx[:, e, 0:1], accum_out=smx[:, e, 2:3])\
                        .then_inc(N.s_exp, 1)
                    act.wait_ge(N.p_T, n1)
                    F(probT[:, e, 0:PAST], bank(5)[:, 0:PAST], ACT.Copy)
                    F(probT[0:NS, e, PAST:384], bank(5)[0:NS, PAST:384], ACT.Copy).then_inc(N.p_evac, 1)
                    met()
                    act.wait_ge(N.pv_mm, n1)
                    F(zq[:, :, new], bank(6)[:, 0:P].rearrange("p (h t) -> p h t", t=DT), ACT.Copy).then_inc(N.o_evac, 1)

            def head(it, e):
                k1 = it * 2 + e + 1
                s0 = it * 12 + B_HG + 6 * e

                def b(g):
                    return bank((6 * e + g) % 2)

                act.wait_ge(N.slab_used, s0 + 1)
                F(f_e, b(0)[:, 0:T], ACT.Exp, scale=-1.0).then_inc(N.bank_free, 1)
                act.wait_ge(N.f_ready, k1)
                F(eb, f_e, ACT.Ln).then_inc(N.logf_ready, 1)
                act.wait_ge(N.slab_used, s0 + 2)
                F(hq, b(1)[:, 0:T], ACT.Copy).then_inc(N.bank_free, 1)
                act.wait_ge(N.d_ready, k1)
                st.did(F(lev[:, 0:LVS], lev[:, 0:LVS], ACT.Exp))
                st.did(F(lev[:, LVS:LV, 0:SEQ], lev[:, LVS:LV, 0:SEQ], ACT.Exp))
                st.did(F(ke, ke, ACT.Exp))
                F(eb, f_b, ACT.Exp).then_inc(N.e_ready, 1)
                act.wait_ge(N.slab_used, s0 + 3)
                st.did(F(vh[:, 0:2], b(2)[:, 0:2 * P].rearrange("p (m c) -> p m c", m=2), ACT.Copy))
                F(vh[0:NS, 2], b(2)[0:NS, 2 * P:3 * P], ACT.Copy).then_inc(N.bank_free, 1)
                act.wait_ge(N.slab_used, s0 + 4)
                act.wait_ge(N.head_done, it * 2 + e)
                st.did(F(hgr, b(3)[:, 0:T], ACT.Copy))
                F(gate[:, 2], b(3)[:, 0:T], ACT.Exp, scale=-1.0).then_inc(N.bank_free, 1)
                act.wait_ge(N.ke_T, k1)
                st.did(F(keN[:, 0:2], bank(7)[:, 0:2 * P].rearrange("p (m c) -> p m c", m=2), ACT.Copy))
                F(keN[0:NS, 2], bank(7)[0:NS, 2 * P:3 * P], ACT.Copy).then_inc(N.keN_ready, 1)
                act.wait_ge(N.slab_used, s0 + 5)
                F(gate[:, 0], b(4)[:, 0:T], ACT.Exp, scale=-1.0).then_inc(N.bank_free, 1)
                act.wait_ge(N.s1_mm, k1)
                F(s1, bank(4)[:, 0:P], ACT.Copy).then_inc(N.s1_ready, 1)
                act.wait_ge(N.o_mm, k1)
                F(osq, bank(6)[:, 0:T], ACT.Square).then_inc(N.osq_ready, 1)
                act.wait_ge(N.slab_used, s0 + 6)
                F(gate[:, 1], b(5)[:, 0:T], ACT.Exp, scale=-1.0).then_inc(N.bank_free, 1)
                act.wait_ge(N.v_ready, k1)
                st.then(F(o_r, osq, ACT.Ln))
                F(o_r, o_r, ACT.Exp, scale=-0.5).then_inc(N.r_seed, 1)

            with act.Fori(0, NHG // 2) as it:
                st.enter(it, 2 * 7)
                head(it, 0)
                head(it, 1)
            st.leave(NHG // 2)

            def seed(nv):
                act.wait_ge(N.n_var, nv)
                st.then(F(rstd, var, ACT.Ln))
                F(rstd, rstd, ACT.Exp, scale=-0.5).then_inc(N.n_seed, 1)

            def slab_high(j, ready, free=None):
                act.wait_ge(slab_ready[j], ready)
                if free is not None:
                    act.wait_ge(N.slab_used, free)
                F(w_hi[:, j % 2], ring[:, j], ACT.Copy).then_inc(N.slab_hi, 1)

            def first_high(n):
                slab_high(0, 16 * (n // R + 1), n - 1)

            def evacuate_split(s0, dst):
                def four(it, last):
                    for j in range(R):
                        if j < R - 1 or not last:
                            n = s0 + j + 1
                            slab_high(n % R, it * 16 + 16 * (n // R + 1), it * R + n - 1)
                        act.wait_ge(N.slab_used, it * R + s0 + j + 1)
                        met()
                        F(dst[:, ds(it * R + j, 1), 0:T].rearrange("p o t -> p (o t)"), bank(j % 2)[:, 0:T], ACT.Copy)\
                            .then_inc(N.bank_free, 1)

                with act.Fori(0, KD // R - 1) as it:
                    four(it, False)
                four(KD // R - 1, True)

            def input_high(src):
                for q in range(4):
                    F(x_hi[:, 4 * q:4 * q + 4], src[:, 4 * q:4 * q + 4], ACT.Copy).then_inc(N.in_hi, 1)

            def norm(i, nv, mmv, pre):
                seed(nv)
                if pre:
                    for f in range(KD):
                        act.wait_ge(N.n_x, i * KD + f + 1)
                        if f >= 2:
                            act.wait_ge(N.n_mm, mmv + f - 1)
                        F(sqbuf[:, f % 2], xT[:, f], ACT.Square).then_inc(N.n_sq, 1)
                    seed(nv + 1)
                    for f in range(KD):
                        act.wait_ge(N.n_h, i * KD + f + 1)
                        F(x_hi[:, f], hT[:, f], ACT.Copy).then_inc(N.in_hi, 1)

            act.wait_ge(N.head_done, NHG)
            act.wait_ge(N.state_sent, 32 * NHG)
            first_high(B_OUT)
            input_high(uT)
            evacuate_split(B_OUT, hT)
            first_high(B_XQ)
            act.wait_ge(N.n_sum, 1)
            norm(0, 1, 1, True)
            evacuate_split(B_XQ, qx)

            def evac_odd(it, e, n0):
                for c in range(1, 8, 2):
                    cc = n0 + c if it is None else it * 16 + 8 * e + c
                    act.wait_ge(N.kx_T, cc + 1)
                    F(kxT[:, 1].rearrange("p a b -> p (a b)"), bank(3), ACT.Copy).then_inc(N.kx_eact, 1)

            with act.Fori(0, DB // 2) as it:
                evac_odd(it, 0, 0)
                evac_odd(it, 1, 0)
            evac_odd(None, 0, 64)
            act.wait_ge(N.kx_used, 8)
            F(sxT.rearrange("p a b -> p (a b)"), bank(0), ACT.Copy).then_inc(N.sx_evac, 1)
            for qt in range(2):
                act.wait_ge(N.px_max, qt + 1)
                for x in range(XH):
                    F(pp[:, qt, x], bank(4 + 2 * qt + x // 2)[:, (x % 2) * MEM:(x % 2 + 1) * MEM], ACT.Exp,
                      bias=smx2[:, 2 + qt, x:x + 1], scale=X_S, accum_out=smx2[:, 4 + qt, x:x + 1]).then_inc(N.px_exp, 1)
            act.wait_ge(N.sx_max, 1)
            for rt in range(2):
                F(px[:, rt], bank(1)[:, rt * MEM:(rt + 1) * MEM], ACT.Exp, bias=smx2[:, 6, 2 + rt:3 + rt], scale=X_S,
                  accum_out=smx2[:, 7, rt:rt + 1]).then_inc(N.sx_exp, 1)
            for x in range(XH):
                act.wait_ge(N.px_T, x + 1)
                F(ppT[:, x % 2], bank(2 + x % 2), ACT.Copy).then_inc(N.px_evac, 1)
                for dt in range(XD):
                    n = x * XD + dt
                    act.wait_ge(N.vx_mm, n + 1)
                    F(qx[:, n, 0:SEQ], bank(4 + n % 2)[:, 0:SEQ], ACT.Copy).then_inc(N.vx_evac, 1)
            act.wait_ge(N.sx_pT, 1)
            F(pxT.rearrange("p a b -> p (a b)"), bank(6), ACT.Copy).then_inc(N.sx_pevac, 1)
            with act.Fori(0, DB // 2) as it:
                for e in range(2):
                    act.wait_ge(N.vx_mm, it * 2 + e + KD + 1)
                    met()
                    F(qx[:, :, ds(it * 16 + SEQ + e * DT, DT)], bank(2 + e)[:, 0:P].rearrange("p (n t) -> p n t", t=DT),
                      ACT.Copy).then_inc(N.vx_evac, 1)
            first_high(B_XO)
            act.wait_ge(N.vx_evac, KD + DB)
            input_high(qx)
            evacuate_split(B_XO, hT)
            first_high(B_UP)
            slab_high(1, 16 * (B_UP // R + 1), B_UP)
            norm(1, 3, 1 + KD + 1, True)

            def conv_input(it, e, more):
                s0 = it * 4 + B_UP + 2 * e
                act.wait_ge(N.slab_used, s0 + 1)
                act.wait_ge(N.y_done, two_back(it, 2, e))
                F(a_ext[:, e, 2:SEQ + 2], bank(0)[:, 0:SEQ], ACT.Copy)
                F(a_ext[:, e, SEQ + 2:].rearrange("p (b t) -> p b t", t=DT + 2)[:, :, 2:DT + 2],
                  bank(0)[:, SEQ:T].rearrange("p (b t) -> p b t", t=DT), ACT.Copy).then_inc(N.bank_free, 1)
                j = (2 * e + 2) % R
                ready = it * 16 + 16 * ((B_UP + 2 * e + 2) // R + 1)
                if more:
                    slab_high(j, ready)
                act.wait_ge(N.slab_used, s0 + 2)
                F(zb[:, e], bank(1)[:, 0:T], ACT.Copy).then_inc(N.bank_free, 1)
                if more:
                    slab_high(j + 1, ready)
                act.wait_ge(N.c_ready, it * 2 + e + 1)
                act.wait_ge(N.bank_free, s0 + 2 + FREE)
                F(gl[:, e], cv[:, e], ACT.Gelu_apprx_tanh).then_inc(N.g_ready, 1)

            with act.Fori(0, FT // 2 - 1) as it:
                conv_input(it, 0, True)
                conv_input(it, 1, True)
            conv_input(FT // 2 - 1, 0, True)
            conv_input(FT // 2 - 1, 1, False)
            with act.Fori(0, KD // 2) as it:
                for e in range(2):
                    act.wait_ge(N.slab_used, it * 8 + B_DOWN + 4 * e + 4)
                    met()
                    F(hT[:, ds(it * 2 + e, 1)].rearrange("p o t -> p (o t)"), bank(e)[:, 0:T], ACT.Copy)\
                        .then_inc(N.bank_free, 1)
            norm(2, 5, 0, False)
            for g in range(FT // 4):
                act.wait_ge(N.cn_T, g + 1)
                F(x_out[0:18, g * 512:(g + 1) * 512], bank(4 + g % 2)[0:18], ACT.Copy).then_inc(N.cn_evac, 1)
            for i in range(1, 12, 2):
                m, g = i // 4, i % 4
                rows = TOK[m][1]
                act.wait_ge(N.xo_T, i + 1)
                F(y_rows[0:rows, m, g * 512:(g + 1) * 512], bank(7)[0:rows], ACT.Copy).then_inc(N.xo_eact, 1)

        @block.gpsimd
        def _(pool):
            G = nc.gpsimd
            pool.dma_start(pages[0:1, :], A["page_table"].rearrange("(o b) g -> o (b g)", o=1)).then_inc(N.pages_loaded, 16)
            pool.wait_ge(N.pages_loaded, 16)
            pool.wait_ge(N.row_T, 3 * KD)
            for i in range(DB * NPG):
                pg = pool.value_load(pages[0:1, i:i + 1], min_val=0, max_val=POOL - 1)
                pool.dma_start(ik_page[:, i, :], A["cache_idx_k"][0][ds(pg, 1)].rearrange("o s d -> (o s) d"))\
                    .then_inc(N.ikpage_loaded, 16)
            G.memset(ikz, 0.0).then_inc(N.idx_zero, 1)
            G.memset(iq_s, 0.0).then_inc(N.idx_zero, 1)
            pool.wait_ge(N.ikpage_loaded, 16 * DB * NPG)
            pool.wait_ge(N.ik_mm, 2)
            G.tensor_copy(ik_dup, ik_page.rearrange("p n (o d) -> p n o d", o=1).broadcast_to([P, DB * NPG, 2, IDX]))\
                .then_inc(N.dup_ready, 1)
            pool.wait_ge(N.out_evac, 5)
            pool.wait_ge(N.bank_free, B_QQ + FREE)
            for dst, src in ((new_k, key_out[:, 0:2]), (new_ks, key_out[0:NS, 2]), (new_v, vN[:, 0:2]),
                             (new_vs, vN[0:NS, 2]), (new_ik, ik_out[:, 0:2]), (new_iks, ik_out[0:NS, 2])):
                pool.dma_start(dst, src).then_inc(N.out_sent, 16)

            pool.wait_ge(N.selected, 3)
            pool.dma_start(rel_sb[0:NB, :], A["rel_bias"]).then_inc(N.rel_loaded, 16)
            pool.wait_ge(N.bias_evac, 1)
            pool.dma_start(bias_dram, dist_sb[0:H, :].rearrange("h (o n) -> h o n", o=1).broadcast_to([H, P, NDIST])).then_inc(N.bias_stored, 16)
            pool.wait_ge(N.bias_stored, 16)

            def table(offset, ap):
                return bass.AP(tensor=bias_dram.tensor, offset=offset, ap=ap)

            pool.dma_start(toep, table(DIST0 - (SEQ - 1) + P - 1, [[NDIST - 1, P], [P * NDIST, H], [1, SEQ]]))\
                .then_inc(N.bias_loaded, 16)
            for h in range(H):
                rows = slice(h * DT, (h + 1) * DT)
                pool.dma_start(bias_s[rows, 0:PAST], table(h * P * NDIST + DT - 1, [[NDIST - 1, DT], [1, PAST]]))\
                    .then_inc(N.bias_loaded, 16)
                pool.dma_start(bias_s[rows, PAST:T].rearrange("p (b t) -> p b t", t=DT),
                               table(h * P * NDIST + DIST0, [[NDIST - 1, DT], [0, DB], [1, DT]])).then_inc(N.bias_loaded, 16)
            pool.wait_ge(N.bias_loaded, 16 * BIAS_DMAS)

            def page_loads(pool_it, e, first):
                for pg in range(NPG):
                    at = pool_it * 4 + (2 * e + pg) if not first else 2 * e + pg
                    src = pages[0:1, ds(at, 1)] if not first else pages[0:1, at:at + 1]
                    page = pool.value_load(src, min_val=0, max_val=POOL - 1)
                    for buf, cache in ((k_page, "cache_k"), (v_page, "cache_v")):
                        pool.dma_start(buf[:, e, pg, :], A[cache][0][ds(page, 1)].rearrange("o s h d -> (o s) (h d)"))\
                            .then_inc(kv_loaded[e], 16)

            pool.wait_ge(N.memo_sent, 128)
            for e in range(2):
                page_loads(0, e, True)
            with pool.Fori(0, KVH) as it:
                for g in range(QPK):
                    pool.wait_ge(N.s_read, two_back(it, QPK, g))
                    hrow = toep[:, ds(it * QPK + g, 1), :].rearrange("p o k -> p (o k)")
                    G.tensor_tensor(bm[:, g % 2, 0:P], hrow[:, P:SEQ], sel_p[:, 0, 0:P], ALU.add).then_inc(N.bm_ready, 1)
                    G.tensor_tensor(bm[:, g % 2, P:384], hrow, sel_p[:, 1, :], ALU.add).then_inc(N.bm_ready, 1)
            with pool.Fori(1, DB // 2) as it:
                for e in range(2):
                    pool.wait_ge(N.pv_mm, it * 2 + e + H - 1)
                    page_loads(it, e, False)

            with pool.Fori(0, NHG // 2) as it:
                for e in range(2):
                    k1 = it * 2 + e + 1
                    pool.wait_ge(N.head_done, it * 2 + e)
                    pool.wait_ge(N.o_evac, H + DB)
                    G.tensor_copy(pcol, head_par[:, ds(it * 2 + e, 1), :].rearrange("p o c -> p (o c)"))\
                        .then_inc(N.pcol_ready, 1)
                    pool.wait_ge(N.bank_free, it * 12 + B_HG + 6 * e + 3 + FREE)
                    G.tensor_tensor(v_m[0:NS], vh[0:NS, 2].rearrange("p (o v) -> p o v", o=1).broadcast_to([NS, DB, P]),
                                    const("seq_of", NS).rearrange("p (b o) -> p b o", o=1).broadcast_to([NS, DB, P]),
                                    ALU.mult).then_inc(N.vm_ready, 1)
                    pool.wait_ge(N.st_ready, k1)
                    pool.dma_start(hg_out_p[ds(it * 2 + e, 1)].rearrange("o c v -> (o c) v"), s2).then_inc(N.state_sent, 16)
                    pool.dma_start(hg_out_s[ds(it * 2 + e, 1)].rearrange("o c b v -> (o c) b v"), s_new)\
                        .then_inc(N.state_sent, 16)

            def input_low(src, lo, n0, parts):
                w = KD // parts
                for q in range(parts):
                    c = slice(q * w, (q + 1) * w)
                    pool.wait_ge(N.in_hi, n0 + q + 1)
                    G.tensor_tensor(lo[:, c], src[:, c], x_hi[:, c].bitcast(FP32), ALU.subtract).then_inc(N.in_lo, 1)

            def add_residual(i):
                for f in range(KD):
                    pool.wait_ge(N.n_t, i * KD + f + 1)
                    G.tensor_tensor(xT[:, f], xT[:, f], hT[:, f], ALU.add).then_inc(N.n_x, 1)

            input_low(uT, u_lo, 0, 4)
            add_residual(0)
            input_low(hT, h_lo, SPLIT_OUT, KD)
            input_low(qx, q_lo, SPLIT_XQ, 4)
            add_residual(1)
            input_low(hT, h_lo, SPLIT_XO, KD)
            pool.wait_ge(N.conv_evac, 1)
            with pool.Fori(0, FT // 2) as it:
                for e in range(2):
                    f = ds(it * 2 + e, 1)
                    pool.wait_ge(N.y_done, two_back(it, 2, e))
                    G.tensor_copy(pcf[:, e], conv_par[:, f, :].rearrange("p o c -> p (o c)")).then_inc(N.ctx_ready, 1)
                    G.tensor_copy(a_ext[:, e, SEQ + 2:].rearrange("p (b t) -> p b t", t=DT + 2)[:, :, 0:2],
                                  conv_old[:, f, :].rearrange("p o (b t) -> p (o b) t", t=2)).then_inc(N.ctx_ready, 1)
            add_residual(2)
            pool.wait_ge(N.out_sent, 96)
            pool.wait_ge(N.state_sent, 32 * NHG)
            pool.wait_ge(N.memo_sent, 128)


OUT_SHAPES = {
    "y_prompt": (1, SEQ, D), "y_sample": (DB, DT, D),
    "new_k_prompt": (1, 1, SEQ, KVH, P), "new_v_prompt": (1, 1, SEQ, KVH, P), "new_idx_k_prompt": (1, 1, SEQ, IDX),
    "new_k_sample": (1, DB, DT, KVH, P), "new_v_sample": (1, DB, DT, KVH, P), "new_idx_k_sample": (1, DB, DT, IDX),
    "new_mem_k_prompt": (1, 1, MEM, XH, 512), "new_mem_v_prompt": (1, 1, MEM, XH, 512),
    "new_hgrn_prompt": (1, 1, NHG, P, P), "new_hgrn_sample": (1, DB, NHG, P, P),
    "new_conv_prompt": (1, 1, 2, FF), "new_conv_sample": (1, DB, 2, FF),
}


def kernel(**inputs):
    import concourse.bacc as bacc
    from concourse.bass_utils import run_bass_kernel_spmd

    nc = bacc.Bacc("TRN2", target_bir_lowering=False, num_devices=1)
    arrays, A = {}, {}
    for name, a in list(inputs.items()) + [("shape_constants", shape_constants())]:
        a = np.ascontiguousarray(a)
        arrays["in_" + name] = a
        A[name] = nc.dram_tensor("in_" + name, a.shape, mybir.dt.from_np(a.dtype), kind="ExternalInput").ap()
    O = {n: nc.dram_tensor("out_" + n, s, FP32, kind="ExternalOutput").ap() for n, s in OUT_SHAPES.items()}
    hybrid_layer(nc, A, O, A["shape_constants"])
    r = run_bass_kernel_spmd(nc, [arrays], core_ids=[0])
    return tuple(r.results[0]["out_" + n] for n in OUT_SHAPES)
```

```python
import math
from contextlib import ExitStack

import numpy as np
import concourse.bass as bass
from concourse import mybir

FP32 = mybir.dt.float32
FP32R = mybir.dt.float32r
I32 = mybir.dt.int32
ALU = mybir.AluOpType
ACT = mybir.ActivationFunctionType
AX = mybir.AxisListType

P = 128
D = 2048
KD = D // P
SEQ = 256
DB, DT = 8, 8
NS = DB * DT
T = SEQ + NS
MEM = 256
PAGE = 128
NPG = 2
PAST = PAGE * NPG
POOL = 20
KVH, QPK, H = 4, 4, 16
IDX = 64
L_S = PAST + DT
TOPK_P, TOPK_S = 64, 66
PAD_S = -TOPK_S % 8
NB, NHG = 32, 16
XH, XD = 4, 4
FF = 5632
FT = FF // P
LV = 7
LVS = 3
R = 4
DOWN_K = FT // R
ARENA = 53184 - R * KD * P - KD * T
EPS = 1e-6
NEG = -1e30
O_Q, O_K, O_V, O_IQ, O_IW, O_IK = 0, 2048, 2560, 3072, 4096, 4112
O_HQ, O_HF, O_HI, O_HG, O_GA, O_GB = 4176, 6224, 8272, 10320, 12368, 14416
DIST0 = PAST + DT - 1
NDIST = 392

PAR_ROWS = (P, 120, 88)
PAR_DMAS = 14
BIAS_DMAS = 1 + 2 * H
HEAD_STEPS = 41


def parameter_rows(A):
    vec = [(0, 16 * i, A[n]) for i, n in enumerate(("g_pre_mix", "hg_norm", "g_post_mix", "g_pre_x", "g_mem",
                                                    "g_post_x", "g_pre_ffn", "g_post_ffn"))]
    vec += [(1, 0, A["hg_lb"][0:1]), (1, 16, A["hg_lb"][1:2]), (1, 32, A["conv_b"]), (1, 76, A["conv_w"][0, 0:1]),
            (2, 0, A["conv_w"][0, 1:2]), (2, 44, A["conv_w"][0, 2:3])]
    return [(g, r, v.rearrange("o (k p) -> (o k) p", p=P)) for g, r, v in vec]


CONST = {}
_at = 0
for _name, _cols in (("ident", 128), ("ones", 128), ("level", 8 * 128), ("level_s", 4 * 64), ("causal", 512),
                     ("causal_new", 8), ("other_seq", 64), ("dist", NDIST), ("heads_of", 128),
                     ("w_place", 512), ("spread", 1024), ("scan_keep", T), ("seq_of", 8)):
    CONST[_name] = (_at, _cols)
    _at += _cols
NCONST = _at


def shape_constants():
    c = np.zeros((P, NCONST), np.float32)

    def put(name, a):
        o, n = CONST[name]
        a = np.asarray(a, np.float32).reshape(a.shape[0], n)
        c[:a.shape[0], o:o + n] = a

    put("ident", np.eye(P))
    put("ones", np.ones((P, P)))
    s, t = np.meshgrid(np.arange(P), np.arange(P), indexing="ij")
    lev = np.zeros((P, 8, P))
    for l in range(LV):
        same = (s >> (l + 1)) == (t >> (l + 1))
        lev[:, l] = same & (((s >> l) & 1) == 0) & (((t >> l) & 1) == 1)
    lev[:, 7] = s == t
    put("level", lev)
    put("level_s", lev[:NS, [0, 1, 2, 7], :NS])
    q = np.arange(P)[:, None, None] + P * np.arange(2)[None, :, None]
    put("causal", np.where(np.arange(SEQ)[None, None, :] <= q, 0.0, NEG))
    row = np.arange(NS)
    put("causal_new", np.where(np.arange(DT)[None] <= (row % DT)[:, None], 0.0, NEG))
    put("other_seq", np.where((row // DT)[:, None] == (row // DT)[None], 0.0, NEG))
    dist = DIST0 - np.arange(NDIST)
    d = np.maximum(dist, 0)
    ratio = np.log(np.maximum(d, 1).astype(np.float32) / np.float32(16)) / np.float32(math.log(8))
    large = np.minimum(16 + (ratio * np.float32(16)).astype(np.int32), NB - 1)
    bucket = np.where(d < 16, d, large)
    put("dist", np.arange(NB)[:, None] == bucket[None])
    r = np.arange(P)
    put("heads_of", np.arange(H)[:, None] == (2 * ((r // 8) % 8) + r // 64)[None])
    seq, tok = np.arange(NS) // DT, np.arange(NS) % DT
    put("w_place", (np.arange(DB)[None, :, None] == seq[None, None]) & ((r % 8)[:, None, None] == tok[None, None]))
    put("spread", (seq[:, None, None] == np.arange(DB)[None, :, None]) & (tok[:, None, None] == (r % 8)[None, None]))
    keep = np.ones(T)
    keep[[0, P]] = 0
    keep[SEQ::DT] = 0
    put("scan_keep", np.broadcast_to(keep, (P, T)))
    put("seq_of", (row // DT)[:, None] == np.arange(DB)[None])
    return c


class Steps:

    def __init__(self, eng, sem):
        self.eng, self.sem, self.base, self.n = eng, sem, 0, 0

    def did(self, ins):
        ins.then_inc(self.sem, 1)
        self.n += 1

    def sync(self):
        self.eng.wait_ge(self.sem, self.base + self.n)

    def then(self, ins):
        self.did(ins)
        self.sync()

    def enter(self, it, per):
        self.start, self.per = self.base + self.n, per
        self.base, self.n = self.start + it * per, 0

    def leave(self, count):
        assert self.n == self.per, (self.n, self.per)
        self.base, self.n = self.start + count * self.per, 0


def hybrid_layer(nc, A, O, const_dram):
    ctx = ExitStack()
    with ctx:
        def sem(name):
            return ctx.enter_context(nc.semaphore(name))

        ds = bass.ds
        ring_at = -(-nc.sbuf_base // 64) * 64
        ring = ctx.enter_context(nc.sbuf_tensor("ring", [P, R, KD, P], FP32))[:]
        h_at = ring_at + 4 * R * KD * P
        hT = ctx.enter_context(nc.sbuf_tensor("h", [P, KD, T], FP32))[:]
        arena_at = h_at + 4 * KD * T
        arena = ctx.enter_context(nc.sbuf_tensor("arena", [P, ARENA], FP32))
        pages = ctx.enter_context(nc.sbuf_tensor("pages", [1, DB * NPG], I32))
        psum = ctx.enter_context(nc.psum_tensor("psum", [P, 8 * 512], FP32))
        bias_dram = nc.dram_tensor("bias_by_distance", (H, P, NDIST), FP32, kind="Internal").ap()

        top = [0]

        def take(*shape):
            n = int(np.prod(shape))
            a = arena[:, top[0]:top[0] + n]
            top[0] += n
            assert top[0] <= ARENA
            if len(shape) == 2:
                a = a.rearrange("p (a b) -> p a b", a=shape[0])
            elif len(shape) == 3:
                a = a.rearrange("p (a b c) -> p a b c", a=shape[0], b=shape[1])
            return a

        def alias(name, offset, *shape):
            return nc.alloc_sbuf_tensor_at(name, [P] + list(shape), FP32R, offset=offset)[:]

        h_lo = alias("h_low", h_at, KD, T)
        w_lo = alias("w_low", ring_at, R, KD, P)
        SPLIT_AT = ARENA - KD * T - 2 * KD * P
        x_hi = alias("x_high", arena_at + 4 * SPLIT_AT, KD, T)
        w_hi = alias("w_high", arena_at + 4 * (SPLIT_AT + KD * T), 2, KD, P)

        def bank(i, n=1):
            return psum[:, 512 * i:512 * (i + n)]

        consts = take(NCONST)

        def const(name, rows=P):
            o, n = CONST[name]
            return consts[0:rows, o:o + n]

        ident, ones = const("ident"), const("ones")
        level = const("level").rearrange("p (l t) -> p l t", l=8)
        level_s = const("level_s", NS).rearrange("p (l t) -> p l t", l=4)
        causal = const("causal").rearrange("p (a k) -> p a k", a=2)

        par = take(3, P)
        head_par = take(NHG, 3)
        conv_par = take(FT, 4)
        xT = take(KD, T)
        small = take(64)
        mf = arena[:, top[0]:top[0] + 2 * MEM].rearrange("p (a b) -> p a b", a=2)
        sqacc = take(T)
        rstd = take(T)
        var = take(T)
        ntmp = take(T)
        sqbuf = take(2, T)
        BASE = top[0]
        G_PRE_MIX, G_HG, G_POST_MIX, G_PRE_X, G_MEM, G_POST_X, G_PRE_FFN, G_POST_FFN = \
            [par[:, 0, 16 * i:16 * i + 16] for i in range(8)]

        zq_lo = alias("zq_low", arena_at + 4 * top[0], KD, T)
        zq = take(KD, T)
        MIX = top[0]
        kT = take(KVH, T)
        vN = take(3, 512)
        sel_p = take(2, SEQ)
        sel_s = take(T)
        key_out = take(3, 512)
        ik_out = take(3, IDX)
        m_lo = alias("m_low", arena_at + 4 * top[0], KD, MEM)
        mT = take(KD, MEM)
        mem_out = key_out[:, 0:2]
        C0 = top[0]
        top[0] = C0
        iqT = take(8, T)
        w_ik = take(KD, 144)
        ikz = take(2, SEQ)
        ikd = take(T)
        iwT = take(T)
        iwN = take(2, H)
        iq_s = take(DB, P)
        ik_page = key_out.rearrange("p a b -> p (a b)")[:, 0:DB * NPG * IDX].rearrange("p (n d) -> p n d", n=DB * NPG)
        ik_dup = w_ik.rearrange("p a b -> p (a b)")[:, 0:DB * NPG * 2 * IDX]\
            .rearrange("p (n o d) -> p n o d", n=DB * NPG, o=2)
        ik_all = take(DB, L_S)
        w_sel = take(DB, NS)
        score = take(2, SEQ)
        score_t = take(4, SEQ)
        relu_s = take(2, L_S)
        work = take(PAD_S + L_S)
        best = take(8)
        top[0] = C0
        x_rows = take(3, D)
        TA = top[0]
        top[0] = C0 - 1024 - 4096
        top[0] = C0
        toep = take(H, SEQ)
        bias_s = take(T)
        rel_sb = take(H)
        dist_sb = take(NDIST)
        M_HI = SPLIT_AT + KD * (T - MEM)
        m_hi = alias("m_high", arena_at + 4 * M_HI, KD, MEM)
        assert top[0] <= M_HI
        qs = take(QPK, SEQ)
        vs = take(2, P)
        bm = take(2, 384)
        prob = take(2, 384)
        probT = take(2, 384)
        smx = take(8, 4)
        ktp = take(KVH, PAST)
        q_b = take(2, H, DT)
        rep_b = take(2, P)
        logit = take(2, 384)
        top[0] = C0 - 4096
        k_page = take(2, NPG, 512)
        v_page = take(2, NPG, 512)
        top[0] = TA
        m_rows = take(2, D)
        junk = hT.rearrange("p a b -> p (a b)")[:, 0:D]
        diag = take(5, P)
        par_rows = zq.rearrange("p a b -> p (a b)")[:, 0:384].rearrange("p (g c) -> p g c", g=3)

        top[0] = MIX
        f_k = take(T)
        f_b = take(T)
        hq = take(T)
        vh = take(3, P)
        lev = take(LV, T)
        levq = take(LV, T)
        a_m = take(8, P)
        a_T = take(3, P)
        eb = take(T)
        qb = take(T)
        ke = take(T)
        keN = take(3, P)
        s1 = take(P)
        s2 = take(P)
        v_m = take(DB, P)
        s_new = take(DB, P)
        gate = take(3, T)
        hgr = take(T)
        osq = take(T)
        o_n = take(T)
        o_r = take(T)
        vf = o_n
        pcol = take(3)
        assert top[0] <= SPLIT_AT
        top[0] = CONST["causal"][0]
        s_old = take(2, DB, P)
        f_e = take(T)
        assert top[0] <= CONST["scan_keep"][0]

        top[0] = BASE
        qx = take(KD, T)
        top[0] = MIX + KD * T
        kx = take(2, 2, D)
        assert top[0] <= SPLIT_AT
        top[0] = CONST["level"][0]
        kxT = take(2, XD, P)
        top[0] = MIX
        sxT = take(2, 4 * MEM // 4)
        px = take(2, MEM)
        pxT = take(2, MEM)
        pp = take(2, XH, MEM)
        ppT = take(2, 2 * SEQ)
        smx2 = take(8, 4)
        assert top[0] <= MIX + KD * T

        top[0] = BASE
        yT = take(FT, T)
        top[0] = BASE + 3 * D
        conv_rows = take(FF)
        assert top[0] <= BASE + FT * T
        top[0] = CONST["level"][0]
        conv_old = take(FT, 16)
        wd_hi = alias("w_down_high", arena_at + 4 * top[0], 2, DOWN_K, P)
        assert top[0] + 2 * DOWN_K * P <= NCONST
        top[0] = BASE + FT * T
        conv_new = take(FT, 18)
        part = DOWN_K * T
        y_hi = [None] + [alias(f"y_high{j}", arena_at + 4 * (top[0] + (j - 1) * part), DOWN_K, T) for j in range(1, R)]
        y_lo = [None] + [alias(f"y_low{j}", arena_at + 4 * (BASE + j * part), DOWN_K, T) for j in range(1, R)]
        assert top[0] + (R - 1) * part <= ARENA
        a_ext = take(2, SEQ + 2 + DB * (DT + 2))
        cv = take(2, T)
        cvt = take(2, T)
        zb = take(2, T)
        gl = take(2, T)
        pcf = take(2, 4)
        x_out = conv_rows
        assert top[0] <= SPLIT_AT
        top[0] = BASE
        y_rows = take(3, D)

        S = {n: sem(n) for n in """
            x_loaded mem_loaded const_loaded par_loaded pages_loaded wik_loaded ikpage_loaded rel_loaded
            slab_used bank_free act_step dve_step pool_step small_set
            sumsq_done var_ready seed_ready diag_ready par_T par_evac lb_max lb_exp
            row_T x_evac h_evac m_evac
            ik_mm ik_evac idx_zero iw_T iw_evac idx_mm idx_free page_T page_evac dup_ready iqs_ready
            sidx_mm sidx_relu sidx_sum selected out_T out_evac out_sent memo_sent
            bias_mm bias_evac bias_stored bias_loaded
            q_staged v_staged bm_ready s_mm s_read s_max s_exp s_prob p_T p_evac pv_mm o_evac
            kv_loaded0 kv_loaded1 kt_T kt_evac b_staged
            f_ready logf_ready d_ready e_ready qk_ready a_mm aT_ready ke_T keN_ready s1_mm s1_ready st_mm
            vm_ready o_mm osq_ready ss_mm v_ready r_seed st_ready state_sent head_done pcol_ready
            sold_loaded0 sold_loaded1
            n_sum n_mm n_var n_seed n_t n_x n_sq n_h slab_hi slab_lo in_hi in_lo h_low v_T v_evac m_high m_low mem_T mem_copied y_high y_low
            kx_loaded0 kx_loaded1 kx_T kx_edve kx_eact kx_used sx_evac sx_T sx_max sx_exp sx_prob sx_pT sx_pevac
            px_max px_exp px_prob px_T px_evac vx_mm vx_evac
            conv_loaded conv_T conv_evac ctx_ready c_ready g_ready y_done cn_T cn_evac xo_T xo_edve xo_eact final_sent
            """.split()}
        N = type("Semaphores", (), S)
        slab_ready = [sem(f"slab{j}_ready") for j in range(R)]
        kv_loaded = [N.kv_loaded0, N.kv_loaded1]
        sold_loaded = [N.sold_loaded0, N.sold_loaded1]
        kx_loaded = [N.kx_loaded0, N.kx_loaded1]

        w_in = A["w_in"][0].rearrange("(k p) n -> p k n", p=P)
        B_IQ, B_K, B_V, B_QQ, B_MEM = 0, 8, 12, 16, 32
        B_HG = 64
        B_OUT = B_HG + 6 * NHG
        B_XQ, B_XO = B_OUT + KD, B_OUT + 2 * KD
        B_UP = B_XO + KD
        B_DOWN = B_UP + 2 * FT
        B_END = B_DOWN + R * KD
        IN_HG, IN_OUT = 0, 4
        IN_XQ = IN_OUT + 4
        IN_XO = IN_XQ + KD
        IN_UP = IN_XO + 4
        FREE = 2
        ATT_S = float(P) ** -0.5
        X_S = float(512) ** -0.5
        TOK = [(0, P), (P, P), (SEQ, NS)]
        x_rows_of = [A["x_prompt"][0, 0:P], A["x_prompt"][0, P:SEQ], A["x_sample"].rearrange("b t d -> (b t) d")]
        mem_rows_of = A["mem_prompt"][0].rearrange("(m p) d -> p m d", p=P)
        new_k = O["new_k_prompt"][0, 0].rearrange("(m p) h d -> p m (h d)", p=P)
        new_v = O["new_v_prompt"][0, 0].rearrange("(m p) h d -> p m (h d)", p=P)
        new_ik = O["new_idx_k_prompt"][0, 0].rearrange("(m p) d -> p m d", p=P)
        new_ks = O["new_k_sample"][0].rearrange("b t h d -> (b t) (h d)")
        new_vs = O["new_v_sample"][0].rearrange("b t h d -> (b t) (h d)")
        new_iks = O["new_idx_k_sample"][0].rearrange("b t d -> (b t) d")
        new_mk = O["new_mem_k_prompt"][0, 0].rearrange("(m p) h d -> p m (h d)", p=P)
        new_mv = O["new_mem_v_prompt"][0, 0].rearrange("(m p) h d -> p m (h d)", p=P)
        mem_k = A["cache_mem_k"][0].rearrange("b (m p) h d -> b p m (h d)", p=P)
        mem_v = A["cache_mem_v"][0].rearrange("b (m p) h d -> b p m (h d)", p=P)
        hg_in = A["state_hgrn"][0].rearrange("b h c v -> h c b v")
        hg_out_s = O["new_hgrn_sample"][0].rearrange("b h c v -> h c b v")
        hg_out_p = O["new_hgrn_prompt"][0, 0]
        iq_cols = iq_s.rearrange("p b (j t) -> p b j t", t=DT)

        def two_back(it, per, g):
            return it * per + max(g - 1, 0)

        block = ctx.enter_context(nc.Block())

        @block.sync
        def _(sp):
            for m, (_, rows) in enumerate(TOK):
                sp.dma_start(x_rows[0:rows, m, :], x_rows_of[m]).then_inc(N.x_loaded, 16)
            sp.dma_start(m_rows, mem_rows_of).then_inc(N.mem_loaded, 16)

            def slab(s, j, src):
                sp.wait_ge(N.slab_used, s - (R - 1))
                sp.dma_start(ring[:, j], src).then_inc(slab_ready[j], 16)

            def stretch(s0, tiles, w, col):
                with sp.Fori(0, tiles // R) as it:
                    for j in range(R):
                        slab(it * R + s0 + j, j, w[:, :, ds(it * (R * P) + col + j * P, P)])

            for j in range(R):
                sp.dma_start(ring[:, j], w_in[:, :, O_IQ + j * P:O_IQ + (j + 1) * P]).then_inc(slab_ready[j], 16)
            sp.wait_ge(N.row_T, 3 * KD)
            sp.dma_start(w_ik[:, :, 0:80], w_in[:, :, O_IW:O_IW + 80]).then_inc(N.wik_loaded, 16)
            sp.dma_start(w_ik[:, :, 80:144], w_in[:, :, O_IK:O_IK + 64]).then_inc(N.wik_loaded, 16)
            stretch(B_IQ + R, 4, w_in, O_IQ + R * P)
            stretch(B_K, 8, w_in, O_K)
            stretch(B_QQ, 16, w_in, O_Q)
            for w, s0 in ((A["w_xk"], B_MEM), (A["w_xv"], B_MEM + 16)):
                stretch(s0, 16, w[0].rearrange("(k p) n -> p k n", p=P), 0)
            with sp.Fori(0, NHG // 2) as it:
                for e in range(2):
                    for g, col in enumerate((O_HF, O_HQ, O_HI, O_HG, O_GA, O_GB)):
                        n = 6 * e + g
                        slab(it * 12 + B_HG + n, n % R, w_in[:, :, ds(it * (2 * P) + col + e * P, P)])
                        if g == 4:
                            sp.wait_ge(N.head_done, two_back(it, 2, e))
                            sp.dma_start(s_old[:, e], hg_in[ds(it * 2 + e, 1)].rearrange("o c b v -> (o c) b v"))\
                              .then_inc(sold_loaded[e], 16)
            stretch(B_OUT, 16, A["w_out"][0].rearrange("(k p) n -> p k n", p=P), 0)
            sp.wait_ge(N.head_done, NHG)
            sp.wait_ge(N.state_sent, 32 * NHG)
            for n in range(2):
                sp.dma_start(kx[:, n], mem_k[n]).then_inc(kx_loaded[n], 16)
            stretch(B_XQ, 16, A["w_xq"][0].rearrange("(k p) n -> p k n", p=P), 0)
            with sp.Fori(0, 3) as it:
                for e in range(2):
                    sp.wait_ge(N.kx_used, it * 2 + e + 1)
                    sp.dma_start(kx[:, e], mem_k[ds(it * 2 + 2 + e, 1)].rearrange("o p m d -> (o p) m d"))\
                      .then_inc(kx_loaded[e], 16)
            sp.wait_ge(N.kx_used, 7)
            sp.wait_ge(N.memo_sent, 16 * 8)
            sp.dma_start(kx[:, 0], new_mk).then_inc(kx_loaded[0], 16)
            sp.wait_ge(N.kx_used, 8)
            sp.dma_start(kx[:, 1], new_mv).then_inc(kx_loaded[1], 16)
            sp.wait_ge(N.kx_used, 9)
            sp.dma_start(kx[:, 0], mem_v[0]).then_inc(kx_loaded[0], 16)
            sp.wait_ge(N.vx_mm, KD)
            sp.dma_start(kx[:, 1], mem_v[1]).then_inc(kx_loaded[1], 16)
            with sp.Fori(0, 3) as it:
                for e in range(2):
                    sp.wait_ge(N.vx_mm, it * 2 + e + KD + 1)
                    sp.dma_start(kx[:, e], mem_v[ds(it * 2 + e + 2, 1)].rearrange("o p m d -> (o p) m d"))\
                      .then_inc(kx_loaded[e], 16)
            stretch(B_XO, 16, A["w_xo"][0].rearrange("(k p) n -> p k n", p=P), 0)
            sp.wait_ge(N.vx_evac, KD + DB)
            sp.dma_start(conv_rows[0:16, :], A["state_conv"][0].rearrange("b j f -> (b j) f"))\
              .then_inc(N.conv_loaded, 16)
            w_up = A["w_up"][0].rearrange("(k p) n -> p k n", p=P)
            with sp.Fori(0, FT // 2) as it:
                for j in range(R):
                    slab(it * R + B_UP + j, j, w_up[:, :, ds(it * (2 * P) + (j % 2) * FF + (j // 2) * P, P)])
            w_down = A["w_down"][0].rearrange("(k p) n -> p k n", p=P)
            with sp.Fori(0, KD) as it:
                for j in range(R):
                    sp.wait_ge(N.slab_used, it * R + B_DOWN + j - (R - 1))
                    sp.dma_start(ring[:, j, 0:DOWN_K], w_down[:, j * DOWN_K:(j + 1) * DOWN_K, ds(it * P, P)])\
                      .then_inc(slab_ready[j], 16)
            sp.wait_ge(N.xo_edve, 6)
            sp.wait_ge(N.xo_eact, 6)
            sp.dma_start(O["y_prompt"][0].rearrange("(m p) d -> p m d", p=P), y_rows[:, 0:2]).then_inc(N.final_sent, 16)
            sp.dma_start(O["y_sample"].rearrange("b t d -> (b t) d"), y_rows[0:NS, 2]).then_inc(N.final_sent, 16)
            sp.wait_ge(N.cn_evac, 11)
            sp.dma_start(O["new_conv_prompt"][0, 0], x_out[0:2, :]).then_inc(N.final_sent, 16)
            sp.dma_start(O["new_conv_sample"][0].rearrange("b j f -> (b j) f"), x_out[2:18, :])\
              .then_inc(N.final_sent, 16)
            sp.wait_ge(N.final_sent, 64)

        @block.tensor
        def _(pe):
            mm, tr = nc.tensor.matmul, nc.tensor.transpose

            def project(s0, tiles, rhs, n=T):
                with pe.Fori(0, tiles // R) as it:
                    for j in range(R):
                        pe.wait_ge(slab_ready[j], it * 16 + 16 * (s0 // R + 1))
                        pe.wait_ge(N.bank_free, it * R + s0 + j + FREE - 1)
                        for k in range(KD):
                            last = mm(bank(j % 2)[:, 0:n], ring[:, j, k, :], rhs[:, k, :], start=k == 0, stop=k == KD - 1)
                        last.then_inc(N.slab_used, 1)

            def three_products(j, n, lo, split, count):
                out = bank(j % 2)[:, 0:T]
                pe.wait_ge(N.slab_hi, n)
                for k in range(KD):
                    mm(out, w_hi[:, j % 2, k, :], x_hi[:, k, :], start=k == 0, stop=False)
                pe.wait_ge(N.slab_lo, n)
                for k in range(KD):
                    mm(out, w_lo[:, j, k, :], x_hi[:, k, :], start=False, stop=False)
                pe.wait_ge(split, count)
                for k in range(KD):
                    last = mm(out, w_hi[:, j % 2, k, :], lo[:, k, :], start=False, stop=k == KD - 1)
                return last

            def project_split(s0, tiles, lo, split, count):
                with pe.Fori(0, tiles // R) as it:
                    for j in range(R):
                        pe.wait_ge(N.bank_free, it * R + s0 + j + FREE - 1)
                        three_products(j, it * R + s0 - B_MEM + j + 1, lo, split, count).then_inc(N.slab_used, 1)

            def project_rows(s_ready, j, free, xx, tiles):
                pe.wait_ge(slab_ready[j], s_ready)
                pe.wait_ge(N.bank_free, free)
                for m, (t0, rows) in enumerate(tiles):
                    for k in range(KD):
                        last = mm(bank(j % 2)[0:rows, m * P:(m + 1) * P], xx[:, k, t0:t0 + rows], ring[:, j, k, :],
                                  start=k == 0, stop=k == KD - 1)
                last.then_inc(N.slab_used, 1)

            pe.wait_ge(N.const_loaded, 16)
            pe.wait_ge(N.par_loaded, PAR_DMAS * 16)
            for g, rows in enumerate(PAR_ROWS):
                last = tr(bank(6)[:, g * P:g * P + rows], par_rows[0:rows, g, :], ident[0:rows, 0:rows])
            last.then_inc(N.par_T, 1)
            pe.wait_ge(N.x_loaded, 48)
            pe.wait_ge(N.mem_loaded, 16)
            pe.wait_ge(N.diag_ready, 1)
            for f in range(KD):
                fc = slice(f * P, (f + 1) * P)
                if f >= 2:
                    pe.wait_ge(N.x_evac, f - 1)
                for m, (t0, rows) in enumerate(TOK):
                    last = tr(bank(f % 2)[:, t0:t0 + rows], x_rows[0:rows, m, fc], ident[0:rows, 0:rows])
                last.then_inc(N.row_T, 1)
                if f >= 2:
                    pe.wait_ge(N.h_evac, f - 1)
                for m, (t0, rows) in enumerate(TOK):
                    last = mm(bank(2 + f % 2)[:, t0:t0 + rows], x_rows[0:rows, m, fc], diag[0:rows, m, 0:rows],
                              start=True, stop=True)
                last.then_inc(N.row_T, 1)
                if f >= 2:
                    pe.wait_ge(N.m_evac, f - 1)
                for m in range(2):
                    last = mm(bank(4 + f % 2)[:, m * P:(m + 1) * P], m_rows[:, m, fc], diag[:, 3 + m, :],
                              start=True, stop=True)
                last.then_inc(N.row_T, 1)
            pe.wait_ge(N.h_evac, KD)

            project(B_IQ, 8, hT)
            pe.wait_ge(N.wik_loaded, 32)
            pe.wait_ge(N.m_evac, KD)
            for b, (c0, c1) in ((2, (16, 144)), (3, (0, 16))):
                for k in range(KD):
                    last = mm(bank(b)[0:c1 - c0, 0:T], w_ik[:, k, c0:c1], hT[:, k, :], start=k == 0, stop=k == KD - 1)
                last.then_inc(N.ik_mm, 1)
            project(B_K, 4, hT)
            for j in range(R):
                project_rows(16 * (B_V // R + 1), j, B_V + j + FREE - 1, hT, TOK)

            pe.wait_ge(N.ik_evac, 4)
            for m in range(2):
                tr(bank(4)[:, m * H:(m + 1) * H], iwT[0:H, m * P:(m + 1) * P], ident[0:H, 0:H])
            mm(bank(4)[:, 64:64 + NS], const("heads_of", H), iwT[0:H, SEQ:T], start=True, stop=True).then_inc(N.iw_T, 1)
            pe.wait_ge(N.iw_evac, 2)
            pe.wait_ge(N.idx_zero, 2)
            for n in range(16):
                qt, j = n // 8, n % 8
                if n >= 6:
                    pe.wait_ge(N.idx_free, n - 5)
                kk = P * (qt + 1)
                mm(bank(2 + n % 6)[:, 0:2 * kk], iqT[:, j, qt * P:(qt + 1) * P], ikz[:, :, 0:kk],
                   start=True, stop=True).then_inc(N.idx_mm, 1)
            pe.wait_ge(N.idx_free, 16)
            pe.wait_ge(N.dup_ready, 1)
            for i in range(4):
                for q in range(4):
                    last = tr(bank(2 + i)[:, q * P:(q + 1) * P], ik_dup[:, 4 * i + q].rearrange("p a d -> p (a d)"), ident)
                last.then_inc(N.page_T, 1)
            pe.wait_ge(N.page_evac, 5)
            pe.wait_ge(N.iqs_ready, 2)

            def sample_scores(b):
                if b >= 2:
                    pe.wait_ge(N.sidx_relu, b - 1)
                mm(bank(6 + b % 2)[:, 0:L_S], iq_s[:, b], ik_all[:, b], start=True, stop=True).then_inc(N.sidx_mm, 1)

            def sample_sum(b):
                pe.wait_ge(N.sidx_relu, b + 1)
                mm(bank(2)[0:NS, 0:L_S], w_sel[:, b], relu_s[:, b % 2], start=b == 0, stop=b == DB - 1)\
                    .then_inc(N.sidx_sum, 1)

            sample_scores(0)
            for b in range(1, DB):
                sample_scores(b)
                sample_sum(b - 1)
            sample_sum(DB - 1)
            for m, (t0, rows) in enumerate(TOK):
                for h in range(KVH):
                    last = tr(bank(3 + m)[0:rows, h * P:(h + 1) * P], kT[:, h, t0:t0 + rows], ident)
                last.then_inc(N.out_T, 1)
            for m, (t0, rows) in enumerate(TOK):
                last = tr(bank(6)[0:rows, m * IDX:(m + 1) * IDX], ikd[0:IDX, t0:t0 + rows], ident[0:IDX, 0:IDX])
            last.then_inc(N.out_T, 1)

            project(B_QQ, 16, hT)
            pe.wait_ge(N.rel_loaded, 16)
            mm(bank(7)[0:H, 0:NDIST], rel_sb[0:NB, :], const("dist", NB), start=True, stop=True).then_inc(N.bias_mm, 1)

            def memory_tile(it, i):
                n, j, out = it * R + i, i % R, bank(i % 2)[:, 0:MEM]
                pe.wait_ge(N.bank_free, it * R + i + B_MEM + FREE - 1)
                pe.wait_ge(N.slab_hi, n + 1)
                for k in range(KD):
                    mm(out, w_hi[:, j % 2, k, :], m_hi[:, k, :], start=k == 0, stop=False)
                pe.wait_ge(N.slab_lo, n + 1)
                for k in range(KD):
                    mm(out, w_lo[:, j, k, :], m_hi[:, k, :], start=False, stop=False)
                for k in range(KD):
                    last = mm(out, w_hi[:, j % 2, k, :], m_lo[:, k, :], start=False, stop=k == KD - 1)
                last.then_inc(N.slab_used, 1)

            def memory_T(it, i):
                pe.wait_ge(N.bank_free, it * R + i + B_MEM + FREE + 1)
                pe.wait_ge(N.mem_copied, it * R + max(i - 1, 0))
                for m in range(2):
                    last = tr(bank(2 + i % 2)[:, m * P:(m + 1) * P], mf[:, i % 2, m * P:(m + 1) * P], ident)
                last.then_inc(N.mem_T, 1)

            pe.wait_ge(N.m_low, 4)
            memory_tile(0, 0)
            with pe.Fori(0, 7) as it:
                for i in range(R):
                    memory_tile(it, i + 1)
                    memory_T(it, i)
            for i in range(R):
                if i < R - 1:
                    memory_tile(7, i + 1)
                memory_T(7, i)

            def scores(it, g):
                pe.wait_ge(N.s_read, two_back(it, QPK, g))
                b = bank(2 + g % 2)
                mm(b[:, 0:P], qs[:, g, 0:P], kT[:, ds(it, 1), 0:P].rearrange("p o k -> p (o k)"), start=True, stop=True)
                mm(b[:, P:3 * P], qs[:, g, P:SEQ], kT[:, ds(it, 1), 0:SEQ].rearrange("p o k -> p (o k)"),
                   start=True, stop=True).then_inc(N.s_mm, 1)

            def weigh(it, g):
                pe.wait_ge(N.s_prob, it * QPK + g + 1)
                pe.wait_ge(N.p_evac, two_back(it, QPK, g))
                b = bank(4 + g % 2)
                for i, (src) in enumerate((0, P, 2 * P)):
                    last = tr(b[:, i * P:(i + 1) * P], prob[:, g % 2, src:src + P], ident)
                last.then_inc(N.p_T, 1)
                pe.wait_ge(N.p_evac, it * QPK + g + 1)
                pe.wait_ge(N.o_evac, two_back(it, QPK, g))
                o = bank(6 + g % 2)
                mm(o[:, 0:SEQ], vs[:, 0], probT[:, g % 2, 0:SEQ], start=True, stop=False)
                mm(o[:, P:SEQ], vs[:, 1], probT[:, g % 2, SEQ:384], start=False, stop=True).then_inc(N.pv_mm, 1)

            pe.wait_ge(N.bias_evac, 1)
            with pe.Fori(0, KVH) as it:
                pe.wait_ge(N.q_staged, it + 1)
                pe.wait_ge(N.v_staged, it + 1)
                scores(it, 0)
                for g in range(1, QPK):
                    scores(it, g)
                    weigh(it, g - 1)
                weigh(it, QPK - 1)

            with pe.Fori(0, DB // 2) as it:
                for e in range(2):
                    n1 = it * 2 + e + 1
                    pe.wait_ge(kv_loaded[e], it * 64 + 64)
                    pe.wait_ge(N.kt_evac, it * 4 + 2 * e)
                    pe.wait_ge(N.s_read, it * 2 + e + H)
                    for i in range(2):
                        for hh in range(2):
                            for pg in range(NPG):
                                h = 2 * i + hh
                                last = tr(bank(2 + i)[:, (2 * hh + pg) * P:(2 * hh + pg + 1) * P],
                                          k_page[:, e, pg, h * P:(h + 1) * P], ident)
                        last.then_inc(N.kt_T, 1)
                    pe.wait_ge(N.b_staged, it * 4 + 2 * e + 2)
                    pe.wait_ge(N.kt_evac, it * 4 + 2 * e + 2)
                    s = bank(4)
                    mm(s[:, 0:T], rep_b[0:NS, e], sel_s[0:NS, :], start=True, stop=False, skip_group_check=True)
                    for h in range(KVH):
                        q4 = q_b[:, e, 4 * h:4 * h + 4, :].rearrange("p g t -> p (g t)")
                        mm(s[32 * h:32 * h + 32, 0:PAST], q4, ktp[:, h, :], start=False, stop=False,
                           skip_group_check=True)
                        last = mm(s[32 * h:32 * h + 32, PAST:T], q4, kT[:, h, SEQ:T], start=False, stop=True,
                                  skip_group_check=True)
                    last.then_inc(N.s_mm, 1)
                    pe.wait_ge(N.s_prob, n1 + H)
                    pe.wait_ge(N.p_evac, it * 2 + e + H)
                    for i in range(2):
                        tr(bank(5)[:, i * P:(i + 1) * P], prob[:, e, i * P:(i + 1) * P], ident)
                    tr(bank(5)[0:NS, 2 * P:3 * P], prob[:, e, PAST:T], ident).then_inc(N.p_T, 1)
                    pe.wait_ge(N.p_evac, n1 + H)
                    pe.wait_ge(N.o_evac, it * 2 + e + H)
                    for h in range(KVH):
                        oc = slice(32 * h, 32 * h + 32)
                        for pg in range(NPG):
                            mm(bank(6)[:, oc], v_page[:, e, pg, h * P:(h + 1) * P],
                               probT[:, e, pg * P + 32 * h:pg * P + 32 * h + 32], start=pg == 0, stop=False)
                        last = mm(bank(6)[:, oc], vN[0:NS, 2, h * P:(h + 1) * P],
                                  probT[0:NS, e, 2 * P + 32 * h:2 * P + 32 * h + 32], start=False, stop=True)
                    last.then_inc(N.pv_mm, 1)
            pe.wait_ge(N.o_evac, H + DB)

            def head(it, e):
                k1 = it * 2 + e + 1

                def tile(g):
                    n = 6 * e + g
                    pe.wait_ge(N.bank_free, it * 12 + B_HG + n + FREE - 1)
                    return n % R, it * 12 + B_HG - B_MEM + n + 1

                def project_one(g):
                    three_products(*tile(g), h_lo, N.in_lo, 4).then_inc(N.slab_used, 1)

                project_one(0)
                project_one(1)
                project_one(2)
                project_one(3)
                pe.wait_ge(N.head_done, it * 2 + e)
                pe.wait_ge(N.bank_free, it * 12 + B_HG + 6 * e + 3 + FREE)
                for m, (t0, rows) in enumerate(TOK):
                    last = tr(bank(7)[0:rows, m * P:(m + 1) * P], vf[:, t0:t0 + rows], ident)
                last.then_inc(N.v_T, 1)
                project_one(4)
                pe.wait_ge(N.qk_ready, k1)
                for b in range(2):
                    c = slice(b * P, (b + 1) * P)
                    for l in range(LV + 1):
                        kk, qq = (lev[:, l, c], levq[:, l, c]) if l < LV else (f_k[:, c], hq[:, c])
                        last = mm(bank(2 + 2 * b + l // 4)[:, (l % 4) * P:(l % 4 + 1) * P], kk, qq, start=True, stop=True)
                    last.then_inc(N.a_mm, 1)
                for l in range(LVS + 1):
                    kk, qq = (lev[:, l, SEQ:T], levq[:, l, SEQ:T]) if l < LVS else (f_k[:, SEQ:T], hq[:, SEQ:T])
                    last = mm(bank(6)[0:NS, l * NS:(l + 1) * NS], kk, qq, start=True, stop=True)
                last.then_inc(N.a_mm, 1)
                pe.wait_ge(N.v_evac, k1)
                for m, (t0, rows) in enumerate(TOK):
                    last = tr(bank(7)[0:rows, m * P:(m + 1) * P], ke[:, t0:t0 + rows], ident)
                last.then_inc(N.ke_T, 1)
                project_one(5)
                pe.wait_ge(N.keN_ready, k1)
                pe.wait_ge(N.aT_ready, k1)
                mm(bank(4)[:, 0:P], keN[:, 0], vh[:, 0], start=True, stop=True).then_inc(N.s1_mm, 1)
                mm(bank(5)[:, 0:P], keN[:, 1], vh[:, 1], start=True, stop=True)
                pe.wait_ge(N.vm_ready, k1)
                for i in range(2):
                    last = mm(bank(2 + i)[:, 0:512], keN[0:NS, 2], v_m[0:NS, 4 * i:4 * i + 4, :], start=True, stop=True)
                last.then_inc(N.st_mm, 1)
                o = bank(6)
                mm(o[:, 0:P], vh[:, 0], a_T[:, 0], start=True, stop=True)
                mm(o[:, P:SEQ], vh[:, 1], a_T[:, 1], start=True, stop=False)
                pe.wait_ge(N.s1_ready, k1)
                mm(o[:, P:SEQ], s1, qb[:, P:SEQ], start=False, stop=True)
                mm(o[:, SEQ:T], vh[0:NS, 2], a_T[0:NS, 2, 0:NS], start=True, stop=False, skip_group_check=True)
                pe.wait_ge(sold_loaded[e], it * 16 + 16)
                for b in range(DB):
                    c = slice(SEQ + b * DT, SEQ + (b + 1) * DT)
                    last = mm(o[:, c], s_old[:, e, b], qb[:, c], start=False, stop=b == DB - 1, skip_group_check=True)
                last.then_inc(N.o_mm, 1)
                pe.wait_ge(N.osq_ready, k1)
                mm(bank(7)[:, 0:T], ones, osq, start=True, stop=True).then_inc(N.ss_mm, 1)

            pe.wait_ge(N.in_hi, IN_OUT)
            with pe.Fori(0, NHG // 2) as it:
                head(it, 0)
                head(it, 1)

            def norm_sums(i, pre):
                pe.wait_ge(N.n_sum, i + 1)
                mm(bank(2)[:, 0:T], ones, sqacc, start=True, stop=True).then_inc(N.n_mm, 1)
                if pre:
                    for f in range(KD):
                        pe.wait_ge(N.n_sq, i * KD + f + 1)
                        last = mm(bank(3)[:, 0:T], ones, sqbuf[:, f % 2], start=f == 0, stop=f == KD - 1)
                        last.then_inc(N.n_mm, 1)

            pe.wait_ge(N.head_done, NHG)
            pe.wait_ge(N.in_hi, IN_XQ)
            project_split(B_OUT, 16, zq_lo, N.in_lo, 8)
            norm_sums(0, True)
            pe.wait_ge(N.in_hi, IN_XO)
            project_split(B_XQ, 16, h_lo, N.h_low, KD)
            pe.wait_ge(N.bank_free, B_XQ + KD + FREE)

            def chunk_T(c, e):
                for dt in range(XD):
                    last = tr(bank(2 + c % 2)[:, dt * P:(dt + 1) * P],
                              kx[:, e, c % 2, (c // 2) * 512 + dt * P:(c // 2) * 512 + (dt + 1) * P], ident)
                last.then_inc(N.kx_T, 1)

            def chunk_evac_wait(half, c):
                pe.wait_ge(N.kx_eact if c % 2 else N.kx_edve, half + c // 2 + 1)

            def sample_chunk(it, e, c):
                chunk_evac_wait((it * 2 + e) * 4, c)
                x, mt = c // 2, c % 2
                for dt in range(XD):
                    last = mm(bank(0)[:, ds(it * 64 + mt * 256 + e * 32 + x * 8, 8)], kxT[:, mt, dt],
                              qx[:, 4 * x + dt, ds(it * 16 + SEQ + e * DT, DT)], start=dt == 0, stop=dt == XD - 1)
                if c == 7:
                    last.then_inc(N.kx_used, 1)

            with pe.Fori(0, DB // 2) as it:
                for e in range(2):
                    pe.wait_ge(kx_loaded[e], it * 16 + 16)
                    chunk_T(0, e)
                    for c in range(1, 8):
                        chunk_T(c, e)
                        sample_chunk(it, e, c - 1)
                    sample_chunk(it, e, 7)

            def prompt_chunk(c):
                chunk_evac_wait(32, c)
                x, mt = c // 2, c % 2
                for qt in range(2):
                    for dt in range(XD):
                        last = mm(bank(4 + 2 * qt + x // 2)[:, (x % 2) * 256 + mt * P:(x % 2) * 256 + (mt + 1) * P],
                                  qx[:, 4 * x + dt, qt * P:(qt + 1) * P], kxT[:, mt, dt], start=dt == 0, stop=dt == XD - 1)
                if c == 7:
                    last.then_inc(N.kx_used, 1)

            pe.wait_ge(kx_loaded[0], 5 * 16)
            chunk_T(0, 0)
            for c in range(1, 8):
                chunk_T(c, 0)
                prompt_chunk(c - 1)
            prompt_chunk(7)
            pe.wait_ge(N.sx_evac, 1)
            for rt in range(2):
                for mt in range(2):
                    last = tr(bank(1)[:, rt * 256 + mt * P:rt * 256 + (mt + 1) * P],
                              sxT[:, mt, rt * P:(rt + 1) * P], ident)
            last.then_inc(N.sx_T, 1)
            pe.wait_ge(kx_loaded[1], 5 * 16)
            for x in range(XH):
                pe.wait_ge(N.px_prob, 2)
                if x >= 2:
                    pe.wait_ge(N.px_evac, x - 1)
                for mt in range(2):
                    for qt in range(2):
                        last = tr(bank(2 + x % 2)[:, mt * 256 + qt * P:mt * 256 + (qt + 1) * P],
                                  pp[:, qt, x, mt * P:(mt + 1) * P], ident)
                last.then_inc(N.px_T, 1)
                pe.wait_ge(N.px_evac, x + 1)
                for dt in range(XD):
                    n = x * XD + dt
                    if n >= 2:
                        pe.wait_ge(N.vx_evac, n - 1)
                    for mt in range(2):
                        last = mm(bank(4 + n % 2)[:, 0:SEQ], kx[:, 1, mt, n * P:(n + 1) * P],
                                  ppT[:, x % 2, mt * 256:(mt + 1) * 256], start=mt == 0, stop=mt == 1)
                    last.then_inc(N.vx_mm, 1)
            pe.wait_ge(N.sx_prob, 2)
            for mt in range(2):
                for rt in range(2):
                    last = tr(bank(6)[:, mt * 256 + rt * P:mt * 256 + (rt + 1) * P], px[:, rt, mt * P:(mt + 1) * P], ident)
            last.then_inc(N.sx_pT, 1)
            pe.wait_ge(N.sx_pevac, 1)
            with pe.Fori(0, DB // 2) as it:
                for e in range(2):
                    pe.wait_ge(kx_loaded[e], it * 16 + 6 * 16)
                    pe.wait_ge(N.vx_evac, it * 2 + max(e - 1, 0) + 16)
                    for n in range(KD):
                        for mt in range(2):
                            last = mm(bank(2 + e)[:, n * DT:(n + 1) * DT], kx[:, e, mt, n * P:(n + 1) * P],
                                      pxT[:, mt, ds(it * 64 + e * 32 + (n // 4) * 8, DT)], start=mt == 0, stop=mt == 1)
                    last.then_inc(N.vx_mm, 1)
            pe.wait_ge(N.vx_evac, 16 + DB)
            pe.wait_ge(N.in_hi, IN_UP)
            project_split(B_XO, 16, zq_lo, N.in_lo, 12)
            norm_sums(1, True)
            pe.wait_ge(N.conv_loaded, 16)
            for f in range(FT):
                last = tr(bank(4 + f // 32)[:, (f % 32) * 16:(f % 32) * 16 + 16], conv_rows[0:16, f * P:(f + 1) * P],
                          ident[0:16, 0:16])
            last.then_inc(N.conv_T, 1)
            pe.wait_ge(N.in_hi, IN_UP + KD)
            project_split(B_UP, 2 * FT, h_lo, N.h_low, 2 * KD)
            pe.wait_ge(N.y_done, FT)
            with pe.Fori(0, KD // 2) as it:
                for e in range(2):
                    pe.wait_ge(N.bank_free, it * 2 + B_DOWN + e + FREE - 1)
                    pe.wait_ge(slab_ready[0], it * 32 + 16 * (B_DOWN // R + e + 1))
                    for k in range(DOWN_K):
                        last = mm(bank(e)[:, 0:T], ring[:, 0, k, :], yT[:, k, :], start=k == 0, stop=False)
                    last.then_inc(N.slab_used, 1)
                    for j in range(1, R):
                        pe.wait_ge(N.y_low, j)
                        pe.wait_ge(N.slab_lo, it * 6 + B_DOWN - B_MEM + 3 * e + j)
                        for k in range(DOWN_K):
                            wh = wd_hi[:, (3 * e + j) % 2, k, :]
                            mm(bank(e)[:, 0:T], wh, y_hi[j][:, k, :], start=False, stop=False)
                            mm(bank(e)[:, 0:T], wh, y_lo[j][:, k, :], start=False, stop=False)
                            last = mm(bank(e)[:, 0:T], w_lo[:, j, k, :], y_hi[j][:, k, :], start=False,
                                      stop=j == R - 1 and k == DOWN_K - 1)
                        last.then_inc(N.slab_used, 1)
            norm_sums(2, False)
            for f in range(FT):
                g, c = f // 4, f % 4
                if c == 0 and g >= 2:
                    pe.wait_ge(N.cn_evac, g - 1)
                last = tr(bank(4 + g % 2)[0:18, c * P:(c + 1) * P], conv_new[:, f, :], ident)
                if c == 3:
                    last.then_inc(N.cn_T, 1)
            pe.wait_ge(N.n_x, 3 * KD)
            i = 0
            for m, (t0, rows) in enumerate(TOK):
                for g in range(4):
                    if i >= 2:
                        pe.wait_ge(N.xo_eact if i % 2 else N.xo_edve, (i - 2) // 2 + 1)
                    for c in range(4):
                        last = tr(bank(6 + i % 2)[0:rows, c * P:(c + 1) * P], xT[:, 4 * g + c, t0:t0 + rows], ident)
                    last.then_inc(N.xo_T, 1)
                    i += 1

        @block.vector
        def _(dve):
            V = nc.vector
            st = Steps(dve, N.dve_step)

            def refine(r, v, tmp):
                st.then(V.tensor_tensor(tmp, r, r, ALU.mult))
                st.then(V.tensor_tensor(tmp, tmp, v, ALU.mult))
                st.then(V.tensor_scalar(tmp, tmp, -0.5, 1.5, ALU.mult, ALU.add))
                return V.tensor_tensor(r, r, tmp, ALU.mult)

            V.memset(small, 1.0).then_inc(N.small_set, 1)
            dve.wait_ge(N.sumsq_done, 5)
            V.tensor_scalar(small[:, 8:13], small[:, 0:5], 1.0 / D, EPS, ALU.mult, ALU.add).then_inc(N.var_ready, 1)
            dve.wait_ge(N.var_ready, 1)
            dve.wait_ge(N.par_T, 1)
            for g, rows in enumerate(PAR_ROWS):
                last = V.tensor_copy(par[:, g, 0:rows], bank(6)[:, g * P:g * P + rows])
            last.then_inc(N.par_evac, 1)
            dve.wait_ge(N.seed_ready, 1)
            st.then(refine(small[:, 24:29], small[:, 8:13], small[:, 32:37]))
            dve.wait_ge(N.const_loaded, 16)
            for i in range(5):
                last = V.tensor_scalar(diag[:, i], ident, small[:, 24 + i:25 + i], None, ALU.mult)
            last.then_inc(N.diag_ready, 1)
            dve.wait_ge(N.par_evac, 1)
            l0, l1 = par[:, 1, 0:16], par[:, 1, 16:32]
            t0_, t1_, t2_, t3_ = [sqbuf[:, 0, 16 * i:16 * i + 16] for i in range(4)]
            st.then(V.tensor_tensor(t0_, l0, l1, ALU.max))
            st.then(V.tensor_tensor(t1_, l0, t0_, ALU.subtract))
            V.tensor_tensor(t2_, l1, t0_, ALU.subtract).then_inc(N.lb_max, 1)
            dve.wait_ge(N.lb_exp, 1)
            st.then(V.tensor_tensor(t0_, t1_, t2_, ALU.add))
            st.then(V.reciprocal(t3_, t0_))
            st.then(V.tensor_tensor(t1_, t1_, t3_, ALU.mult))
            st.then(V.tensor_tensor(t2_, t2_, t3_, ALU.mult))
            st.then(V.tensor_tensor(t2_, t1_, t2_, ALU.add))
            st.then(V.tensor_tensor(head_par[:, :, 0], t2_, t1_, ALU.subtract))
            st.did(V.tensor_scalar(head_par[:, :, 1], head_par[:, :, 0], -1.0, 1.0, ALU.mult, ALU.add))
            st.did(V.tensor_copy(head_par[:, :, 2], G_HG))
            for i, src in enumerate((par[:, 1, 76:120], par[:, 2, 0:44], par[:, 2, 44:88], par[:, 1, 32:76])):
                st.did(V.tensor_copy(conv_par[:, :, i], src))
            st.sync()
            for f in range(KD - 2):
                dve.wait_ge(N.row_T, 3 * f + 1)
                V.tensor_copy(xT[:, f], bank(f % 2)[:, 0:T]).then_inc(N.x_evac, 1)

            dve.wait_ge(N.idx_zero, 2)
            dve.wait_ge(N.bank_free, 8 + FREE)
            for par_, off in ((0, 0), (1, 64)):
                rows = slice(off, off + 64)
                V.tensor_copy(iq_s[rows, :, off:off + 64].rearrange("p b (j t) -> p b j t", t=DT),
                              iqT[rows, :, SEQ:T].rearrange("p j (b t) -> p b j t", t=DT)).then_inc(N.iqs_ready, 1)
            dve.wait_ge(N.iw_T, 1)
            V.tensor_copy(iwN.rearrange("p a h -> p (a h)"), bank(4)[:, 0:2 * H]).then_inc(N.iw_evac, 1)
            V.tensor_tensor(w_sel, bank(4)[:, 64:64 + NS].rearrange("p (o c) -> p o c", o=1).broadcast_to([P, DB, NS]),
                            const("w_place").rearrange("p (b c) -> p b c", b=DB), ALU.mult).then_inc(N.iw_evac, 1)
            dve.wait_ge(N.iw_evac, 2)
            for n in range(16):
                qt, j = n // 8, n % 8
                kk = P * (qt + 1)
                dve.wait_ge(N.idx_mm, n + 1)
                for hp in range(2):
                    dst = score[:, qt, 0:kk] if j == 0 and hp == 0 else score_t[:, (2 * n + hp) % 4, 0:kk]
                    ins = V.tensor_scalar(dst, bank(2 + n % 6)[:, hp * kk:(hp + 1) * kk], 0.0,
                                          iwN[:, qt, 2 * j + hp:2 * j + hp + 1], ALU.max, ALU.mult)
                    if hp == 0:
                        st.did(ins)
                ins.then_inc(N.idx_free, 1)
                st.sync()
                if j:
                    st.then(V.tensor_tensor(score[:, qt, 0:kk], score[:, qt, 0:kk], score_t[:, (2 * n) % 4, 0:kk], ALU.add))
                dve.wait_ge(N.idx_free, n + 1)
                st.then(V.tensor_tensor(score[:, qt, 0:kk], score[:, qt, 0:kk], score_t[:, (2 * n + 1) % 4, 0:kk], ALU.add))

            def top(w, rounds, rows):
                for _ in range(rounds):
                    st.then(V.max(best[0:rows], w))
                    st.then(V.match_replace(w, best[0:rows], w, -3e38))

            for qt in range(2):
                kk = P * (qt + 1)
                w = work[:, 0:kk]
                st.then(V.scalar_tensor_tensor(w, causal[:, qt, 0:kk], 1e8, score[:, qt, 0:kk], ALU.mult, ALU.add))
                top(w, TOPK_P // 8, P)
                st.then(V.tensor_scalar(w, w, -2e38, NEG, ALU.is_gt, ALU.mult))
                V.tensor_tensor(sel_p[:, qt, 0:kk], w, causal[:, qt, 0:kk], ALU.add).then_inc(N.selected, 1)
                dve.wait_ge(N.selected, qt + 1)
            dve.wait_ge(N.sidx_sum, DB)
            st.did(V.memset(work[0:NS, 0:PAD_S], 3e38))
            st.did(V.tensor_copy(work[0:NS, PAD_S:PAD_S + PAST], bank(2)[0:NS, 0:PAST]))
            st.then(V.scalar_tensor_tensor(work[0:NS, PAD_S + PAST:PAD_S + L_S], const("causal_new", NS), 1e8,
                                           bank(2)[0:NS, PAST:L_S], ALU.mult, ALU.add))
            top(work[0:NS, 0:PAD_S + L_S], (TOPK_S + PAD_S) // 8, NS)
            w = work[0:NS, PAD_S:PAD_S + L_S]
            st.then(V.tensor_scalar(w, w, -2e38, NEG, ALU.is_gt, ALU.mult))
            st.did(V.tensor_copy(sel_s[0:NS, 0:PAST], w[:, 0:PAST]))
            new = w[:, PAST:L_S]
            st.then(V.tensor_tensor(new, new, const("causal_new", NS), ALU.add))
            V.tensor_tensor(sel_s[0:NS, PAST:T].rearrange("p (b t) -> p b t", t=DT),
                            new.rearrange("p (o t) -> p o t", o=1).broadcast_to([NS, DB, DT]),
                            const("other_seq", NS).rearrange("p (b t) -> p b t", t=DT), ALU.add).then_inc(N.selected, 1)
            dve.wait_ge(N.selected, 3)

            def slab_low(n, j):
                dve.wait_ge(N.slab_hi, n - B_MEM + 1)
                V.tensor_tensor(w_lo[:, j], ring[:, j], w_hi[:, j % 2].bitcast(FP32), ALU.subtract).then_inc(N.slab_lo, 1)

            for q in range(4):
                c = slice(4 * q, 4 * q + 4)
                dve.wait_ge(N.m_high, q + 1)
                V.tensor_tensor(m_lo[:, c], mT[:, c], m_hi[:, c].bitcast(FP32), ALU.subtract).then_inc(N.m_low, 1)
            dve.wait_ge(N.bias_mm, 1)
            V.tensor_copy(dist_sb[0:H, :], bank(7)[0:H, 0:NDIST]).then_inc(N.bias_evac, 1)
            with dve.Fori(0, 8) as it:
                for j in range(R):
                    slab_low(it * R + B_MEM + j, j)
            dve.wait_ge(N.slab_used, B_HG)

            dve.wait_ge(N.bias_loaded, 16 * BIAS_DMAS)

            def logits(it, g):
                dve.wait_ge(N.s_mm, it * QPK + g + 1)
                dve.wait_ge(N.bm_ready, it * 8 + 2 * g + 2)
                V.scalar_tensor_tensor(logit[:, g % 2], bank(2 + g % 2)[:, 0:384], ATT_S, bm[:, g % 2], ALU.mult, ALU.add)\
                    .then_inc(N.s_read, 1)
                dve.wait_ge(N.s_read, it * QPK + g + 1)
                st.did(V.tensor_reduce(smx[:, g, 0:1], logit[:, g % 2, 0:P], AX.X, ALU.max, negate=True))
                V.tensor_reduce(smx[:, g, 1:2], logit[:, g % 2, P:384], AX.X, ALU.max, negate=True).then_inc(N.s_max, 1)

            def normalise(it, g):
                dve.wait_ge(N.s_exp, it * QPK + g + 1)
                st.then(V.reciprocal(smx[:, 4 + g, 2:4], smx[:, g, 2:4]))
                st.did(V.tensor_scalar(prob[:, g % 2, 0:P], prob[:, g % 2, 0:P], smx[:, 4 + g, 2:3], None, ALU.mult))
                V.tensor_scalar(prob[:, g % 2, P:384], prob[:, g % 2, P:384], smx[:, 4 + g, 3:4], None, ALU.mult)\
                    .then_inc(N.s_prob, 1)

            with dve.Fori(0, KVH) as it:
                st.enter(it, 3 * QPK)
                dve.wait_ge(N.pv_mm, it * QPK)
                V.tensor_copy(vs, vN[:, 0:2, ds(it * P, P)]).then_inc(N.v_staged, 1)
                logits(it, 0)
                for g in range(1, QPK):
                    logits(it, g)
                    normalise(it, g - 1)
                normalise(it, QPK - 1)
            st.leave(KVH)

            with dve.Fori(0, DB // 2) as it:
                st.enter(it, 2)
                for e in range(2):
                    n1 = it * 2 + e + 1 + H
                    dve.wait_ge(N.s_mm, n1)
                    V.scalar_tensor_tensor(logit[:, e, 0:T], bank(4)[:, 0:T], ATT_S, bias_s, ALU.mult, ALU.add)\
                        .then_inc(N.s_read, 1)
                    dve.wait_ge(N.s_read, n1)
                    V.tensor_reduce(smx[:, e, 0:1], logit[:, e, 0:T], AX.X, ALU.max, negate=True).then_inc(N.s_max, 1)
                    dve.wait_ge(N.s_exp, n1)
                    st.then(V.reciprocal(smx[:, 4 + e, 2:3], smx[:, e, 2:3]))
                    V.tensor_scalar(prob[:, e, 0:T], prob[:, e, 0:T], smx[:, 4 + e, 2:3], None, ALU.mult)\
                        .then_inc(N.s_prob, 1)
            st.leave(DB // 2)
            dve.wait_ge(N.o_evac, H + DB)

            def input_low(src, lo, q0, n0):
                for q in range(4):
                    c = slice(4 * q, 4 * q + 4)
                    dve.wait_ge(N.in_hi, n0 + q + 1)
                    V.tensor_tensor(lo[:, c], src[:, c], x_hi[:, c].bitcast(FP32), ALU.subtract).then_inc(N.in_lo, 1)

            for j in range(2):
                slab_low(B_HG + j, j)
            input_low(hT, h_lo, 0, IN_HG)

            def bcast(a, n):
                return a.rearrange("p (o t) -> p o t", o=1).broadcast_to([P, n, a.shape[1]])

            def head(it, e, last_head=False):
                k1 = it * 2 + e + 1
                s0 = it * 12 + B_HG + 6 * e + FREE

                def low(g):
                    n = 6 * e + g + 2
                    slab_low(it * 12 + B_HG + n, n % R)

                dve.wait_ge(N.bank_free, s0 + 1)
                dve.wait_ge(N.pcol_ready, k1)
                st.then(V.tensor_scalar(f_e, f_e, 1.0, None, ALU.add))
                st.then(V.reciprocal(f_k, f_e))
                V.tensor_scalar(f_e, f_k, pcol[:, 1:2], pcol[:, 0:1], ALU.mult, ALU.add).then_inc(N.f_ready, 1)
                dve.wait_ge(N.f_ready, k1)
                st.did(V.tensor_scalar(f_k, f_e, -1.0, 1.0, ALU.mult, ALU.add))
                low(1)
                dve.wait_ge(N.logf_ready, k1)
                st.then(V.tensor_tensor_scan(f_b, const("scan_keep"), eb, 0.0, ALU.mult, ALU.add))
                for l in range(LV):
                    w, half = (T if l < LVS else SEQ), 2 ** l
                    segs = w // (2 * half)
                    b4 = f_b[:, 0:w].rearrange("p (s u h) -> p s u h", u=2, h=half)
                    d4 = lev[:, l, 0:w].rearrange("p (s u h) -> p s u h", u=2, h=half)
                    mid = b4[:, :, 0, half - 1:half].broadcast_to([P, segs, half])
                    st.did(V.tensor_tensor(d4[:, :, 0, :], mid, b4[:, :, 0, :], ALU.subtract))
                    st.did(V.tensor_tensor(d4[:, :, 1, :], b4[:, :, 1, :], mid, ALU.subtract))
                for c0, c1, w in ((0, SEQ, P), (SEQ, T, DT)):
                    b3 = f_b[:, c0:c1].rearrange("p (s t) -> p s t", t=w)
                    last = V.tensor_tensor(ke[:, c0:c1].rearrange("p (s t) -> p s t", t=w),
                                           b3[:, :, w - 1:w].broadcast_to([P, (c1 - c0) // w, w]), b3, ALU.subtract)
                    if c0 == 0:
                        st.did(last)
                last.then_inc(N.d_ready, 1)
                low(2)
                dve.wait_ge(N.e_ready, k1)
                dve.wait_ge(N.bank_free, s0 + 2)
                st.did(V.tensor_tensor(levq[:, 0:LVS], lev[:, 0:LVS], bcast(hq, LVS), ALU.mult))
                st.did(V.tensor_tensor(levq[:, LVS:LV, 0:SEQ], lev[:, LVS:LV, 0:SEQ], bcast(hq[:, 0:SEQ], LV - LVS), ALU.mult))
                st.did(V.tensor_tensor(lev[:, 0:LVS], lev[:, 0:LVS], bcast(f_k, LVS), ALU.mult))
                st.did(V.tensor_tensor(lev[:, LVS:LV, 0:SEQ], lev[:, LVS:LV, 0:SEQ], bcast(f_k[:, 0:SEQ], LV - LVS), ALU.mult))
                st.did(V.tensor_tensor(ke, ke, f_k, ALU.mult))
                V.tensor_tensor(qb[:, P:T], eb[:, P:T], hq[:, P:T], ALU.mult).then_inc(N.qk_ready, 1)
                low(3)
                for b in range(3):
                    rows, nl, w = (P, LV + 1, P) if b < 2 else (NS, LVS + 1, NS)
                    src = (bank(2 + 2 * b, 2) if b < 2 else bank(6)[0:NS, 0:nl * NS]).rearrange("p (l t) -> p l t", l=nl)
                    am = a_m.rearrange("p l t -> p (l t)")[0:rows, 0:nl * w].rearrange("p (l t) -> p l t", l=nl)
                    dve.wait_ge(N.a_mm, it * 6 + 3 * e + b + 1)
                    st.then(V.tensor_tensor(am, src, level if b < 2 else level_s, ALU.mult))
                    last = V.tensor_reduce(a_T[0:rows, b, 0:w], am.rearrange("p l t -> p t l"), AX.X, ALU.add)
                    if b < 2:
                        st.then(last)
                last.then_inc(N.aT_ready, 1)
                low(4)
                dve.wait_ge(N.bank_free, s0 + 6)
                st.then(V.tensor_scalar(gate[:, 0:2], gate[:, 0:2], 1.0, None, ALU.add))
                st.then(V.scalar_tensor_tensor(gate[:, 1], gate[:, 2], 1.0, gate[:, 1], ALU.add, ALU.mult))
                st.then(V.reciprocal(gate[:, 0:2], gate[:, 0:2]))
                dve.wait_ge(N.st_mm, k1)
                dve.wait_ge(N.s1_ready, k1)
                dve.wait_ge(N.state_sent, it * 64 + 32 * e)
                dve.wait_ge(sold_loaded[e], it * 16 + 16)
                st.did(V.scalar_tensor_tensor(s2, s1, eb[:, SEQ - 1:SEQ], bank(5)[:, 0:P], ALU.mult, ALU.add))
                for b in range(DB):
                    at = SEQ + (b + 1) * DT
                    last = V.scalar_tensor_tensor(s_new[:, b], s_old[:, e, b], eb[:, at - 1:at],
                                                  bank(2 + b // 4)[:, (b % 4) * P:(b % 4 + 1) * P], ALU.mult, ALU.add)
                last.then_inc(N.st_ready, 1)
                low(5)
                dve.wait_ge(N.ss_mm, k1)
                V.tensor_scalar(osq, bank(7)[:, 0:T], 1.0 / P, EPS, ALU.mult, ALU.add).then_inc(N.v_ready, 1)
                dve.wait_ge(N.r_seed, k1)
                dve.wait_ge(N.v_ready, k1)
                st.then(refine(o_r, osq, ntmp))
                if not last_head:
                    low(6)
                st.then(V.tensor_tensor(o_n, bank(6)[:, 0:T], o_r, ALU.mult))
                st.then(V.scalar_tensor_tensor(o_n, o_n, pcol[:, 2:3], hgr, ALU.mult, ALU.mult))
                st.then(V.tensor_tensor(o_n, o_n, gate[:, 1], ALU.mult))
                st.then(V.tensor_tensor(gate[:, 0], gate[:, 0], zq[:, ds(it * 2 + e, 1)].rearrange("p o t -> p (o t)"), ALU.mult))
                V.tensor_tensor(zq[:, ds(it * 2 + e, 1)].rearrange("p o t -> p (o t)"), gate[:, 0], o_n, ALU.add)\
                    .then_inc(N.head_done, 1)

            slab_low(B_HG + 2, 2)
            with dve.Fori(0, NHG // 2 - 1) as it:
                st.enter(it, 2 * HEAD_STEPS)
                head(it, 0)
                head(it, 1)
            st.leave(NHG // 2 - 1)
            head(NHG // 2 - 1, 0)
            head(NHG // 2 - 1, 1, last_head=True)
            dve.wait_ge(N.head_done, NHG)

            def squares_split(s0):
                st.then(V.memset(sqacc, 0.0))

                def four(it):
                    for j in range(R):
                        y = hT[:, ds(it * R + j, 1)].rearrange("p o t -> p (o t)")
                        dve.wait_ge(N.bank_free, it * R + s0 + FREE + j + 1)
                        st.then(V.tensor_tensor(ntmp, y, y, ALU.mult))
                        st.then(V.tensor_tensor(sqacc, sqacc, ntmp, ALU.add))
                        slab_low(it * R + s0 + j + 2, (j + 2) % R)

                with dve.Fori(0, KD // R) as it:
                    st.enter(it, 2 * R)
                    four(it)
                st.leave(KD // R)
                V.memset(rstd[:, 0:1], 0.0).then_inc(N.n_sum, 1)

            def post_norm(i, nv, g_post, g_pre, mmv):
                dve.wait_ge(N.n_mm, mmv)
                V.tensor_scalar(var, bank(2)[:, 0:T], 1.0 / D, EPS, ALU.mult, ALU.add).then_inc(N.n_var, 1)
                dve.wait_ge(N.n_seed, nv)
                dve.wait_ge(N.n_var, nv)
                st.then(refine(rstd, var, ntmp))
                for f in range(KD):
                    V.scalar_tensor_tensor(hT[:, f], hT[:, f], g_post[:, f:f + 1], rstd, ALU.mult, ALU.mult)\
                        .then_inc(N.n_t, 1)
                if g_pre is None:
                    return
                dve.wait_ge(N.n_mm, mmv + KD)
                V.tensor_scalar(var, bank(3)[:, 0:T], 1.0 / D, EPS, ALU.mult, ALU.add).then_inc(N.n_var, 1)
                dve.wait_ge(N.n_seed, nv + 1)
                dve.wait_ge(N.n_var, nv + 1)
                st.then(refine(rstd, var, ntmp))
                for f in range(KD):
                    V.scalar_tensor_tensor(hT[:, f], xT[:, f], g_pre[:, f:f + 1], rstd, ALU.mult, ALU.mult).then_inc(N.n_h, 1)
                dve.wait_ge(N.n_h, KD * (i + 1))

            input_low(zq, zq_lo, 4, IN_OUT)
            squares_split(B_OUT)
            post_norm(0, 1, G_POST_MIX, G_PRE_X, 1)

            def evac_even(it, e, n0):
                for c in range(0, 8, 2):
                    cc = n0 + c if it is None else it * 16 + 8 * e + c
                    dve.wait_ge(N.kx_T, cc + 1)
                    V.tensor_copy(kxT[:, 0].rearrange("p a b -> p (a b)"), bank(2)).then_inc(N.kx_edve, 1)

            for j in range(2, R):
                slab_low(B_XQ + j, j)
            with dve.Fori(1, KD // R) as it:
                for j in range(R):
                    slab_low(it * R + B_XQ + j, j)
            with dve.Fori(0, DB // 2) as it:
                evac_even(it, 0, 0)
                evac_even(it, 1, 0)
            evac_even(None, 0, 64)
            dve.wait_ge(N.kx_used, 9)
            for qt in range(2):
                s3 = bank(4 + 2 * qt, 2).rearrange("p (x m) -> p x m", x=XH)
                st.then(V.tensor_reduce(smx2[:, qt, :], s3, AX.X, ALU.max, negate=True))
                V.tensor_scalar(smx2[:, 2 + qt, :], smx2[:, qt, :], X_S, None, ALU.mult).then_inc(N.px_max, 1)
            dve.wait_ge(N.sx_T, 1)
            s3 = bank(1).rearrange("p (r m) -> p r m", r=2)
            st.then(V.tensor_reduce(smx2[:, 6, 0:2], s3, AX.X, ALU.max, negate=True))
            V.tensor_scalar(smx2[:, 6, 2:4], smx2[:, 6, 0:2], X_S, None, ALU.mult).then_inc(N.sx_max, 1)
            for qt in range(2):
                dve.wait_ge(N.px_exp, 4 * qt + 4)
                st.then(V.reciprocal(smx2[:, qt, :], smx2[:, 4 + qt, :]))
                V.tensor_tensor(pp[:, qt], pp[:, qt], smx2[:, qt, :].rearrange("p (x o) -> p x o", o=1)
                                .broadcast_to([P, XH, MEM]), ALU.mult).then_inc(N.px_prob, 1)
            dve.wait_ge(N.sx_exp, 2)
            st.then(V.reciprocal(smx2[:, 6, 0:2], smx2[:, 7, 0:2]))
            for rt in range(2):
                V.tensor_scalar(px[:, rt], px[:, rt], smx2[:, 6, rt:rt + 1], None, ALU.mult).then_inc(N.sx_prob, 1)
            for j in range(2):
                slab_low(B_XO + j, j)
            input_low(qx, zq_lo, 8, IN_XO)
            squares_split(B_XO)
            post_norm(1, 3, G_POST_X, G_PRE_FFN, 1 + KD + 1)

            dve.wait_ge(N.conv_T, 1)
            st.did(V.tensor_copy(conv_old.rearrange("p f c -> p (f c)")[:, 0:512], bank(4)))
            V.tensor_copy(conv_old.rearrange("p f c -> p (f c)")[:, 512:FT * 16], bank(5)[:, 0:FT * 16 - 512])\
                .then_inc(N.conv_evac, 1)
            st.did(V.memset(a_ext[:, :, 0:2], 0.0))
            st.sync()
            def conv_gate(it, e, more):
                f1 = it * 2 + e + 1
                if more:
                    slab_low(it * R + B_UP + 2 * e + 2, (2 * e + 2) % R)
                dve.wait_ge(N.ctx_ready, it * 4 + 2 * e + 2)
                dve.wait_ge(N.bank_free, it * 4 + B_UP + 2 * e + 1 + FREE)
                ap = a_ext[:, e, 0:SEQ + 2]
                asm = a_ext[:, e, SEQ + 2:].rearrange("p (b t) -> p b t", t=DT + 2)
                cp = cv[:, e, 0:SEQ]
                cs = cv[:, e, SEQ:T].rearrange("p (b t) -> p b t", t=DT)
                st.did(V.tensor_scalar(cp, ap[:, 0:SEQ], pcf[:, e, 0:1], pcf[:, e, 3:4], ALU.mult, ALU.add))
                st.then(V.tensor_scalar(cs, asm[:, :, 0:DT], pcf[:, e, 0:1], pcf[:, e, 3:4], ALU.mult, ALU.add))
                st.did(V.scalar_tensor_tensor(cp, ap[:, 1:SEQ + 1], pcf[:, e, 1:2], cp, ALU.mult, ALU.add))
                st.then(V.scalar_tensor_tensor(cs, asm[:, :, 1:DT + 1], pcf[:, e, 1:2], cs, ALU.mult, ALU.add))
                st.did(V.scalar_tensor_tensor(cp, ap[:, 2:SEQ + 2], pcf[:, e, 2:3], cp, ALU.mult, ALU.add))
                V.scalar_tensor_tensor(cs, asm[:, :, 2:DT + 2], pcf[:, e, 2:3], cs, ALU.mult, ALU.add)\
                    .then_inc(N.c_ready, 1)
                if more:
                    slab_low(it * R + B_UP + 2 * e + 3, (2 * e + 3) % R)
                tail = conv_new[:, ds(it * 2 + e, 1), :].rearrange("p o c -> p (o c)")
                st.did(V.tensor_copy(tail[:, 0:2], ap[:, SEQ:SEQ + 2]))
                st.did(V.tensor_copy(tail[:, 2:18].rearrange("p (b t) -> p b t", t=2), asm[:, :, DT:DT + 2]))
                dve.wait_ge(N.g_ready, f1)
                V.tensor_tensor(yT[:, ds(it * 2 + e, 1)].rearrange("p o t -> p (o t)"), gl[:, e], zb[:, e], ALU.mult)\
                    .then_inc(N.y_done, 1)

            with dve.Fori(0, FT // 2 - 1) as it:
                st.enter(it, 2 * 7)
                conv_gate(it, 0, True)
                conv_gate(it, 1, True)
            st.leave(FT // 2 - 1)
            conv_gate(FT // 2 - 1, 0, True)
            conv_gate(FT // 2 - 1, 1, False)
            for j in range(1, R):
                dve.wait_ge(N.y_high, j)
                V.tensor_tensor(y_lo[j], yT[:, j * DOWN_K:(j + 1) * DOWN_K], y_hi[j].bitcast(FP32), ALU.subtract)\
                    .then_inc(N.y_low, 1)
                if j == 1:
                    st.then(V.memset(sqacc, 0.0))
            with dve.Fori(0, KD // 2) as it:
                st.enter(it, 4)
                for e in range(2):
                    for j in range(1, R):
                        dve.wait_ge(N.slab_hi, it * 6 + B_DOWN - B_MEM + 3 * e + j)
                        V.tensor_tensor(w_lo[:, j, 0:DOWN_K], ring[:, j, 0:DOWN_K], wd_hi[:, (3 * e + j) % 2].bitcast(FP32),
                                        ALU.subtract).then_inc(N.slab_lo, 1)
                    y = hT[:, ds(it * 2 + e, 1)].rearrange("p o t -> p (o t)")
                    dve.wait_ge(N.bank_free, it * 2 + B_DOWN + FREE + e + 1)
                    st.then(V.tensor_tensor(ntmp, y, y, ALU.mult))
                    st.then(V.tensor_tensor(sqacc, sqacc, ntmp, ALU.add))
            st.leave(KD // 2)
            V.memset(rstd[:, 0:1], 0.0).then_inc(N.n_sum, 1)
            post_norm(2, 5, G_POST_FFN, None, 2 * (1 + KD) + 1)
            for i in range(0, 12, 2):
                m, g = i // 4, i % 4
                rows = TOK[m][1]
                dve.wait_ge(N.xo_T, i + 1)
                V.tensor_copy(y_rows[0:rows, m, g * 512:(g + 1) * 512], bank(6)[0:rows]).then_inc(N.xo_edve, 1)

        @block.scalar
        def _(act):
            F = nc.scalar.activation
            st = Steps(act, N.act_step)
            act.dma_start(consts, const_dram).then_inc(N.const_loaded, 16)

            def met():
                act.wait_ge(N.const_loaded, 16)

            for g, r0, src in parameter_rows(A):
                act.dma_start(par_rows[r0:r0 + src.shape[0], g, :], src).then_inc(N.par_loaded, 16)
            act.wait_ge(N.small_set, 1)
            act.wait_ge(N.x_loaded, 48)
            for m, (_, rows) in enumerate(TOK):
                F(junk[0:rows], x_rows[0:rows, m], ACT.Square, accum_out=small[0:rows, m:m + 1]).then_inc(N.sumsq_done, 1)
                act.wait_ge(N.sumsq_done, m + 1)
            act.wait_ge(N.mem_loaded, 16)
            for m in range(2):
                F(junk, m_rows[:, m], ACT.Square, accum_out=small[:, 3 + m:4 + m]).then_inc(N.sumsq_done, 1)
                act.wait_ge(N.sumsq_done, m + 4)
            act.wait_ge(N.var_ready, 1)
            st.then(F(small[:, 16:21], small[:, 8:13], ACT.Ln))
            F(small[:, 24:29], small[:, 16:21], ACT.Exp, scale=-0.5).then_inc(N.seed_ready, 1)
            act.wait_ge(N.lb_max, 1)
            F(sqbuf[:, 0, 16:48], sqbuf[:, 0, 16:48], ACT.Exp).then_inc(N.lb_exp, 1)
            act.wait_ge(N.par_evac, 1)
            for f in range(KD):
                if f >= KD - 2:
                    act.wait_ge(N.row_T, 3 * f + 1)
                    F(xT[:, f], bank(f % 2)[:, 0:T], ACT.Copy).then_inc(N.bank_free, 1)
                act.wait_ge(N.row_T, 3 * f + 2)
                F(hT[:, f], bank(2 + f % 2)[:, 0:T], ACT.Copy, scale=G_PRE_MIX[:, f:f + 1]).then_inc(N.h_evac, 1)
                act.wait_ge(N.row_T, 3 * f + 3)
                F(mT[:, f], bank(4 + f % 2)[:, 0:MEM], ACT.Copy, scale=G_MEM[:, f:f + 1]).then_inc(N.m_evac, 1)

            def evacuate(s0, tiles, dst, n=T):
                with act.Fori(0, tiles // 2) as it:
                    for e in range(2):
                        act.wait_ge(N.slab_used, it * 2 + s0 + e + 1)
                        met()
                        F(dst[:, ds(it * 2 + e, 1), 0:n].rearrange("p o t -> p (o t)"), bank(e)[:, 0:n], ACT.Copy)\
                            .then_inc(N.bank_free, 1)

            evacuate(B_IQ, 8, iqT)
            act.wait_ge(N.ik_mm, 1)
            act.wait_ge(N.idx_zero, 1)
            F(ikd, bank(2)[:, 0:T], ACT.Copy).then_inc(N.ik_evac, 1)
            F(ikz[0:64, 0], bank(2)[0:64, 0:SEQ], ACT.Copy).then_inc(N.ik_evac, 1)
            F(ikz[64:P, 1], bank(2)[64:P, 0:SEQ], ACT.Copy).then_inc(N.ik_evac, 1)
            act.wait_ge(N.ik_mm, 2)
            F(iwT[0:H], bank(3)[0:H, 0:T], ACT.Copy, scale=(IDX ** -0.5) * (H ** -0.5)).then_inc(N.ik_evac, 1)
            evacuate(B_K, 4, kT)
            for j in range(R):
                act.wait_ge(N.slab_used, B_V + j + 1)
                F(vN[:, 0:2, j * P:(j + 1) * P], bank(j % 2)[:, 0:2 * P].rearrange("p (m c) -> p m c", m=2), ACT.Copy)
                F(vN[0:NS, 2, j * P:(j + 1) * P], bank(j % 2)[0:NS, 2 * P:3 * P], ACT.Copy).then_inc(N.bank_free, 1)
            act.wait_ge(N.ik_evac, 4)
            for i in range(4):
                act.wait_ge(N.page_T, i + 1)
                F(ik_all[:, 2 * i:2 * i + 2, 0:PAST], bank(2 + i).rearrange("p (b s) -> p b s", b=2), ACT.Copy)\
                    .then_inc(N.page_evac, 1)
            F(ik_all[:, :, PAST:L_S], ikd[:, SEQ:T].rearrange("p (b t) -> p b t", t=DT), ACT.Copy).then_inc(N.page_evac, 1)
            for b in range(DB):
                act.wait_ge(N.sidx_mm, b + 1)
                if b >= 2:
                    act.wait_ge(N.sidx_sum, b - 1)
                F(relu_s[:, b % 2], bank(6 + b % 2)[:, 0:L_S], ACT.Relu).then_inc(N.sidx_relu, 1)
            for m, (_, rows) in enumerate(TOK):
                act.wait_ge(N.out_T, m + 1)
                F(key_out[0:rows, m], bank(3 + m)[0:rows], ACT.Copy).then_inc(N.out_evac, 1)
            act.wait_ge(N.out_T, 4)
            F(ik_out[:, 0:2], bank(6)[:, 0:2 * IDX].rearrange("p (m c) -> p m c", m=2), ACT.Copy).then_inc(N.out_evac, 1)
            F(ik_out[0:NS, 2], bank(6)[0:NS, 2 * IDX:3 * IDX], ACT.Copy).then_inc(N.out_evac, 1)
            def slab_high(j, ready):
                act.wait_ge(slab_ready[j], ready)
                F(w_hi[:, j % 2], ring[:, j], ACT.Copy).then_inc(N.slab_hi, 1)

            def first_highs(n):
                for j in range(2):
                    slab_high(j, 16 * (n // R + 1))

            evacuate(B_QQ, 8, zq[:, 0:8])
            act.wait_ge(N.selected, 3)
            for q in range(4):
                F(m_hi[:, 4 * q:4 * q + 4], mT[:, 4 * q:4 * q + 4], ACT.Copy).then_inc(N.m_high, 1)
            evacuate(B_QQ + 8, 8, zq[:, 8:16])
            first_highs(B_MEM)

            def memory_evac(it, i, more=True):
                act.wait_ge(N.slab_used, it * R + i + B_MEM + 1)
                F(mf[:, i % 2], bank(i % 2)[:, 0:MEM], ACT.Copy).then_inc(N.bank_free, 1)
                if more:
                    slab_high((i + 2) % R, it * 16 + 16 * ((B_MEM + i + 2) // R + 1))

            def memory_rows(it, i):
                act.wait_ge(N.mem_T, it * R + i + 1)
                F(mem_out[:, :, i * P:(i + 1) * P], bank(2 + i % 2)[:, 0:2 * P].rearrange("p (m c) -> p m c", m=2), ACT.Copy)\
                    .then_inc(N.mem_copied, 1)

            def send(it, dst, col):
                act.wait_ge(N.mem_copied, it * R + R)
                act.dma_start(dst[:, :, ds(col, 512)], mem_out).then_inc(N.memo_sent, 16)

            memory_evac(0, 0)
            act.wait_ge(N.out_sent, 96)
            for first, end, dst in ((0, 4, new_mk), (4, 7, new_mv)):
                with act.Fori(first, end) as it:
                    for i in range(R):
                        memory_evac(it, i + 1)
                        if i == 0:
                            act.wait_ge(N.memo_sent, it * 16)
                        memory_rows(it, i)
                    send(it, dst, it * 512 - first * 512)
            for i in range(R):
                if i < R - 1:
                    memory_evac(7, i + 1, more=i == 0)
                if i == 0:
                    act.wait_ge(N.memo_sent, 7 * 16)
                memory_rows(7, i)
            send(7, new_mv, 3 * 512)
            act.wait_ge(N.memo_sent, 128)

            def exps(it, g):
                act.wait_ge(N.s_max, it * QPK + g + 1)
                act.wait_ge(N.p_T, two_back(it, QPK, g))
                F(prob[:, g % 2, 0:P], logit[:, g % 2, 0:P], ACT.Exp, bias=smx[:, g, 0:1], accum_out=smx[:, g, 2:3])
                F(prob[:, g % 2, P:384], logit[:, g % 2, P:384], ACT.Exp, bias=smx[:, g, 1:2],
                  accum_out=smx[:, g, 3:4]).then_inc(N.s_exp, 1)

            def copies(it, g):
                act.wait_ge(N.p_T, it * QPK + g + 1)
                F(probT[:, g % 2], bank(4 + g % 2)[:, 0:384], ACT.Copy).then_inc(N.p_evac, 1)
                met()
                act.wait_ge(N.pv_mm, it * QPK + g + 1)
                F(zq[:, ds(it * QPK + g, 1), 0:SEQ].rearrange("p o t -> p (o t)"), bank(6 + g % 2)[:, 0:SEQ], ACT.Copy)\
                    .then_inc(N.o_evac, 1)

            act.wait_ge(N.selected, 3)
            with act.Fori(0, KVH) as it:
                act.wait_ge(N.s_mm, it * QPK)
                met()
                F(qs, zq[:, ds(it * QPK, QPK), 0:SEQ], ACT.Copy).then_inc(N.q_staged, 1)
                exps(it, 0)
                for g in range(1, QPK):
                    exps(it, g)
                    copies(it, g - 1)
                copies(it, QPK - 1)

            with act.Fori(0, DB // 2) as it:
                for e in range(2):
                    n1 = it * 2 + e + 1 + H
                    act.wait_ge(N.pv_mm, it * 2 + e + H)
                    new = ds(it * 16 + SEQ + e * DT, DT)
                    F(q_b[:, e], zq[:, :, new], ACT.Copy).then_inc(N.b_staged, 1)
                    met()
                    F(rep_b[0:NS, e], const("spread", NS)[:, ds(it * 256 + e * P, P)], ACT.Copy).then_inc(N.b_staged, 1)
                    for i in range(2):
                        act.wait_ge(N.kt_T, it * 4 + 2 * e + i + 1)
                        F(ktp[:, 2 * i:2 * i + 2, :], bank(2 + i).rearrange("p (h s) -> p h s", h=2), ACT.Copy)\
                            .then_inc(N.kt_evac, 1)
                    act.wait_ge(N.s_max, n1)
                    F(prob[:, e, 0:T], logit[:, e, 0:T], ACT.Exp, bias=smx[:, e, 0:1], accum_out=smx[:, e, 2:3])\
                        .then_inc(N.s_exp, 1)
                    act.wait_ge(N.p_T, n1)
                    F(probT[:, e, 0:PAST], bank(5)[:, 0:PAST], ACT.Copy)
                    F(probT[0:NS, e, PAST:384], bank(5)[0:NS, PAST:384], ACT.Copy).then_inc(N.p_evac, 1)
                    met()
                    act.wait_ge(N.pv_mm, n1)
                    F(zq[:, :, new], bank(6)[:, 0:P].rearrange("p (h t) -> p h t", t=DT), ACT.Copy).then_inc(N.o_evac, 1)

            def evacuate_split(s0, dst, more=True):
                def four(it, last):
                    for j in range(R):
                        n = s0 + j + 2
                        act.wait_ge(N.slab_used, it * R + s0 + j + 1)
                        met()
                        F(dst[:, ds(it * R + j, 1), 0:T].rearrange("p o t -> p (o t)"), bank(j % 2)[:, 0:T], ACT.Copy)\
                            .then_inc(N.bank_free, 1)
                        if j < 2 or not last:
                            slab_high(n % R, it * 16 + 16 * (n // R + 1))

                with act.Fori(0, KD // R - (0 if more else 1)) as it:
                    four(it, False)
                if not more:
                    four(KD // R - 1, True)

            def input_high(src, heads=0):
                for q in range(4):
                    if heads:
                        act.wait_ge(N.head_done, heads * (q + 1))
                    F(x_hi[:, 4 * q:4 * q + 4], src[:, 4 * q:4 * q + 4], ACT.Copy).then_inc(N.in_hi, 1)

            act.wait_ge(N.o_evac, H + DB)
            first_highs(B_HG)
            input_high(hT)

            def head(it, e):
                k1 = it * 2 + e + 1
                s0 = it * 12 + B_HG + 6 * e

                def high(g):
                    n = B_HG + 6 * e + g + 2
                    slab_high(n % R, it * 48 + 16 * (n // R + 1))

                def b(g):
                    return bank((6 * e + g) % 2)

                act.wait_ge(N.slab_used, s0 + 1)
                F(f_e, b(0)[:, 0:T], ACT.Exp, scale=-1.0).then_inc(N.bank_free, 1)
                high(0)
                act.wait_ge(N.slab_used, s0 + 2)
                F(hq, b(1)[:, 0:T], ACT.Copy).then_inc(N.bank_free, 1)
                high(1)
                act.wait_ge(N.f_ready, k1)
                F(eb, f_e, ACT.Ln).then_inc(N.logf_ready, 1)
                act.wait_ge(N.slab_used, s0 + 3)
                act.wait_ge(N.head_done, it * 2 + e)
                F(vf, b(2)[:, 0:T], ACT.Copy).then_inc(N.bank_free, 1)
                high(2)
                act.wait_ge(N.d_ready, k1)
                st.did(F(lev[:, 0:LVS], lev[:, 0:LVS], ACT.Exp))
                st.did(F(lev[:, LVS:LV, 0:SEQ], lev[:, LVS:LV, 0:SEQ], ACT.Exp))
                st.did(F(ke, ke, ACT.Exp))
                F(eb, f_b, ACT.Exp).then_inc(N.e_ready, 1)
                act.wait_ge(N.slab_used, s0 + 4)
                st.did(F(hgr, b(3)[:, 0:T], ACT.Copy))
                F(gate[:, 2], b(3)[:, 0:T], ACT.Exp, scale=-1.0).then_inc(N.bank_free, 1)
                act.wait_ge(N.v_T, k1)
                st.did(F(vh[:, 0:2], bank(7)[:, 0:2 * P].rearrange("p (m c) -> p m c", m=2), ACT.Copy))
                F(vh[0:NS, 2], bank(7)[0:NS, 2 * P:3 * P], ACT.Copy).then_inc(N.v_evac, 1)
                high(3)
                act.wait_ge(N.slab_used, s0 + 5)
                F(gate[:, 0], b(4)[:, 0:T], ACT.Exp, scale=-1.0).then_inc(N.bank_free, 1)
                high(4)
                act.wait_ge(N.ke_T, k1)
                st.did(F(keN[:, 0:2], bank(7)[:, 0:2 * P].rearrange("p (m c) -> p m c", m=2), ACT.Copy))
                F(keN[0:NS, 2], bank(7)[0:NS, 2 * P:3 * P], ACT.Copy).then_inc(N.keN_ready, 1)
                act.wait_ge(N.slab_used, s0 + 6)
                F(gate[:, 1], b(5)[:, 0:T], ACT.Exp, scale=-1.0).then_inc(N.bank_free, 1)
                high(5)
                act.wait_ge(N.s1_mm, k1)
                F(s1, bank(4)[:, 0:P], ACT.Copy).then_inc(N.s1_ready, 1)
                act.wait_ge(N.o_mm, k1)
                F(osq, bank(6)[:, 0:T], ACT.Square).then_inc(N.osq_ready, 1)
                act.wait_ge(N.v_ready, k1)
                st.then(F(o_r, osq, ACT.Ln))
                F(o_r, o_r, ACT.Exp, scale=-0.5).then_inc(N.r_seed, 1)

            with act.Fori(0, NHG // 2) as it:
                st.enter(it, 2 * 7)
                head(it, 0)
                head(it, 1)
            st.leave(NHG // 2)

            def seed(nv):
                act.wait_ge(N.n_var, nv)
                st.then(F(rstd, var, ACT.Ln))
                F(rstd, rstd, ACT.Exp, scale=-0.5).then_inc(N.n_seed, 1)

            def norm(i, nv, mmv, pre):
                seed(nv)
                if pre:
                    for f in range(KD):
                        act.wait_ge(N.n_x, i * KD + f + 1)
                        if f >= 2:
                            act.wait_ge(N.n_mm, mmv + f - 1)
                        F(sqbuf[:, f % 2], xT[:, f], ACT.Square).then_inc(N.n_sq, 1)
                    seed(nv + 1)
                    for f in range(KD):
                        act.wait_ge(N.n_h, i * KD + f + 1)
                        F(x_hi[:, f], hT[:, f], ACT.Copy).then_inc(N.in_hi, 1)

            act.wait_ge(N.slab_used, B_OUT)
            input_high(zq, heads=4)
            act.wait_ge(N.state_sent, 32 * NHG)
            evacuate_split(B_OUT, hT)
            act.wait_ge(N.n_sum, 1)
            norm(0, 1, 1, True)
            evacuate_split(B_XQ, qx, more=False)

            def evac_odd(it, e, n0):
                for c in range(1, 8, 2):
                    cc = n0 + c if it is None else it * 16 + 8 * e + c
                    act.wait_ge(N.kx_T, cc + 1)
                    F(kxT[:, 1].rearrange("p a b -> p (a b)"), bank(3), ACT.Copy).then_inc(N.kx_eact, 1)

            with act.Fori(0, DB // 2) as it:
                evac_odd(it, 0, 0)
                evac_odd(it, 1, 0)
            evac_odd(None, 0, 64)
            act.wait_ge(N.kx_used, 8)
            F(sxT.rearrange("p a b -> p (a b)"), bank(0), ACT.Copy).then_inc(N.sx_evac, 1)
            for qt in range(2):
                act.wait_ge(N.px_max, qt + 1)
                for x in range(XH):
                    F(pp[:, qt, x], bank(4 + 2 * qt + x // 2)[:, (x % 2) * MEM:(x % 2 + 1) * MEM], ACT.Exp,
                      bias=smx2[:, 2 + qt, x:x + 1], scale=X_S, accum_out=smx2[:, 4 + qt, x:x + 1]).then_inc(N.px_exp, 1)
            act.wait_ge(N.sx_max, 1)
            for rt in range(2):
                F(px[:, rt], bank(1)[:, rt * MEM:(rt + 1) * MEM], ACT.Exp, bias=smx2[:, 6, 2 + rt:3 + rt], scale=X_S,
                  accum_out=smx2[:, 7, rt:rt + 1]).then_inc(N.sx_exp, 1)
            for x in range(XH):
                act.wait_ge(N.px_T, x + 1)
                F(ppT[:, x % 2], bank(2 + x % 2), ACT.Copy).then_inc(N.px_evac, 1)
                for dt in range(XD):
                    n = x * XD + dt
                    act.wait_ge(N.vx_mm, n + 1)
                    F(qx[:, n, 0:SEQ], bank(4 + n % 2)[:, 0:SEQ], ACT.Copy).then_inc(N.vx_evac, 1)
            act.wait_ge(N.sx_pT, 1)
            F(pxT.rearrange("p a b -> p (a b)"), bank(6), ACT.Copy).then_inc(N.sx_pevac, 1)
            with act.Fori(0, DB // 2) as it:
                for e in range(2):
                    act.wait_ge(N.vx_mm, it * 2 + e + KD + 1)
                    met()
                    F(qx[:, :, ds(it * 16 + SEQ + e * DT, DT)], bank(2 + e)[:, 0:P].rearrange("p (n t) -> p n t", t=DT),
                      ACT.Copy).then_inc(N.vx_evac, 1)
            first_highs(B_XO)
            act.wait_ge(N.vx_evac, KD + DB)
            input_high(qx)
            evacuate_split(B_XO, hT)
            norm(1, 3, 1 + KD + 1, True)

            def conv_input(it, e, more):
                s0 = it * 4 + B_UP + 2 * e
                act.wait_ge(N.slab_used, s0 + 1)
                act.wait_ge(N.y_done, two_back(it, 2, e))
                F(a_ext[:, e, 2:SEQ + 2], bank(0)[:, 0:SEQ], ACT.Copy)
                F(a_ext[:, e, SEQ + 2:].rearrange("p (b t) -> p b t", t=DT + 2)[:, :, 2:DT + 2],
                  bank(0)[:, SEQ:T].rearrange("p (b t) -> p b t", t=DT), ACT.Copy).then_inc(N.bank_free, 1)
                j = (2 * e + 2) % R
                ready = it * 16 + 16 * ((B_UP + 2 * e + 2) // R + 1)
                if more:
                    slab_high(j, ready)
                act.wait_ge(N.slab_used, s0 + 2)
                F(zb[:, e], bank(1)[:, 0:T], ACT.Copy).then_inc(N.bank_free, 1)
                if more:
                    slab_high(j + 1, ready)
                act.wait_ge(N.c_ready, it * 2 + e + 1)
                act.wait_ge(N.bank_free, s0 + 2 + FREE)
                F(gl[:, e], cv[:, e], ACT.Gelu_apprx_tanh).then_inc(N.g_ready, 1)

            with act.Fori(0, FT // 2 - 1) as it:
                conv_input(it, 0, True)
                conv_input(it, 1, True)
            conv_input(FT // 2 - 1, 0, True)
            conv_input(FT // 2 - 1, 1, False)
            def down_high(it, e, j):
                act.wait_ge(slab_ready[j], it * 32 + 16 * (B_DOWN // R + e + 1))
                act.wait_ge(N.slab_used, it * 8 + B_DOWN + 4 * e + (-1, 0, 2)[j - 1])
                F(wd_hi[:, (3 * e + j) % 2], ring[:, j, 0:DOWN_K], ACT.Copy).then_inc(N.slab_hi, 1)

            act.wait_ge(N.y_done, FT)
            act.wait_ge(N.slab_used, B_DOWN)
            for j in range(1, R):
                F(y_hi[j], yT[:, j * DOWN_K:(j + 1) * DOWN_K], ACT.Copy).then_inc(N.y_high, 1)
            with act.Fori(0, KD // 2) as it:
                for e in range(2):
                    for j in range(1, R):
                        down_high(it, e, j)
                    act.wait_ge(N.slab_used, it * 8 + B_DOWN + 4 * e + 4)
                    met()
                    F(hT[:, ds(it * 2 + e, 1)].rearrange("p o t -> p (o t)"), bank(e)[:, 0:T], ACT.Copy)\
                        .then_inc(N.bank_free, 1)
            norm(2, 5, 0, False)
            for g in range(FT // 4):
                act.wait_ge(N.cn_T, g + 1)
                F(x_out[0:18, g * 512:(g + 1) * 512], bank(4 + g % 2)[0:18], ACT.Copy).then_inc(N.cn_evac, 1)
            for i in range(1, 12, 2):
                m, g = i // 4, i % 4
                rows = TOK[m][1]
                act.wait_ge(N.xo_T, i + 1)
                F(y_rows[0:rows, m, g * 512:(g + 1) * 512], bank(7)[0:rows], ACT.Copy).then_inc(N.xo_eact, 1)

        @block.gpsimd
        def _(pool):
            G = nc.gpsimd
            pool.dma_start(pages[0:1, :], A["page_table"].rearrange("(o b) g -> o (b g)", o=1)).then_inc(N.pages_loaded, 16)
            pool.wait_ge(N.pages_loaded, 16)
            pool.wait_ge(N.row_T, 3 * KD)
            for i in range(DB * NPG):
                pg = pool.value_load(pages[0:1, i:i + 1], min_val=0, max_val=POOL - 1)
                pool.dma_start(ik_page[:, i, :], A["cache_idx_k"][0][ds(pg, 1)].rearrange("o s d -> (o s) d"))\
                    .then_inc(N.ikpage_loaded, 16)
            G.memset(ikz, 0.0).then_inc(N.idx_zero, 1)
            G.memset(iq_s, 0.0).then_inc(N.idx_zero, 1)
            pool.wait_ge(N.ikpage_loaded, 16 * DB * NPG)
            pool.wait_ge(N.ik_mm, 2)
            G.tensor_copy(ik_dup, ik_page.rearrange("p n (o d) -> p n o d", o=1).broadcast_to([P, DB * NPG, 2, IDX]))\
                .then_inc(N.dup_ready, 1)
            pool.wait_ge(N.out_evac, 5)
            pool.wait_ge(N.bank_free, B_QQ + FREE)
            for dst, src in ((new_k, key_out[:, 0:2]), (new_ks, key_out[0:NS, 2]), (new_v, vN[:, 0:2]),
                             (new_vs, vN[0:NS, 2]), (new_ik, ik_out[:, 0:2]), (new_iks, ik_out[0:NS, 2])):
                pool.dma_start(dst, src).then_inc(N.out_sent, 16)

            pool.wait_ge(N.selected, 3)
            pool.dma_start(rel_sb[0:NB, :], A["rel_bias"]).then_inc(N.rel_loaded, 16)
            pool.wait_ge(N.bias_evac, 1)
            pool.dma_start(bias_dram, dist_sb[0:H, :].rearrange("h (o n) -> h o n", o=1).broadcast_to([H, P, NDIST])).then_inc(N.bias_stored, 16)
            pool.wait_ge(N.bias_stored, 16)

            def table(offset, ap):
                return bass.AP(tensor=bias_dram.tensor, offset=offset, ap=ap)

            pool.dma_start(toep, table(DIST0 - (SEQ - 1) + P - 1, [[NDIST - 1, P], [P * NDIST, H], [1, SEQ]]))\
                .then_inc(N.bias_loaded, 16)
            for h in range(H):
                rows = slice(h * DT, (h + 1) * DT)
                pool.dma_start(bias_s[rows, 0:PAST], table(h * P * NDIST + DT - 1, [[NDIST - 1, DT], [1, PAST]]))\
                    .then_inc(N.bias_loaded, 16)
                pool.dma_start(bias_s[rows, PAST:T].rearrange("p (b t) -> p b t", t=DT),
                               table(h * P * NDIST + DIST0, [[NDIST - 1, DT], [0, DB], [1, DT]])).then_inc(N.bias_loaded, 16)
            pool.wait_ge(N.bias_loaded, 16 * BIAS_DMAS)

            def page_loads(pool_it, e, first):
                for pg in range(NPG):
                    at = pool_it * 4 + (2 * e + pg) if not first else 2 * e + pg
                    src = pages[0:1, ds(at, 1)] if not first else pages[0:1, at:at + 1]
                    page = pool.value_load(src, min_val=0, max_val=POOL - 1)
                    for buf, cache in ((k_page, "cache_k"), (v_page, "cache_v")):
                        pool.dma_start(buf[:, e, pg, :], A[cache][0][ds(page, 1)].rearrange("o s h d -> (o s) (h d)"))\
                            .then_inc(kv_loaded[e], 16)

            def bias_and_mask(it):
                for g in range(QPK):
                    pool.wait_ge(N.s_read, two_back(it, QPK, g))
                    hrow = toep[:, ds(it * QPK + g, 1), :].rearrange("p o k -> p (o k)")
                    G.tensor_tensor(bm[:, g % 2, 0:P], hrow[:, P:SEQ], sel_p[:, 0, 0:P], ALU.add).then_inc(N.bm_ready, 1)
                    G.tensor_tensor(bm[:, g % 2, P:384], hrow, sel_p[:, 1, :], ALU.add).then_inc(N.bm_ready, 1)

            pool.wait_ge(N.memo_sent, 128)
            bias_and_mask(0)
            for e in range(2):
                page_loads(0, e, True)
            with pool.Fori(1, KVH) as it:
                bias_and_mask(it)
            with pool.Fori(1, DB // 2) as it:
                for e in range(2):
                    pool.wait_ge(N.pv_mm, it * 2 + e + H - 1)
                    page_loads(it, e, False)

            with pool.Fori(0, NHG // 2) as it:
                for e in range(2):
                    k1 = it * 2 + e + 1
                    pool.wait_ge(N.head_done, it * 2 + e)
                    pool.wait_ge(N.o_evac, H + DB)
                    G.tensor_copy(pcol, head_par[:, ds(it * 2 + e, 1), :].rearrange("p o c -> p (o c)"))\
                        .then_inc(N.pcol_ready, 1)
                    pool.wait_ge(N.v_evac, k1)
                    G.tensor_tensor(v_m[0:NS], vh[0:NS, 2].rearrange("p (o v) -> p o v", o=1).broadcast_to([NS, DB, P]),
                                    const("seq_of", NS).rearrange("p (b o) -> p b o", o=1).broadcast_to([NS, DB, P]),
                                    ALU.mult).then_inc(N.vm_ready, 1)
                    pool.wait_ge(N.st_ready, k1)
                    pool.dma_start(hg_out_p[ds(it * 2 + e, 1)].rearrange("o c v -> (o c) v"), s2).then_inc(N.state_sent, 16)
                    pool.dma_start(hg_out_s[ds(it * 2 + e, 1)].rearrange("o c b v -> (o c) b v"), s_new)\
                        .then_inc(N.state_sent, 16)

            def h_low(n0):
                for f in range(KD):
                    pool.wait_ge(N.in_hi, n0 + f + 1)
                    G.tensor_tensor(h_lo[:, f], hT[:, f], x_hi[:, f].bitcast(FP32), ALU.subtract).then_inc(N.h_low, 1)

            def add_residual(i):
                for f in range(KD):
                    pool.wait_ge(N.n_t, i * KD + f + 1)
                    G.tensor_tensor(xT[:, f], xT[:, f], hT[:, f], ALU.add).then_inc(N.n_x, 1)

            add_residual(0)
            h_low(IN_XQ)
            add_residual(1)
            h_low(IN_UP)
            pool.wait_ge(N.conv_evac, 1)
            with pool.Fori(0, FT // 2) as it:
                for e in range(2):
                    f = ds(it * 2 + e, 1)
                    pool.wait_ge(N.y_done, two_back(it, 2, e))
                    G.tensor_copy(pcf[:, e], conv_par[:, f, :].rearrange("p o c -> p (o c)")).then_inc(N.ctx_ready, 1)
                    G.tensor_copy(a_ext[:, e, SEQ + 2:].rearrange("p (b t) -> p b t", t=DT + 2)[:, :, 0:2],
                                  conv_old[:, f, :].rearrange("p o (b t) -> p (o b) t", t=2)).then_inc(N.ctx_ready, 1)
            add_residual(2)
            pool.wait_ge(N.out_sent, 96)
            pool.wait_ge(N.state_sent, 32 * NHG)
            pool.wait_ge(N.memo_sent, 128)


OUT_SHAPES = {
    "y_prompt": (1, SEQ, D), "y_sample": (DB, DT, D),
    "new_k_prompt": (1, 1, SEQ, KVH, P), "new_v_prompt": (1, 1, SEQ, KVH, P), "new_idx_k_prompt": (1, 1, SEQ, IDX),
    "new_k_sample": (1, DB, DT, KVH, P), "new_v_sample": (1, DB, DT, KVH, P), "new_idx_k_sample": (1, DB, DT, IDX),
    "new_mem_k_prompt": (1, 1, MEM, XH, 512), "new_mem_v_prompt": (1, 1, MEM, XH, 512),
    "new_hgrn_prompt": (1, 1, NHG, P, P), "new_hgrn_sample": (1, DB, NHG, P, P),
    "new_conv_prompt": (1, 1, 2, FF), "new_conv_sample": (1, DB, 2, FF),
}


def kernel(**inputs):
    import concourse.bacc as bacc
    from concourse.bass_utils import run_bass_kernel_spmd

    nc = bacc.Bacc("TRN2", target_bir_lowering=False, num_devices=1)
    arrays, A = {}, {}
    for name, a in list(inputs.items()) + [("shape_constants", shape_constants())]:
        a = np.ascontiguousarray(a)
        arrays["in_" + name] = a
        A[name] = nc.dram_tensor("in_" + name, a.shape, mybir.dt.from_np(a.dtype), kind="ExternalInput").ap()
    O = {n: nc.dram_tensor("out_" + n, s, FP32, kind="ExternalOutput").ap() for n, s in OUT_SHAPES.items()}
    hybrid_layer(nc, A, O, A["shape_constants"])
    r = run_bass_kernel_spmd(nc, [arrays], core_ids=[0])
    return tuple(r.results[0]["out_" + n] for n in OUT_SHAPES)
```
